# Optimizing a Trainium2 kernel written in Bass

```python
import jax, jax.numpy as jnp
from jax import lax
import numpy as np

D_MODEL = 1024
BATCH = 1
SEQ = 512
DEPTH = 2

GRID_W = 64
CTX_LEN = 256
HEAD_DIM = 128
N_Q_HEADS = 4
N_KV_HEADS = 2
ATTN_WIDTH = N_Q_HEADS * HEAD_DIM
KV_WIDTH = N_KV_HEADS * HEAD_DIM
CONV_WIDTH = D_MODEL - ATTN_WIDTH
SHORT_CONV_K = 3
IN_PROJ_WIDTH = ATTN_WIDTH + 2 * KV_WIDTH + 3 * CONV_WIDTH
PROJ_SPLITS = (ATTN_WIDTH,
               ATTN_WIDTH + KV_WIDTH,
               ATTN_WIDTH + 2 * KV_WIDTH,
               ATTN_WIDTH + 2 * KV_WIDTH + CONV_WIDTH,
               ATTN_WIDTH + 2 * KV_WIDTH + 2 * CONV_WIDTH)
Q_BLOCK = 128
ROPE_THETA = 10000.0
POOL_WINDOWS = (2, 4, 8, 16)
N_POOL_GROUPS = len(POOL_WINDOWS)
POOL_GROUP = D_MODEL // N_POOL_GROUPS
D_FF = 2816
FFN_CONV_K = 3
N_MOD = 6
EPS = 1e-6
N_EVEN = (DEPTH + 1) // 2
N_ODD = DEPTH // 2

kernel_name = "hybrid_gqa_shortconv_pool_convglu_dit"

def rms_norm(x, gain):
    xf = x.astype(jnp.float32)
    y = xf * lax.rsqrt(jnp.mean(xf * xf, axis=-1, keepdims=True) + EPS)
    return (y * gain.astype(jnp.float32)).astype(x.dtype)

def modulate(h, shift, scale):
    return h * (1.0 + scale) + shift

def dwconv_centred(h, w):
    k = w.shape[0]
    p = k // 2
    n = h.shape[1]
    hp = jnp.pad(h, ((0, 0), (p, p), (0, 0)))
    return sum(hp[:, j:j + n] * w[j] for j in range(k))

def axial_rope_tables(rows):
    row_ids = jnp.repeat(jnp.arange(rows), GRID_W).astype(jnp.float32)
    col_ids = jnp.tile(jnp.arange(GRID_W), rows).astype(jnp.float32)
    axis_dim = HEAD_DIM // 2
    inv_freq = jnp.power(ROPE_THETA, -jnp.arange(0, axis_dim, 2, dtype=jnp.float32) / axis_dim)
    ang = jnp.stack([row_ids[:, None] * inv_freq, col_ids[:, None] * inv_freq], axis=1)
    return jnp.cos(ang), jnp.sin(ang)

def apply_axial_rope(x, cos, sin):
    b, n, h, d = x.shape
    xr = x.reshape(b, n, h, 2, 2, d // 4)
    x1, x2 = xr[..., 0, :], xr[..., 1, :]
    c = cos[None, :, None].astype(x.dtype)
    s = sin[None, :, None].astype(x.dtype)
    out = jnp.stack([x1 * c - x2 * s, x2 * c + x1 * s], axis=-2)
    return out.reshape(b, n, h, d)

def gqa_softmax(qg, k, v):
    scores = jnp.einsum('bqkgd,btkd->bkgqt', qg, k).astype(jnp.float32) * (HEAD_DIM ** -0.5)
    p = jax.nn.softmax(scores, axis=-1).astype(v.dtype)
    return jnp.einsum('bkgqt,btkd->bqkgd', p, v)

def latent_attention(q, k_lat, v_lat, k_ctx, v_ctx):
    b, n, hq, hd = q.shape
    g = hq // N_KV_HEADS
    k_all = jnp.concatenate([k_ctx, k_lat], axis=1)
    v_all = jnp.concatenate([v_ctx, v_lat], axis=1)
    nblk = n // Q_BLOCK
    qb = q.reshape(b, nblk, Q_BLOCK, N_KV_HEADS, g, hd).transpose(1, 0, 2, 3, 4, 5)
    out = lax.map(lambda qblk: gqa_softmax(qblk, k_all, v_all), qb)
    return out.transpose(1, 0, 2, 3, 4, 5).reshape(b, n, hq * hd)

def context_attention(q, k, v):
    b, n, hq, hd = q.shape
    qg = q.reshape(b, n, N_KV_HEADS, hq // N_KV_HEADS, hd)
    return gqa_softmax(qg, k, v).reshape(b, n, hq * hd)

def split_projection(p, q_gain, k_gain):
    b, n, _ = p.shape
    q, k, v, gate_b, gate_c, x_in = jnp.split(p, PROJ_SPLITS, axis=-1)
    q = rms_norm(q.reshape(b, n, N_Q_HEADS, HEAD_DIM), q_gain)
    k = rms_norm(k.reshape(b, n, N_KV_HEADS, HEAD_DIM), k_gain)
    v = v.reshape(b, n, N_KV_HEADS, HEAD_DIM)
    return q, k, v, gate_b, gate_c, x_in

def even_mixer(a_lat, a_ctx, cos, sin, w_in, q_gain, k_gain, conv_w, w_out, with_ctx_out):
    b, lc, _ = a_ctx.shape
    if with_ctx_out:
        cq, ck, cv, cgb, cgc, cxin = split_projection(a_ctx @ w_in, q_gain, k_gain)
    else:
        ckv = a_ctx @ w_in[:, ATTN_WIDTH:ATTN_WIDTH + 2 * KV_WIDTH]
        ck, cv = jnp.split(ckv, 2, axis=-1)
        ck = rms_norm(ck.reshape(b, lc, N_KV_HEADS, HEAD_DIM), k_gain)
        cv = cv.reshape(b, lc, N_KV_HEADS, HEAD_DIM)
    q, k, v, gate_b, gate_c, x_in = split_projection(a_lat @ w_in, q_gain, k_gain)
    q = apply_axial_rope(q, cos, sin)
    k = apply_axial_rope(k, cos, sin)
    attn = latent_attention(q, k, v, ck, cv)
    conv = gate_b * dwconv_centred(gate_c * x_in, conv_w)
    y_lat = jnp.concatenate([attn, conv], axis=-1) @ w_out
    y_ctx = None
    if with_ctx_out:
        c_attn = context_attention(cq, ck, cv)
        c_conv = cgb * dwconv_centred(cgc * cxin, conv_w)
        y_ctx = jnp.concatenate([c_attn, c_conv], axis=-1) @ w_out
    return y_lat, y_ctx

def pool_mixer(h, pool_w, pool_scale):
    b, n, d = h.shape
    hf = h.astype(jnp.float32)
    cs = jnp.pad(jnp.cumsum(hf, axis=1), ((0, 0), (1, 0), (0, 0)))
    t = jnp.arange(n)
    groups = []
    for gi, w in enumerate(POOL_WINDOWS):
        lo = jnp.clip(t - w // 2, 0, n)
        hi = jnp.clip(t + w - w // 2, 0, n)
        sl = slice(gi * POOL_GROUP, (gi + 1) * POOL_GROUP)
        csg = cs[:, :, sl]
        mean = (csg[:, hi] - csg[:, lo]) / (hi - lo).astype(jnp.float32)[None, :, None]
        groups.append(mean - hf[:, :, sl])
    pooled = jnp.stack(groups, axis=2).astype(h.dtype)
    mixed = jnp.einsum('bngc,gce->bnge', pooled, pool_w).reshape(b, n, d)
    return mixed * pool_scale

def conv_glu(h, w_up, conv_w, conv_b, w_down):
    gate, val = jnp.split(h @ w_up, 2, axis=-1)
    gate = dwconv_centred(gate, conv_w) + conv_b
    return (jax.nn.silu(gate) * val) @ w_down

def setup_inputs(seed: int = 0) -> dict:
    key = jax.random.key(seed)
    ks = jax.random.split(key, 24)
    f32 = jnp.float32
    nrm = lambda k, shape, s: jax.random.normal(k, shape, f32) * s
    d = D_MODEL
    return {
        "x": nrm(ks[0], (BATCH, SEQ, d), 1.0),
        "c": nrm(ks[1], (BATCH, d), 1.0),
        "ctx": nrm(ks[2], (BATCH, CTX_LEN, d), 1.0),
        "c_ctx": nrm(ks[3], (d,), 1.0),
        "ada_w": nrm(ks[4], (DEPTH, d, N_MOD * d), 0.5 * d ** -0.5),
        "ada_b": nrm(ks[5], (DEPTH, N_MOD * d), 0.02),
        "mix_norm": 1.0 + nrm(ks[6], (DEPTH, d), 0.02),
        "ffn_norm": 1.0 + nrm(ks[7], (DEPTH, d), 0.02),
        "even_w_in": nrm(ks[8], (N_EVEN, d, IN_PROJ_WIDTH), d ** -0.5),
        "even_q_gain": 1.0 + nrm(ks[9], (N_EVEN, HEAD_DIM), 0.02),
        "even_k_gain": 1.0 + nrm(ks[10], (N_EVEN, HEAD_DIM), 0.02),
        "even_conv_w": nrm(ks[11], (N_EVEN, SHORT_CONV_K, CONV_WIDTH), SHORT_CONV_K ** -0.5),
        "even_w_out": nrm(ks[12], (N_EVEN, ATTN_WIDTH + CONV_WIDTH, d), (ATTN_WIDTH + CONV_WIDTH) ** -0.5),
        "odd_pool_w": nrm(ks[13], (N_ODD, N_POOL_GROUPS, POOL_GROUP, POOL_GROUP), POOL_GROUP ** -0.5),
        "odd_pool_scale": 1.0 + nrm(ks[14], (N_ODD, d), 0.02),
        "ffn_w_up": nrm(ks[15], (DEPTH, d, 2 * D_FF), d ** -0.5),
        "ffn_conv_w": nrm(ks[16], (DEPTH, FFN_CONV_K, D_FF), FFN_CONV_K ** -0.5),
        "ffn_conv_b": nrm(ks[17], (DEPTH, D_FF), 0.02),
        "ffn_w_down": nrm(ks[18], (DEPTH, D_FF, d), D_FF ** -0.5),
    }

def reference(x, c, ctx, c_ctx, ada_w, ada_b, mix_norm, ffn_norm, even_w_in, even_q_gain, even_k_gain,
              even_conv_w, even_w_out, odd_pool_w, odd_pool_scale, ffn_w_up, ffn_conv_w, ffn_conv_b, ffn_w_down):
    b, n, d = x.shape
    rows = n // GRID_W
    cos, sin = axial_rope_tables(rows)
    silu_c = jax.nn.silu(c)
    silu_cc = jax.nn.silu(c_ctx)
    h_ctx = ctx
    for l in range(DEPTH):
        ctx_later = any(j % 2 == 0 for j in range(l + 1, DEPTH))
        need_ctx = (l % 2 == 0) or ctx_later
        mod_lat = (silu_c @ ada_w[l] + ada_b[l])[:, None, :]
        sh1, sc1, g1, sh2, sc2, g2 = jnp.split(mod_lat, N_MOD, axis=-1)
        a_lat = modulate(rms_norm(x, mix_norm[l]), sh1, sc1)
        if need_ctx:
            mod_ctx = (silu_cc @ ada_w[l] + ada_b[l])[None, None, :]
            csh1, csc1, cg1, csh2, csc2, cg2 = jnp.split(mod_ctx, N_MOD, axis=-1)
            a_ctx = modulate(rms_norm(h_ctx, mix_norm[l]), csh1, csc1)
        if l % 2 == 0:
            e = l // 2
            y_lat, y_ctx = even_mixer(a_lat, a_ctx, cos, sin, even_w_in[e], even_q_gain[e], even_k_gain[e],
                                      even_conv_w[e], even_w_out[e], ctx_later)
        else:
            o = l // 2
            y_lat = pool_mixer(a_lat, odd_pool_w[o], odd_pool_scale[o])
            y_ctx = pool_mixer(a_ctx, odd_pool_w[o], odd_pool_scale[o]) if ctx_later else None
        x = x + g1 * y_lat
        f_lat = modulate(rms_norm(x, ffn_norm[l]), sh2, sc2)
        x = x + g2 * conv_glu(f_lat, ffn_w_up[l], ffn_conv_w[l], ffn_conv_b[l], ffn_w_down[l])
        if ctx_later:
            h_ctx = h_ctx + cg1 * y_ctx
            f_ctx = modulate(rms_norm(h_ctx, ffn_norm[l]), csh2, csc2)
            h_ctx = h_ctx + cg2 * conv_glu(f_ctx, ffn_w_up[l], ffn_conv_w[l], ffn_conv_b[l], ffn_w_down[l])
    return x


_drawn_inputs = setup_inputs


def setup_inputs(seed=0):
    import zlib

    import numpy as np

    out = dict(_drawn_inputs(seed))
    spreads = {}
    factors = {'ctx': 7.528,
     'c_ctx': 2.768,
     'mix_norm': 5.342,
     'ffn_norm': 34.449,
     'even_q_gain': 64.0,
     'even_k_gain': 64.0,
     'odd_pool_scale': 64.0,
     'ffn_conv_b': 50.305}
    for name, (base, spread) in spreads.items():
        noise = np.random.default_rng([zlib.crc32(name.encode()), seed]).standard_normal(out[name].shape)
        drawn = base * np.exp(spread * noise) if base else spread * noise
        out[name] = __import__('jax').numpy.asarray(drawn.astype(out[name].dtype))
    for name, factor in factors.items():
        out[name] = (out[name] * factor).astype(out[name].dtype)
    return out
```

```python
import numpy as np
import concourse.bass as bass
from concourse import mybir
from contextlib import ExitStack
from typing import NamedTuple

P = 128
D, SEQ, CTX = 1024, 512, 256
KT = D // P
TT = SEQ // P
HQ, HKV, HD = 4, 2, 128
KEYS = CTX + SEQ
JT = KEYS // P
FF = 2816
FT = FF // P
PARTS = [(0, 8), (8, 8), (16, 6)]
WINDOWS = (2, 4, 8, 16)
PAD = 8
EPS = 1e-6
GRID_W = 64
THETA = 10000.0

W_IN_COLS = [0, 256, 768, 512, 1536, 2048, 1024, 1792, 2304, 1280]
OUT0 = 10
FFN_SLOTS = FT + 4 * len(PARTS)
FFN_N = [OUT0 + 4, OUT0 + 4 + FFN_SLOTS + 1]
POOL_N = OUT0 + 4 + FFN_SLOTS
N_SLOTS = FFN_N[1] + FFN_SLOTS
ADA_SLOTS = 8

C_C, C_CC, C_ADAB, C_MIXN, C_FFNN, C_POOL, C_QG, C_KG, C_ECW = 0, 8, 16, 112, 128, 144, 152, 153, 154
C_ROWS = [128, 38, 88, 88]
SH1, SC1, G1, SH2, SC2, G2 = range(0, 48, 8)


def c_fcw(layer, tap):
    return 256 + 128 * layer + tap * FT


def c_fcb(layer):
    return 256 + 128 * layer + 3 * FT


def last_gen(n):
    if n < 2:
        return 6 + n
    if n < 4:
        return 9 + 2 * (n - 2)
    if n < POOL_N:
        return n + 8
    if n == POOL_N:
        return n + 11
    return n + 11


def mixer_schedule():
    s = []

    def slot(n, between, after, ada=None):
        for k in range(8):
            s.append(("mm", n, k))
            s.extend(between.get(k, []))
        if ada is not None:
            s.append(("ada", ada))
        s.append(("ev", n))
        s.append(("sp", n + 2))
        s.extend(after)

    slot(0, {}, [], 0)
    slot(1, {2: [("st", 0)], 3: [("st", 1)], 5: [("rot", 0)], 6: [("rot", 1), ("qf", 0)], 7: [("qf", 1)]}, [], 1)
    slot(2, {1: [("st", 2)], 2: [("st", 3)], 4: [("rot", 2)], 5: [("rot", 3), ("qf", 2)], 6: [("qf", 3)]}, [], 2)
    slot(3, {}, [], 3)
    slot(4, {2: [("st", 4)], 3: [("st", 5)], 4: [("st", 6), ("qf", 4)], 5: [("rot", 5)],
             6: [("rot", 6), ("qf", 5)], 7: [("qf", 6)]}, [], 4)
    slot(5, {1: [("sc", 0, 0)], 3: [("sc", 0, 1), ("pn", 0, 0)], 5: [("sc", 0, 2), ("pn", 0, 1)],
             7: [("sc", 0, 3), ("pn", 0, 2)]}, [("cvc", 0), ("pn", 0, 3)])

    def tp(h, j):
        return [("tr", h, j)] + ([("pv", h, j - 1)] if j else [])

    slot(6, {**{k: tp(0, k) for k in range(6)}, 6: [("pv", 0, 5), ("o", 0), ("sc", 1, 0)],
             7: [("sc", 1, 1), ("pn", 1, 0)]}, [("cvb", 0), ("pn", 1, 1)])
    slot(7, {0: [("sc", 1, 2)], 2: [("sc", 1, 3), ("pn", 1, 2)], 3: [("pn", 1, 3)],
             4: tp(1, 0), 5: tp(1, 1), 6: tp(1, 2), 7: tp(1, 3)}, [])
    slot(8, {0: tp(1, 4), 1: tp(1, 5), 2: [("pv", 1, 5), ("o", 1), ("sc", 2, 0)], 4: [("sc", 2, 1), ("pn", 2, 0)],
             6: [("sc", 2, 2), ("pn", 2, 1)], 7: [("sc", 2, 3), ("pn", 2, 2)]}, [("cvc", 1), ("pn", 2, 3)])
    slot(9, {**{k: tp(2, k) for k in range(6)}, 6: [("pv", 2, 5), ("o", 2), ("sc", 3, 0)],
             7: [("sc", 3, 1), ("pn", 3, 0)]}, [("cvb", 1), ("pn", 3, 1)])
    slot(10, {0: [("sc", 3, 2)], 1: [("sc", 3, 3), ("pn", 3, 2), ("pn", 3, 3)],
              3: tp(3, 0) + tp(3, 1) + tp(3, 2) + tp(3, 3) + tp(3, 4) + tp(3, 5) + [("pv", 3, 5), ("o", 3)]},
         [], 5)
    slot(11, {}, [], 6)
    slot(12, {}, [], 7)
    for k in range(8):
        s.append(("mm", 13, k))
    s.append(("ev", 13))
    return s


MIX = mixer_schedule()
T_USE = {u: i for i, u in enumerate(u for u in MIX if u[0] in ("ada", "tr"))}
T_FFN0 = len(T_USE)
T_OUT = T_FFN0 + 12
AUX_USE = {u: i + 2 for i, u in enumerate(u for u in MIX if u[0] in ("st", "rot"))}
AUX_NORM = [1, 2 + len(AUX_USE), 3 + len(AUX_USE), 4 + len(AUX_USE)]
SC_USE = {u: i for i, u in enumerate(u for u in MIX if u[0] == "sc")}
ROTS = [u for u in MIX if u[0] == "rot"]
ADA0 = 8
ADA1 = 12


class Slot(NamedTuple):
    n: object
    r: int
    half: object
    g: object
    gr: int
    gh: object


def slot_at(n0, i=0, u=0):
    g0 = last_gen(n0)
    return Slot(n0 + u + 2 * i, (n0 + u) % 2, (n0 + u) // 2 + i, g0 + u + 2 * i, (g0 + u) % 2, (g0 + u) // 2 + i)


def build(nc, x, c, ctx, c_ctx, ada_w, ada_b, mix_norm, ffn_norm, w_in, q_gain, k_gain, conv_w, w_out,
          pool_w, pool_scale, w_up, fconv_w, fconv_b, w_down, ident_d, perm_d, rope_d, invcount_d, out):
    f32, f32r = mybir.dt.float32, mybir.dt.float32r
    ALU, ACT, AX = mybir.AluOpType, mybir.ActivationFunctionType, mybir.AxisListType

    with ExitStack() as stack:
        def sb(name, shape, dt=f32):
            return stack.enter_context(nc.sbuf_tensor(name, shape, dt))

        def sem(name):
            return stack.enter_context(nc.semaphore(name))

        xT = sb("xT", [P, KT, SEQ])
        a_hi, a_lo = sb("a_hi", [P, KT, SEQ], f32r), sb("a_lo", [P, KT, SEQ], f32r)
        h_hi, h_lo = sb("h_hi", [P, 10, SEQ], f32r), sb("h_lo", [P, 10, SEQ], f32r)
        QK = HQ * SEQ + HKV * KEYS
        qk_hi, qk_lo = sb("qk_hi", [P, QK], f32r), sb("qk_lo", [P, QK], f32r)
        v_hi, v_lo = sb("v_hi", [P, JT, HKV * HD], f32r), sb("v_lo", [P, JT, HKV * HD], f32r)
        w_raw = sb("w_raw", [P, 2, 2048])
        w_hi, w_lo = sb("w_hi", [P, 2, 2048], f32r), sb("w_lo", [P, 2, 2048], f32r)
        tmp = sb("tmp", [P, 6, SEQ])
        ada_raw = sb("ada_raw", [P, 2, 1024])
        acc = sb("acc", [P, SEQ])
        tbl = sb("tbl", [P, 4, SEQ])
        gp = sb("gp", [P, 2, SEQ + 2])
        cb = sb("cb", [P, 2, SEQ])
        ident, perm, ones = sb("ident", [P, P]), sb("perm", [P, P]), sb("ones", [P, P])
        col = sb("col", [P, 4 * P])
        mod = sb("mod", [P, 2, 48])
        modc = sb("modc", [P, 16])
        gain = sb("gain", [P, 5, KT])
        gainc = sb("gainc", [P, KT])
        silu_c = sb("silu_c", [P, 16])
        eps = sb("eps", [P, 1])
        cstat = sb("cstat", [P, 4])
        red = sb("red", [P, 5])
        sm = sb("sm", [P, 4, 2])
        ctxa_hi = h_hi[:, 4:8, :].rearrange("p a (b t) -> p (a b) t", b=2)
        ctxa_lo = h_lo[:, 4:8, :].rearrange("p a (b t) -> p (a b) t", b=2)
        ctx_t = [cb[:, :, :].rearrange("p a (b t) -> p (a b) t", b=2),
                 tbl[:, 2:4, :].rearrange("p a (b t) -> p (a b) t", b=2)]
        stage = tmp[:, :, :].rearrange("p (a b) t -> p a (b t)", b=2)
        p_t = tmp[:, :, :].rearrange("p a t -> p (a t)").rearrange("p (q k) -> p q k", q=4)
        ss, rstd, sq, nt = tmp[:, 0, :], tmp[:, 1, :], tmp[:, 2:4, :], tmp[:, 4:6, :]
        ada_flat = ada_raw[:, :, :].rearrange("p a b -> p (a b)")
        WP = SEQ + 2 * PAD
        apad = [ada_flat[:, 0:WP], ada_flat[:, WP:2 * WP]]
        win = [ada_flat[:, 2 * WP:3 * WP], cb[:, :, :].rearrange("p a t -> p (a t)")[:, 0:WP]]

        pair = [stack.enter_context(nc.psum_tensor(f"pair{i}", [P, 2, SEQ], f32)) for i in range(2)]
        pS = stack.enter_context(nc.psum_tensor("pS", [P, 2, SEQ], f32))
        pT = stack.enter_context(nc.psum_tensor("pT", [P, SEQ], f32))
        pO = stack.enter_context(nc.psum_tensor("pO", [P, SEQ], f32))
        aux = [pS[:, 0, :], pS[:, 1, :], pO[:, :]]
        s_flat = pS[:, :, :].rearrange("p a t -> p (a t)")[:, 0:KEYS]

        const_loaded, rows_loaded, rope_loaded = sem("const_loaded"), sem("rows_loaded"), sem("rope_loaded")
        x_loaded = [sem(f"x_loaded{i}") for i in range(3)]
        w_loaded = [sem(f"w_loaded{i}") for i in range(2)]
        ada_loaded = [sem(f"ada_loaded{i}") for i in range(2)]
        count_loaded = sem("count_loaded")
        rows_zero, set_up = sem("rows_zero"), sem("set_up")
        mm_done = sem("mm_done")
        evac = [sem(f"evac{i}") for i in range(2)]
        ada_mm = sem("ada_mm")
        w_hi_done, w_split = sem("w_hi_done"), sem("w_split")
        t_ready, t_read = sem("t_ready"), sem("t_read")
        aux_ready = sem("aux_ready")
        aux_read = [sem(f"aux_read{i}") for i in range(3)]
        acc_done = sem("acc_done")
        silu_done, mods_done, gains_done = sem("silu_done"), sem("mods_done"), sem("gains_done")
        ctx_ss, ctx_std, ctx_scaled = sem("ctx_ss"), sem("ctx_std"), sem("ctx_scaled")
        ctxa_full, ctxa_half, ctxa_ready = sem("ctxa_full"), sem("ctxa_half"), sem("ctxa_ready")
        sq_ready, ss_added = sem("sq_ready"), sem("ss_added")
        n_ready, a_half, a_ready = sem("n_ready"), sem("a_half"), sem("a_ready")
        pad_ready, pool_full = sem("pad_ready"), sem("pool_full")
        qsq_ready, qn_ready, q_full, q_half, q_done = (
            sem("qsq_ready"), sem("qn_ready"), sem("q_full"), sem("q_half"), sem("q_done"))
        v_half = sem("v_half")
        s_ready, s_max, s_read, p_ready = sem("s_ready"), sem("s_max"), sem("s_read"), sem("p_ready")
        pt_half, pv_done, o_half, o_read = sem("pt_half"), sem("pv_done"), sem("o_half"), sem("o_read")
        cc_ready, y_half, cv_ready = sem("cc_ready"), sem("y_half"), sem("cv_ready")
        conv_ready, g_ready, hh_ready, h_ready = (
            sem("conv_ready"), sem("g_ready"), sem("hh_ready"), sem("h_ready"))
        dve_seq = sem("dve_seq")
        tap_done = sem("tap_done")
        out_sent = [sem(f"out_sent{i}") for i in range(2)]

        def aux_wait(eng, u):
            if u >= 3:
                eng.wait_ge(aux_read[u % 3], u // 3)

        def bank_evacuated(g):
            return evac[g % 2], 2 * (g // 2)

        def pairs(eng, trips, body, unroll=False):
            if unroll:
                for i in range(trips):
                    body(i)
            else:
                with eng.Fori(0, trips) as i:
                    body(i)

        def bank_done(s, v):
            return evac[s.gr], 2 * s.gh + v + 1

        def q_raw(i):
            return tmp[:, 2 * (i % 3), :]

        def q_sq(i):
            return tmp[:, 2 * (i % 3) + 1, :]

        def q_view(t, i):
            if i < HQ:
                return t[:, i * SEQ:(i + 1) * SEQ]
            keys = t[:, HQ * SEQ:].rearrange("p (h t) -> p h t", h=HKV)
            return keys[:, :, 0:CTX] if i == 4 else keys[:, i - 5, CTX:KEYS]

        def q_src(i):
            return q_raw(i).rearrange("p (h t) -> p h t", h=HKV) if i == 4 else q_raw(i)

        final_tiles = tmp[:, 2:6, :]
        FINAL_N = N_SLOTS - 4

        block = stack.enter_context(nc.Block())

        @block.sync
        def _(sp):
            sp.dma_start(ident[:], ident_d).then_inc(const_loaded, 16)
            sp.wait_ge(rows_zero, 1)
            stage_rows = acc[:, :].rearrange("p (a b) -> p a b", a=4)

            def rows(t, r, src):
                n = src.shape[0]
                sp.dma_start(stage_rows[r:r + n, t, :], src).then_inc(rows_loaded, 16)
                return r + n
            r = rows(0, 0, c.rearrange("a (k p) -> (a k) p", p=P))
            r = rows(0, r, c_ctx.rearrange("(k p) -> k p", p=P))
            r = rows(0, r, ada_b.rearrange("l (k p) -> (l k) p", p=P))
            rows(0, r, mix_norm.rearrange("l (k p) -> (l k) p", p=P))
            r = rows(1, 0, ffn_norm.rearrange("l (k p) -> (l k) p", p=P))
            r = rows(1, r, pool_scale.rearrange("l (k p) -> (l k) p", p=P))
            r = rows(1, r, q_gain)
            r = rows(1, r, k_gain)
            rows(1, r, conv_w.rearrange("e t (k p) -> (e t k) p", p=P))
            for l in range(2):
                r = rows(2 + l, 0, fconv_w[l].rearrange("t (k p) -> (t k) p", p=P))
                rows(2 + l, r, fconv_b[l:l + 1].rearrange("a (k p) -> (a k) p", p=P))

            ada_v = ada_w[0].rearrange("(k p) n -> p k n", p=P)

            def load(r, src):
                nk = src.shape[1]
                for k in (0, nk // 2):
                    sp.dma_start(w_raw[:, r, k * 256:(k + nk // 2) * 256].rearrange("p (k n) -> p k n", n=256),
                                 src[:, k:k + nk // 2, :]).then_inc(w_loaded[r], 16)

            def ada_slot(s):
                if s >= 2:
                    sp.wait_ge(ada_mm, s - 1)
                load(s % 2, ada_v[:, :, s * 256:(s + 1) * 256])

            for i in range(6):
                if i >= 3:
                    sp.wait_ge(mm_done, i - 2)
                src = x[0, i * P:(i + 1) * P, :] if i < TT else ctx[0, (i - TT) * P:(i - TT + 1) * P, :]
                sp.dma_start(stage[:, i % 3, :], src).then_inc(x_loaded[i % 3], 16)
                if 1 <= i < 3:
                    ada_slot(i - 1)
            for s in range(2, ADA_SLOTS):
                ada_slot(s)
            sp.dma_start(perm[:], perm_d).then_inc(rope_loaded, 16)
            sp.dma_start(tbl[:, 0:2, :], rope_d.rearrange("p (a t) -> p a t", a=2)).then_inc(rope_loaded, 16)

            in_v = w_in[0].rearrange("(k p) n -> p k n", p=P)
            out_v = w_out[0].rearrange("(k p) n -> p k n", p=P)
            for n in range(OUT0 + 4):
                if n < 2:
                    sp.wait_ge(ada_mm, ADA_SLOTS - 1 + n)
                else:
                    sp.wait_ge(w_split, n - 1)
                src = in_v[:, :, W_IN_COLS[n]:W_IN_COLS[n] + 256] if n < OUT0 else \
                    out_v[:, :, (n - OUT0) * 256:(n - OUT0 + 1) * 256]
                load(n % 2, src)

            for l in range(2):
                n0 = FFN_N[l]
                up_v = w_up[l].rearrange("(k p) (g j n) -> p k g j n", p=P, g=2, j=FT)
                down_v = w_down[l].rearrange("(j p) (s n) -> p j s n", p=P, n=256)
                for j0, nk in PARTS:
                    def up(i):
                        for u in range(2):
                            s = slot_at(n0, i, u)
                            sp.wait_ge(w_split, s.n - 1)
                            for g in range(2):
                                sp.dma_start(w_raw[:, s.r, :].rearrange("p (k g n) -> p k g n", k=KT, g=2)[:, :, g, :],
                                             up_v[:, :, g, j0 + 2 * i + u, :]).then_inc(w_loaded[s.r], 16)
                    pairs(sp, nk // 2, up)
                    n0 += nk

                    def down(i):
                        for u in range(2):
                            s = slot_at(n0, i, u)
                            sp.wait_ge(w_split, s.n - 1)
                            load(s.r, down_v[:, j0:j0 + nk, 2 * i + u, :])
                    pairs(sp, 2, down)
                    n0 += 4
                if l == 0:
                    sp.wait_ge(w_split, POOL_N - 1)
                    load(POOL_N % 2, pool_w[0].rearrange("g (t p) n -> p (g t) n", p=P))
                    sp.dma_start(tbl[:, :, :], invcount_d.rearrange("p (a t) -> p a t", a=4))\
                        .then_inc(count_loaded, 16)

            out_v2 = out[0].rearrange("(b p) (m n) -> p m b n", p=P, n=P)
            for m in range(KT):
                sp.wait_ge(t_read, T_OUT + m + 1)
                sp.dma_start(out_v2[:, m], tmp[:, m % 2, :].rearrange("p (b n) -> p b n", b=TT))\
                    .then_inc(out_sent[m % 2], 16)
            for i in range(2):
                sp.wait_ge(out_sent[i], 16 * KT // 2)

        @block.gpsimd
        def _(pool):
            src0 = ada_w[0].rearrange("(k p) (b n) -> p k b n", p=P, n=512)
            src1 = ada_w[1].rearrange("(k p) (b n) -> p k b n", p=P, n=512)

            def chunks(src, col_block, b):
                for q in range(4):
                    if not (isinstance(b, int) and b == 0 and q < 2):
                        pool.wait_ge(acc_done, 8 * b + 2 * q - 2)
                    pool.dma_start(ada_raw[:, q % 2, :].rearrange("p (k n) -> p k n", k=2),
                                   src[:, 2 * q:2 * q + 2, col_block, :]).then_inc(ada_loaded[q % 2], 16)
            pool.wait_ge(ada_mm, ADA_SLOTS - 2)
            chunks(src0, 4, 0)
            with pool.Fori(0, ADA0 - 1) as b:
                chunks(src0, b + 5, b + 1)
            with pool.Fori(0, ADA1) as b:
                chunks(src1, b, b + ADA0)

        @block.tensor
        def _(pe):
            def product(dst, lh, ll, rh, rl, start, stop):
                nc.tensor.matmul(dst, lh, rh, start=start, stop=False)
                nc.tensor.matmul(dst, lh, rl, start=False, stop=False)
                return nc.tensor.matmul(dst, ll, rh, start=False, stop=stop)

            def stat(u, rhs):
                aux_wait(pe, u)
                nc.tensor.matmul(aux[u % 3], ones[:], rhs, start=True, stop=True).then_inc(aux_ready, 1)

            def step(s, idx, k, nk, rhs_h, rhs_l, ready=None):
                if idx == 0:
                    pe.wait_ge(w_split, s.n + 1)
                    pe.wait_ge(evac[s.gr], 2 * s.gh)
                if ready is not None:
                    pe.wait_ge(*ready)
                for m in range(2):
                    at = k * 256 + m * P
                    ins = product(pair[s.gr][:, m, :], w_hi[:, s.r, at:at + P], w_lo[:, s.r, at:at + P],
                                  rhs_h, rhs_l, idx == 0, idx == nk - 1)
                if idx == nk - 1:
                    ins.then_inc(mm_done, 1)

            pe.wait_ge(set_up, 1)
            pe.wait_ge(const_loaded, 16)
            pe.wait_ge(rows_loaded, 16 * 13)
            for t in range(4):
                ins = nc.tensor.transpose(aux[0][:, t * P:(t + 1) * P], acc[:, t * P:(t + 1) * P], ident[:])
            ins.then_inc(aux_ready, 1)
            for i in range(6):
                pe.wait_ge(x_loaded[i % 3], 16 * (i // 3 + 1))
                if i >= TT:
                    pe.wait_ge(ctx_scaled, i - TT + 1)
                if i >= 2:
                    pe.wait_ge(*bank_evacuated(i))
                for kt in range(KT):
                    ins = nc.tensor.transpose(pair[i % 2][:, kt // 4, kt % 4 * P:(kt % 4 + 1) * P],
                                              stage[:, i % 3, kt * P:(kt + 1) * P], ident[:])
                ins.then_inc(mm_done, 1)
            pe.wait_ge(silu_done, 1)
            for s in range(ADA_SLOTS):
                pe.wait_ge(w_loaded[s % 2], 32 * (s // 2 + 1))
                for m in range(2):
                    at = 2 * (2 * s + m)
                    for k in range(KT):
                        ins = nc.tensor.matmul(pT[:, at:at + 2],
                                               w_raw[:, s % 2, k * 256 + m * P:k * 256 + (m + 1) * P],
                                               silu_c[:, k:16:8], start=(k == 0), stop=(k == KT - 1))
                ins.then_inc(ada_mm, 1)
                if s == 3:
                    pe.wait_ge(ss_added, KT)
                    stat(AUX_NORM[0], ss)

            def in_mm(n, k):
                s = slot_at(n)
                if n == 2:
                    if k >= 6:
                        return
                    if k == 0:
                        pe.wait_ge(w_split, n + 1)
                        pe.wait_ge(*bank_evacuated(8))
                    if k == 4:
                        pe.wait_ge(ctxa_ready, KT)
                        pe.wait_ge(*bank_evacuated(9))
                    g, i = (8, k) if k < 4 else (9, k - 4)
                    ah, al = (a_hi, a_lo) if k < 4 else (ctxa_hi, ctxa_lo)
                    for kt in range(KT):
                        dst = pair[g % 2][:, i // 2, i % 2 * 256:(i % 2 + 1) * 256]
                        w = slice(kt * 256, (kt + 1) * 256)
                        t = slice(i * P, (i + 1) * P)
                        ins = product(dst, ah[:, kt, t], al[:, kt, t], w_hi[:, s.r, w], w_lo[:, s.r, w],
                                      kt == 0, kt == KT - 1)
                    if k in (3, 5):
                        ins.then_inc(mm_done, 1)
                elif n == 3:
                    lat = s._replace(g=10, gr=0, gh=5)
                    step(lat, k, k, KT, a_hi[:, k, :], a_lo[:, k, :])
                    if k == KT - 1:
                        pe.wait_ge(*bank_evacuated(11))
                        for m in range(2):
                            for kt in range(KT):
                                at = kt * 256 + m * P
                                ins = product(pair[1][:, 0, m * CTX:(m + 1) * CTX], w_hi[:, s.r, at:at + P],
                                              w_lo[:, s.r, at:at + P], ctxa_hi[:, kt, :], ctxa_lo[:, kt, :],
                                              kt == 0, kt == KT - 1)
                        ins.then_inc(mm_done, 1)
                elif n < OUT0:
                    step(s, k, k, KT, a_hi[:, k, :], a_lo[:, k, :], (a_ready, k + 1) if n == 0 else None)
                else:
                    kt = (k + 4) % 8
                    ready = None
                    if n == OUT0:
                        ready = (cv_ready, kt - 3) if kt >= 4 else (o_read, kt + 1)
                    step(s, k, kt, KT, h_hi[:, kt, :], h_lo[:, kt, :], ready)

            def ada_transposes(b, use):
                pe.wait_ge(acc_done, 8 * b + 8)
                if isinstance(use, int) and use == 0:
                    pe.wait_ge(mods_done, 1)
                else:
                    pe.wait_ge(t_read, use)
                for i in range(4):
                    ins = nc.tensor.transpose(pT[:, i * P:(i + 1) * P], acc[:, i * P:(i + 1) * P], ident[:])
                ins.then_inc(t_ready, 1)

            pe.wait_ge(rope_loaded, 32)
            for unit in MIX:
                kind = unit[0]
                if kind == "mm":
                    in_mm(unit[1], unit[2])
                elif kind == "ada":
                    ada_transposes(unit[1], T_USE[unit])
                elif kind == "st":
                    pe.wait_ge(qsq_ready, unit[1] + 1)
                    stat(AUX_USE[unit], q_sq(unit[1]))
                elif kind == "rot":
                    u = AUX_USE[unit]
                    pe.wait_ge(qn_ready, ROTS.index(unit) + 1)
                    aux_wait(pe, u)
                    nc.tensor.matmul(aux[u % 3], perm[:], q_raw(unit[1]), start=True, stop=True)\
                        .then_inc(aux_ready, 1)
                elif kind == "sc":
                    _, h, q = unit
                    su = SC_USE[unit]
                    if su == 0:
                        pe.wait_ge(q_done, 7)
                        for b in range(3):
                            pe.wait_ge(aux_read[b], len(range(b, AUX_NORM[1], 3)))
                    else:
                        pe.wait_ge(s_read, su)
                    qs = slice(h * SEQ + q * P, h * SEQ + (q + 1) * P)
                    k0 = HQ * SEQ + (h // 2) * KEYS
                    for at, n in ((0, SEQ), (SEQ, KEYS - SEQ)):
                        ks = slice(k0 + at, k0 + at + n)
                        ins = product(s_flat[:, at:at + n], qk_hi[:, qs], qk_lo[:, qs], qk_hi[:, ks], qk_lo[:, ks],
                                      True, True)
                    ins.then_inc(s_ready, 1)
                elif kind == "tr":
                    _, h, j = unit
                    if j == 0:
                        pe.wait_ge(p_ready, 4 * (h + 1))
                    pe.wait_ge(t_read, T_USE[unit])
                    for q in range(4):
                        ins = nc.tensor.transpose(pT[:, q * P:(q + 1) * P], p_t[:, q, j * P:(j + 1) * P], ident[:])
                    ins.then_inc(t_ready, 1)
                elif kind == "pv":
                    _, h, j = unit
                    pe.wait_ge(t_read, T_USE[("tr", h, j)] + 1)
                    if j == 0 and h:
                        pe.wait_ge(o_read, h)
                    v = slice((h // 2) * HD, (h // 2 + 1) * HD)
                    product(pO[:, :], v_hi[:, j, v], v_lo[:, j, v], h_hi[:, 8 + j % 2, :], h_lo[:, 8 + j % 2, :],
                            j == 0, j == JT - 1).then_inc(pv_done, 1)

            pe.wait_ge(ss_added, 2 * KT)
            stat(AUX_NORM[1], ss)

            def out_transposes(m):
                pe.wait_ge(*bank_done(slot_at(FINAL_N + m // 2), m % 2))
                pe.wait_ge(t_read, T_OUT + m)
                for b in range(TT):
                    ins = nc.tensor.transpose(pT[:, b * P:(b + 1) * P],
                                              final_tiles[:, m % 4, b * P:(b + 1) * P], ident[:])
                ins.then_inc(t_ready, 1)

            for l in range(2):
                n0 = FFN_N[l]
                norm = 1 + 2 * l
                for part, (j0, nk) in enumerate(PARTS):
                    def up(i):
                        for u in range(2):
                            for k in range(KT):
                                step(slot_at(n0, i, u), k, k, KT, a_hi[:, k, :], a_lo[:, k, :],
                                     (a_ready, norm * KT + k + 1) if part == 0 and u == 0 else None)
                    pairs(pe, nk // 2, up)
                    n0 += nk
                    q0 = l * FT + j0
                    last = l == 1 and part == 2

                    def down(i):
                        for u in range(2):
                            for k in range(nk):
                                step(slot_at(n0, i, u), k, k, nk, h_hi[:, k, :], h_lo[:, k, :],
                                     (h_ready, q0 + k + 1) if u == 0 else None)
                                if last and k == 3 and 2 * i + u > 0:
                                    for v in range(2):
                                        out_transposes(2 * (2 * i + u - 1) + v)
                            if l == 0:
                                b = 4 * part + 2 * i + u
                                ada_transposes(ADA0 + b, T_FFN0 + b)
                    pairs(pe, 2, down, unroll=last)
                    n0 += 4
                if l == 0:
                    pe.wait_ge(ss_added, 3 * KT)
                    stat(AUX_NORM[2], ss)
                    pe.wait_ge(w_split, POOL_N + 1)
                    r = POOL_N % 2
                    for t in range(4):
                        g = POOL_N + 8 + t
                        pe.wait_ge(*bank_evacuated(g))
                        for kk in range(2):
                            k = 2 * t + kk
                            pe.wait_ge(a_ready, 2 * KT + k + 1)
                            for m in range(2):
                                at = k * 256 + m * P
                                ins = product(pair[g % 2][:, m, :], w_hi[:, r, at:at + P], w_lo[:, r, at:at + P],
                                              a_hi[:, k, :], a_lo[:, k, :], kk == 0, kk == 1)
                        ins.then_inc(mm_done, 1)
                    pe.wait_ge(ss_added, 4 * KT)
                    stat(AUX_NORM[3], ss)
            for m in (6, 7):
                out_transposes(m)

        @block.scalar
        def _(act):
            def hi_of_slot(s):
                act.wait_ge(w_loaded[s.r], 32 * (ADA_SLOTS // 2 + s.half + 2))
                act.wait_ge(mm_done, s.g + 1)
                nc.scalar.activation(w_hi[:, s.r, :], w_raw[:, s.r, :], ACT.Copy).then_inc(w_hi_done, 1)

            def hi_of_first(n):
                act.wait_ge(w_loaded[n], 32 * (ADA_SLOTS // 2 + 1))
                nc.scalar.activation(w_hi[:, n, :], w_raw[:, n, :], ACT.Copy).then_inc(w_hi_done, 1)

            def square(norm, k, final):
                act.wait_ge(*final)
                f = norm * KT + k
                if f >= 2:
                    act.wait_ge(ss_added, f - 1)
                nc.scalar.activation(sq[:, k % 2, :], xT[:, k, :], ACT.Square).then_inc(sq_ready, 1)

            def norm_std(norm):
                u = AUX_NORM[norm]
                act.wait_ge(aux_ready, u + 1)
                nc.scalar.activation(rstd, aux[u % 3], ACT.Sqrt, bias=eps[:, 0:1], scale=1.0 / D)\
                    .then_inc(aux_read[u % 3], 1)

            def norm_tiles(norm, shift, ks):
                for k in ks:
                    act.wait_ge(n_ready, norm * KT + k + 1)
                    nc.scalar.activation(a_hi[:, k, :], nt[:, k % 2, :], ACT.Identity,
                                         bias=shift[:, k:k + 1]).then_inc(a_half, 1)

            act.wait_ge(aux_ready, 1)
            nc.scalar.activation(col[:, :], aux[0], ACT.Copy).then_inc(aux_read[0], 1)
            act.wait_ge(aux_read[0], 1)
            nc.scalar.activation(silu_c[:, :], col[:, 0:16], ACT.Silu).then_inc(silu_done, 1)

            def tokens_out(i, dst):
                act.wait_ge(mm_done, i + 1)
                nc.scalar.activation(dst, pair[i % 2][:, 0, :].rearrange("p (k t) -> p k t", k=4), ACT.Copy)\
                    .then_inc(evac[i % 2], 1)
            for i in range(TT):
                tokens_out(i, xT[:, 0:4, i * P:(i + 1) * P])
            act.wait_ge(set_up, 1)
            for i in range(2):
                act.wait_ge(x_loaded[(TT + i) % 3], 32)
                if i:
                    act.wait_ge(ctx_ss, 1)
                nc.scalar.activation(tbl[:, 2:4, :].rearrange("p a t -> p (a t)"), stage[:, (TT + i) % 3, :],
                                     ACT.Square, accum_out=cstat[:, i:i + 1]).then_inc(ctx_ss, 1)
            act.wait_ge(ctx_ss, 2)
            nc.scalar.activation(cstat[:, 2:4], cstat[:, 0:2], ACT.Sqrt, bias=eps[:, 0:1], scale=1.0 / D)\
                .then_inc(ctx_std, 1)
            for i in range(2):
                tokens_out(TT + i, ctx_t[0][:, :, i * P:(i + 1) * P])
            for k in range(KT):
                square(0, k, (evac[1], 6))
            norm_std(0)
            sh = mod[:, 0, SH1:SH1 + 8]
            norm_tiles(0, sh, range(4))
            hi_of_first(0)
            norm_tiles(0, sh, range(4, 8))
            hi_of_first(1)
            for k in range(KT):
                act.wait_ge(ctxa_full, k + 1)
                nc.scalar.activation(ctxa_hi[:, k, :], ctx_t[k // 4][:, k % 4, :], ACT.Copy).then_inc(ctxa_half, 1)

            def q_evac(i, g, b, n):
                act.wait_ge(mm_done, g + 1)
                if i >= 3:
                    act.wait_ge(q_done, i - 2)
                nc.scalar.activation(q_sq(i), pair[g % 2][:, b, :], ACT.Square).then_inc(qsq_ready, 1)
                nc.scalar.activation(q_raw(i), pair[g % 2][:, b, :], ACT.Copy).then_inc(evac[g % 2], n)

            def evac_in(n):
                s = slot_at(n)
                if n < 2:
                    q_evac(2 * n, s.g, 0, 1)
                    q_evac(2 * n + 1, s.g, 1, 1)
                elif n == 2:
                    for g, b, j in ((8, 0, 2), (8, 1, 4), (9, 0, 0)):
                        act.wait_ge(mm_done, g + 1)
                        nc.scalar.activation(v_hi[:, j:j + 2, :],
                                             pair[g % 2][:, b, :].rearrange("p (a n) -> p a n", a=2), ACT.Copy)\
                            .then_inc(v_half, 1)
                elif n == 3:
                    q_evac(4, 11, 0, 2)
                    q_evac(5, 10, 0, 1)
                    q_evac(6, 10, 1, 1)
                elif n in (4, 7):
                    act.wait_ge(mm_done, s.g + 1)
                    for v in range(2):
                        nc.scalar.activation(tbl[:, 2 + v, :], pair[s.gr][:, v, :], ACT.Copy).then_inc(evac[s.gr], 1)
                elif n >= OUT0:
                    for v in range(2):
                        square(1, 2 * (n - OUT0) + v, bank_done(s, v))

            for unit in MIX:
                kind = unit[0]
                if kind == "ev":
                    evac_in(unit[1])
                elif kind == "sp":
                    hi_of_slot(slot_at(unit[1] - 2))
                elif kind == "st":
                    u = AUX_USE[unit]
                    act.wait_ge(aux_ready, u + 1)
                    nc.scalar.activation(q_sq(unit[1]), aux[u % 3], ACT.Sqrt, bias=eps[:, 0:1],
                                         scale=1.0 / HD).then_inc(aux_read[u % 3], 1)
                elif kind == "qf":
                    i = unit[1]
                    act.wait_ge(q_full, i + 1)
                    nc.scalar.activation(q_view(qk_hi, i), q_src(i), ACT.Copy).then_inc(q_half, 1)
                elif kind == "sc":
                    _, h, q = unit
                    su = SC_USE[unit]
                    act.wait_ge(s_max, su + 1)
                    if q == 0 and h:
                        act.wait_ge(t_ready, T_USE[("tr", h - 1, JT - 1)] + 1)
                    nc.scalar.activation(p_t[:, q, :], s_flat, ACT.Exp, bias=sm[:, q, 0:1], scale=HD ** -0.5,
                                         accum_out=sm[:, q, 1:2]).then_inc(s_read, 1)
                elif kind == "tr":
                    _, h, j = unit
                    act.wait_ge(t_ready, T_USE[unit] + 1)
                    if h * JT + j >= 2:
                        act.wait_ge(pv_done, h * JT + j - 1)
                    nc.scalar.activation(h_hi[:, 8 + j % 2, :], pT[:, :], ACT.Copy).then_inc(pt_half, 1)
                elif kind == "o":
                    h = unit[1]
                    act.wait_ge(pv_done, JT * (h + 1))
                    nc.scalar.activation(h_hi[:, h, :], pO[:, :], ACT.Copy).then_inc(o_half, 1)
                elif kind == "cvc":
                    s = slot_at(5 + 3 * unit[1])
                    for v in range(2):
                        ct = 2 * unit[1] + v
                        act.wait_ge(*bank_done(s, v))
                        if unit[1]:
                            act.wait_ge(cv_ready, v + 1)
                        nc.scalar.activation(cb[:, v, :], gp[:, v, 1:1 + SEQ], ACT.Copy,
                                             scale=col[:, C_ECW + 4 + ct:C_ECW + 5 + ct]).then_inc(cc_ready, 1)
                elif kind == "cvb":
                    s = slot_at(6 + 3 * unit[1])
                    for v in range(2):
                        act.wait_ge(*bank_done(s, v))
                        nc.scalar.activation(h_hi[:, 4 + 2 * unit[1] + v, :], cb[:, v, :], ACT.Copy)\
                            .then_inc(y_half, 1)

            def pad_row(k):
                act.wait_ge(n_ready, 2 * KT + k + 1)
                nc.scalar.activation(apad[k % 2][:, PAD:PAD + SEQ], nt[:, k % 2, :], ACT.Identity,
                                     bias=mod[:, 1, SH1 + k:SH1 + k + 1]).then_inc(pad_ready, 1)

            def pool_tiles(ks):
                for k in ks:
                    if k + 1 < KT:
                        pad_row(k + 1)
                    act.wait_ge(pool_full, k + 1)
                    nc.scalar.activation(a_hi[:, k, :], nt[:, k % 2, :], ACT.Copy).then_inc(a_half, 1)

            for l in range(2):
                n0 = FFN_N[l]
                norm = 1 + 2 * l
                norm_std(norm)
                sh = mod[:, l, SH2:SH2 + 8]
                norm_tiles(norm, sh, range(4))
                hi_of_slot(slot_at(n0 - 1))
                norm_tiles(norm, sh, range(4, 8))
                for part, (j0, nk) in enumerate(PARTS):
                    q0 = l * FT + j0

                    def up(i):
                        for u in range(2):
                            s = slot_at(n0, i, u)
                            q, jj, v = q0 + u + 2 * i, j0 + u + 2 * i, (q0 + u) % 2
                            act.wait_ge(mm_done, s.g + 1)
                            nc.scalar.activation(cb[:, v, :], pair[s.gr][:, 0, :], ACT.Identity,
                                                 bias=col[:, bass.ds(c_fcb(l) + jj, 1)],
                                                 scale=col[:, bass.ds(c_fcw(l, 1) + jj, 1)])
                            nc.scalar.activation(gp[:, v, 1:1 + SEQ], pair[s.gr][:, 0, :], ACT.Copy)\
                                .then_inc(evac[s.gr], 1)
                            act.wait_ge(conv_ready, q + 1)
                            nc.scalar.activation(cb[:, v, :], cb[:, v, :], ACT.Silu).then_inc(g_ready, 1)
                            act.wait_ge(*bank_done(s, 1))
                            nc.scalar.activation(h_hi[:, 2 * i + u, :], cb[:, v, :], ACT.Copy).then_inc(hh_ready, 1)
                            hi_of_slot(s)
                    pairs(act, nk // 2, up)
                    n0 += nk
                    final = part == 2

                    def out_copy(m):
                        act.wait_ge(t_ready, T_OUT + m + 1)
                        if m >= 2:
                            act.wait_ge(out_sent[m % 2], 16 * (m // 2))
                        nc.scalar.activation(tmp[:, m % 2, :], pT[:, :], ACT.Copy).then_inc(t_read, 1)

                    def down(i):
                        for u in range(2):
                            s = slot_at(n0, i, u)
                            if final and l == 0:
                                for v in range(2):
                                    square(2, 2 * (2 * i + u) + v, bank_done(s, v))
                            if not final or s.n + 2 < min(N_SLOTS, n0 + 5):
                                hi_of_slot(s)
                            if final and l == 1:
                                for v in range(2):
                                    out_copy(2 * (2 * i + u) + v)

                    pairs(act, 2, down, unroll=final)
                    n0 += 4
                if l == 0:
                    norm_std(2)
                    pad_row(0)
                    pool_tiles(range(4))
                    hi_of_slot(slot_at(POOL_N - 1))
                    pool_tiles(range(4, 8))
                    for t in range(4):
                        g = POOL_N + 8 + t
                        for v in range(2):
                            square(3, 2 * t + v, (evac[g % 2], 2 * (g // 2) + v + 1))

        @block.vector
        def _(dve):
            steps = [0]

            def chain(ins):
                steps[0] += 1
                ins.then_inc(dve_seq, 1)
                dve.wait_ge(dve_seq, steps[0])

            def lo(dst, full, hi):
                return nc.vector.tensor_tensor(dst, full, hi.bitcast(f32), ALU.subtract)

            def lo_of_slot(n, r):
                dve.wait_ge(w_hi_done, n + 1)
                lo(w_lo[:, r, :], w_raw[:, r, :], w_hi[:, r, :]).then_inc(w_split, 1)

            def lo_next(s):
                lo_of_slot(s.n + 2, s.r)

            def residual(dst, s, v, factor, old):
                if v == 0:
                    dve.wait_ge(mm_done, s.g + 1)
                nc.vector.scalar_tensor_tensor(out=dst, in0=pair[s.gr][:, v, :], scalar=factor, in1=old,
                                               op0=ALU.mult, op1=ALU.add).then_inc(evac[s.gr], 1)

            def add_square(norm, k):
                f = norm * KT + k
                dve.wait_ge(sq_ready, f + 1)
                if k == 0:
                    nc.vector.tensor_copy(ss, sq[:, 0, :]).then_inc(ss_added, 1)
                else:
                    dve.wait_ge(ss_added, f)
                    nc.vector.tensor_tensor(ss, ss, sq[:, k % 2, :], ALU.add).then_inc(ss_added, 1)

            def rms_inverse(norm):
                u = AUX_NORM[norm]
                dve.wait_ge(aux_read[u % 3], u // 3 + 1)
                chain(nc.vector.reciprocal(rstd, rstd))

            def scaled(norm, k):
                if k >= 2:
                    dve.wait_ge(a_ready, norm * KT + k - 1)
                nc.vector.scalar_tensor_tensor(out=nt[:, k % 2, :], in0=xT[:, k, :], scalar=gain[:, norm, k:k + 1],
                                               in1=rstd, op0=ALU.mult, op1=ALU.mult).then_inc(n_ready, 1)

            def normed_lo(norm, k, shift):
                dve.wait_ge(a_half, norm * KT + k + 1)
                nc.vector.scalar_tensor_tensor(out=a_lo[:, k, :], in0=nt[:, k % 2, :], scalar=shift[:, k:k + 1],
                                               in1=a_hi[:, k, :].bitcast(f32), op0=ALU.add, op1=ALU.subtract)\
                    .then_inc(a_ready, 1)

            def norm_tiles(norm, shift, between):
                rms_inverse(norm)
                for k in range(KT + 1):
                    if k < KT:
                        scaled(norm, k)
                    if k:
                        normed_lo(norm, k - 1, shift)
                    if k == 4:
                        between()

            def gain_of(dst, scale_at, layer, gain_col):
                chain(nc.vector.scalar_tensor_tensor(out=dst, in0=mod[:, layer, scale_at:scale_at + 8], scalar=1.0,
                                                     in1=col[:, gain_col:gain_col + 8], op0=ALU.add, op1=ALU.mult))

            def ada_sum(b):
                for q in range(4):
                    dve.wait_ge(ada_loaded[q % 2], 32 * b + 16 * (q // 2 + 1))
                    for kk in range(2):
                        k = 2 * q + kk
                        w = ada_raw[:, q % 2, kk * 512:(kk + 1) * 512]
                        if k == 0:
                            ins = nc.vector.tensor_scalar(acc[:, :], w, silu_c[:, 0:1], None, ALU.mult)
                        else:
                            dve.wait_ge(acc_done, 8 * b + k)
                            ins = nc.vector.scalar_tensor_tensor(out=acc[:, :], in0=w, scalar=silu_c[:, k:k + 1],
                                                                 in1=acc[:, :], op0=ALU.mult, op1=ALU.add)
                        ins.then_inc(acc_done, 1)

            def ada_columns(use, dst, bias):
                dve.wait_ge(t_ready, use + 1)
                nc.vector.reduce_sum(red[:, 0:4], pT[:, :].rearrange("p (a b) -> p a b", b=P), axis=AX.X)\
                    .then_inc(t_read, 1)
                dve.wait_ge(t_read, use + 1)
                nc.vector.tensor_tensor(dst, red[:, 0:4], bias, ALU.add)

            nc.vector.memset(acc[:, :], 0.0).then_inc(rows_zero, 1)
            nc.vector.memset(ones[:, :], 1.0)
            nc.vector.memset(gp[:, :, :], 0.0)
            nc.vector.memset(eps[:, :], EPS).then_inc(set_up, 1)

            def tokens_out(i, dst):
                dve.wait_ge(mm_done, i + 1)
                dve.wait_ge(*half_evacuated(i))
                nc.vector.tensor_copy(dst, pair[i % 2][:, 1, :].rearrange("p (k t) -> p k t", k=4))\
                    .then_inc(evac[i % 2], 1)

            def half_evacuated(g):
                return evac[g % 2], 2 * (g // 2) + 1
            for i in range(TT):
                tokens_out(i, xT[:, 4:8, i * P:(i + 1) * P])
            dve.wait_ge(ctx_std, 1)
            chain(nc.vector.reciprocal(cstat[:, 2:4], cstat[:, 2:4]))
            for i in range(2):
                t = stage[:, (TT + i) % 3, :]
                nc.vector.tensor_scalar(t, t, cstat[:, 2 + i:3 + i], None, ALU.mult).then_inc(ctx_scaled, 1)
            for i in range(2):
                tokens_out(TT + i, ctx_t[1][:, :, i * P:(i + 1) * P])
            for k in range(KT):
                add_square(0, k)
            dve.wait_ge(ada_mm, ADA_SLOTS)
            nc.vector.tensor_tensor(mod[:, 0, 0:16], pT[:, 0:32:2], col[:, C_ADAB:C_ADAB + 16], ALU.add)
            nc.vector.tensor_tensor(modc[:, :], pT[:, 1:32:2], col[:, C_ADAB:C_ADAB + 16], ALU.add)\
                .then_inc(mods_done, 1)
            dve.wait_ge(mods_done, 1)
            gain_of(gain[:, 0, :], SC1, 0, C_MIXN)
            chain(nc.vector.scalar_tensor_tensor(out=gainc[:, :], in0=modc[:, 8:16], scalar=1.0,
                                                 in1=col[:, C_MIXN:C_MIXN + 8], op0=ALU.add, op1=ALU.mult))
            norm_tiles(0, mod[:, 0, SH1:SH1 + 8], lambda: lo_of_slot(0, 0))
            lo_of_slot(1, 1)
            for k in range(KT + 1):
                if k < KT:
                    t = ctx_t[k // 4][:, k % 4, :]
                    nc.vector.tensor_scalar(t, t, gainc[:, k:k + 1], modc[:, k:k + 1], ALU.mult, ALU.add)\
                        .then_inc(ctxa_full, 1)
                if k:
                    dve.wait_ge(ctxa_half, k)
                    lo(ctxa_lo[:, k - 1, :], ctx_t[(k - 1) // 4][:, (k - 1) % 4, :], ctxa_hi[:, k - 1, :])\
                        .then_inc(ctxa_ready, 1)

            def evac_in(n):
                s = slot_at(n)
                if n == 2:
                    for i, (g, b, j, inc) in enumerate(((8, 0, 2, 1), (8, 1, 4, 1), (9, 0, 0, 2))):
                        dve.wait_ge(v_half, i + 1)
                        lo(v_lo[:, j:j + 2, :], pair[g % 2][:, b, :].rearrange("p (a n) -> p a n", a=2),
                           v_hi[:, j:j + 2, :]).then_inc(evac[g % 2], inc)
                elif n in (5, 8):
                    before = slot_at(n - 1)
                    dve.wait_ge(mm_done, s.g + 1)
                    for v in range(2):
                        dve.wait_ge(*bank_done(before, v))
                        nc.vector.tensor_tensor(gp[:, v, 1:1 + SEQ], pair[s.gr][:, v, :], tbl[:, 2 + v, :], ALU.mult)\
                            .then_inc(evac[s.gr], 1)
                elif n in (6, 9):
                    dve.wait_ge(mm_done, s.g + 1)
                    for v in range(2):
                        nc.vector.tensor_tensor(cb[:, v, :], cb[:, v, :], pair[s.gr][:, v, :], ALU.mult)\
                            .then_inc(evac[s.gr], 1)
                elif n >= OUT0:
                    for v in range(2):
                        m = 2 * (n - OUT0) + v
                        residual(xT[:, m, :], s, v, mod[:, 0, G1 + m:G1 + m + 1], xT[:, m, :])
                    for v in range(2):
                        add_square(1, 2 * (n - OUT0) + v)

            for unit in MIX:
                kind = unit[0]
                if kind == "ada":
                    ada_sum(unit[1])
                    at = 16 + 4 * unit[1]
                    ada_columns(T_USE[unit], mod[:, 0, at:at + 4], col[:, C_ADAB + at:C_ADAB + at + 4])
                elif kind == "ev":
                    evac_in(unit[1])
                elif kind == "sp":
                    lo_of_slot(unit[1], unit[1] % 2)
                elif kind == "st":
                    i, u = unit[1], AUX_USE[unit]
                    dve.wait_ge(aux_read[u % 3], u // 3 + 1)
                    chain(nc.vector.reciprocal(q_sq(i), q_sq(i)))
                    g = C_QG if i < HQ else C_KG
                    nc.vector.scalar_tensor_tensor(out=q_raw(i), in0=q_raw(i), scalar=col[:, g:g + 1], in1=q_sq(i),
                                                   op0=ALU.mult, op1=ALU.mult)\
                        .then_inc(q_full if i == 4 else qn_ready, 1)
                elif kind == "rot":
                    i, u = unit[1], AUX_USE[unit]
                    dve.wait_ge(aux_ready, u + 1)
                    nc.vector.tensor_tensor(q_sq(i), aux[u % 3], tbl[:, 1, :], ALU.mult).then_inc(aux_read[u % 3], 1)
                    chain(nc.vector.tensor_tensor(q_raw(i), q_raw(i), tbl[:, 0, :], ALU.mult))
                    nc.vector.tensor_tensor(q_raw(i), q_raw(i), q_sq(i), ALU.add).then_inc(q_full, 1)
                elif kind == "qf":
                    i = unit[1]
                    dve.wait_ge(q_half, i + 1)
                    lo(q_view(qk_lo, i), q_src(i), q_view(qk_hi, i)).then_inc(q_done, 1)
                elif kind == "sc":
                    q = unit[2]
                    dve.wait_ge(s_ready, SC_USE[unit] + 1)
                    chain(nc.vector.reduce_max(red[:, 4:5], s_flat, axis=AX.X))
                    nc.vector.tensor_scalar(sm[:, q, 0:1], red[:, 4:5], -HD ** -0.5, None, ALU.mult)\
                        .then_inc(s_max, 1)
                elif kind == "pn":
                    _, h, q = unit
                    dve.wait_ge(s_read, SC_USE[("sc", h, q)] + 1)
                    chain(nc.vector.reciprocal(sm[:, q, 1:2], sm[:, q, 1:2]))
                    nc.vector.tensor_scalar(p_t[:, q, :], p_t[:, q, :], sm[:, q, 1:2], None, ALU.mult)\
                        .then_inc(p_ready, 1)
                elif kind == "tr":
                    _, h, j = unit
                    dve.wait_ge(pt_half, h * JT + j + 1)
                    lo(h_lo[:, 8 + j % 2, :], pT[:, :], h_hi[:, 8 + j % 2, :]).then_inc(t_read, 1)
                elif kind == "o":
                    h = unit[1]
                    dve.wait_ge(o_half, h + 1)
                    lo(h_lo[:, h, :], pO[:, :], h_hi[:, h, :]).then_inc(o_read, 1)
                elif kind == "cvc":
                    for tap, at in ((0, 0), (2, 2)):
                        for v in range(2):
                            ct = 2 * unit[1] + v
                            dve.wait_ge(cc_ready, ct + 1)
                            w = C_ECW + 4 * tap + ct
                            chain(nc.vector.scalar_tensor_tensor(
                                out=cb[:, v, :], in0=gp[:, v, at:at + SEQ], scalar=col[:, w:w + 1],
                                in1=cb[:, v, :], op0=ALU.mult, op1=ALU.add))
                elif kind == "cvb":
                    for v in range(2):
                        ct = 2 * unit[1] + v
                        dve.wait_ge(y_half, ct + 1)
                        lo(h_lo[:, 4 + ct, :], cb[:, v, :], h_hi[:, 4 + ct, :]).then_inc(cv_ready, 1)

            def window_mean(k):
                dve.wait_ge(pad_ready, k + 1)
                src, half = apad[k % 2], 0
                for level in range(k // 2 + 1):
                    dst = win[level % 2]
                    if level == 0:
                        lo_i, hi_i = 1, WP
                        a, b = src[:, 0:WP - 1], src[:, 1:WP]
                    else:
                        half = 2 ** (level - 1)
                        lo_i, hi_i = lo_i + half, hi_i - half
                        a, b = src[:, lo_i - half:hi_i - half], src[:, lo_i + half:hi_i + half]
                    chain(nc.vector.tensor_tensor(dst[:, lo_i:hi_i], a, b, ALU.add))
                    src = dst
                chain(nc.vector.tensor_tensor(nt[:, k % 2, :], src[:, PAD:PAD + SEQ], tbl[:, k // 2, :], ALU.mult))
                nc.vector.tensor_tensor(nt[:, k % 2, :], nt[:, k % 2, :], apad[k % 2][:, PAD:PAD + SEQ],
                                        ALU.subtract).then_inc(pool_full, 1)

            def pooled_lo(k):
                dve.wait_ge(a_half, 2 * KT + k + 1)
                lo(a_lo[:, k, :], nt[:, k % 2, :], a_hi[:, k, :]).then_inc(a_ready, 1)

            for l in range(2):
                n0 = FFN_N[l]
                norm = 1 + 2 * l
                if l == 0:
                    gain_of(gain[:, 1, :], SC2, 0, C_FFNN)
                norm_tiles(norm, mod[:, l, SH2:SH2 + 8], lambda: lo_next(slot_at(n0 - 1)))
                for part, (j0, nk) in enumerate(PARTS):
                    q0 = l * FT + j0

                    def up(i):
                        for u in range(2):
                            s = slot_at(n0, i, u)
                            q, jj, v = q0 + u + 2 * i, j0 + u + 2 * i, (q0 + u) % 2
                            dve.wait_ge(*bank_done(s, 0))
                            nc.vector.scalar_tensor_tensor(
                                out=cb[:, v, :], in0=gp[:, v, 0:SEQ], scalar=col[:, bass.ds(c_fcw(l, 0) + jj, 1)],
                                in1=cb[:, v, :], op0=ALU.mult, op1=ALU.add).then_inc(tap_done, 1)
                            dve.wait_ge(tap_done, q + 1)
                            nc.vector.scalar_tensor_tensor(
                                out=cb[:, v, :], in0=gp[:, v, 2:2 + SEQ], scalar=col[:, bass.ds(c_fcw(l, 2) + jj, 1)],
                                in1=cb[:, v, :], op0=ALU.mult, op1=ALU.add).then_inc(conv_ready, 1)
                            dve.wait_ge(g_ready, q + 1)
                            nc.vector.tensor_tensor(cb[:, v, :], cb[:, v, :], pair[s.gr][:, 1, :], ALU.mult)\
                                .then_inc(evac[s.gr], 1)
                            dve.wait_ge(hh_ready, q + 1)
                            lo(h_lo[:, 2 * i + u, :], cb[:, v, :], h_hi[:, 2 * i + u, :]).then_inc(h_ready, 1)
                            lo_next(s)
                    pairs(dve, nk // 2, up)
                    n0 += nk
                    final = part == 2

                    def down(i):
                        for u in range(2):
                            s = slot_at(n0, i, u)
                            b = 4 * part + 2 * i + u
                            if l == 0:
                                ada_sum(ADA0 + b)
                            for v in range(2):
                                m = 2 * (2 * i + u) + v
                                old = xT[:, m, :]
                                if final and l == 1:
                                    if m >= 4:
                                        dve.wait_ge(t_ready, T_OUT + m - 3)
                                    dst = final_tiles[:, m % 4, :]
                                else:
                                    dst = old
                                residual(dst, s, v, mod[:, l, bass.ds(G2 + m, 1)], old)
                            if final and l == 0:
                                for v in range(2):
                                    add_square(2, 2 * (2 * i + u) + v)
                            if l == 0:
                                ada_columns(T_FFN0 + b, mod[:, 1, bass.ds(4 * b, 4)],
                                            col[:, bass.ds(C_ADAB + 48 + 4 * b, 4)])
                            if not final or s.n + 2 < min(N_SLOTS, n0 + 5):
                                lo_next(s)

                    pairs(dve, 2, down, unroll=final)
                    n0 += 4
                if l == 0:
                    for t in apad:
                        nc.vector.memset(t[:, 0:PAD], 0.0)
                        nc.vector.memset(t[:, PAD + SEQ:], 0.0)
                    gain_of(gain[:, 2, :], SC1, 1, C_MIXN + 8)
                    gain_of(gain[:, 3, :], SC2, 1, C_FFNN + 8)
                    chain(nc.vector.tensor_tensor(gain[:, 4, :], mod[:, 1, G1:G1 + 8], col[:, C_POOL:C_POOL + 8],
                                                  ALU.mult))
                    dve.wait_ge(count_loaded, 16)
                    rms_inverse(2)
                    scaled(2, 0)
                    for k in range(KT):
                        if k:
                            pooled_lo(k - 1)
                        if k == 4:
                            lo_next(slot_at(POOL_N - 1))
                        if k + 1 < KT:
                            scaled(2, k + 1)
                        window_mean(k)
                    pooled_lo(KT - 1)
                    for t in range(4):
                        s = Slot(POOL_N, POOL_N % 2, POOL_N // 2, POOL_N + 8 + t, t % 2, (POOL_N + 8 + t) // 2)
                        for v in range(2):
                            m = 2 * t + v
                            residual(xT[:, m, :], s, v, gain[:, 4, m:m + 1], xT[:, m, :])
                        for v in range(2):
                            add_square(3, 2 * t + v)


_INS = ["x", "c", "ctx", "c_ctx", "ada_w", "ada_b", "mix_norm", "ffn_norm", "even_w_in", "even_q_gain",
        "even_k_gain", "even_conv_w", "even_w_out", "odd_pool_w", "odd_pool_scale", "ffn_w_up", "ffn_conv_w",
        "ffn_conv_b", "ffn_w_down"]


def shape_constants():
    f = np.float32
    ident = np.eye(P, dtype=f)
    perm = ident[np.arange(P) ^ (HD // 4)]
    t = np.arange(SEQ)
    axis_dim = HD // 2
    inv_freq = np.power(f(THETA), -np.arange(0, axis_dim, 2, dtype=f) / f(axis_dim)).astype(f)
    pos = np.stack([t // GRID_W, t % GRID_W]).astype(f)
    dim = np.arange(HD)
    ang = pos[dim // axis_dim] * inv_freq[dim % (HD // 4)][:, None]
    sign = np.where(dim // (HD // 4) % 2 == 0, f(-1), f(1))[:, None]
    rope = np.concatenate([np.cos(ang), np.sin(ang) * sign], axis=1).astype(f)
    counts = [np.minimum(t + w - w // 2, SEQ) - np.maximum(t - w // 2, 0) for w in WINDOWS]
    inv = np.concatenate([f(1) / n.astype(f) for n in counts]).astype(f)
    return {"ident": ident, "perm": perm, "rope": rope, "invcount": np.ascontiguousarray(np.tile(inv, (P, 1)))}


def kernel(**inputs):
    import concourse.bacc as _bacc
    from concourse import mybir as _mybir
    from concourse.bass_utils import run_bass_kernel_spmd as _run

    nc = _bacc.Bacc("TRN2", target_bir_lowering=False, num_devices=1, dynamic_dma_scratch_size=4096)
    arrays, args = {}, []
    given = {name: inputs[name] for name in _INS}
    given.update(shape_constants())
    for name, a in given.items():
        a = np.ascontiguousarray(a)
        arrays[f"in_{name}_dram"] = a
        args.append(nc.dram_tensor(f"in_{name}_dram", a.shape, _mybir.dt.from_np(a.dtype), kind="ExternalInput").ap())
    args.append(nc.dram_tensor("out_0_dram", (1, SEQ, D), _mybir.dt.float32, kind="ExternalOutput").ap())
    build(nc, *args)
    r = _run(nc, [arrays], core_ids=[0])
    return r.results[0]["out_0_dram"]
```

```python
import numpy as np
import concourse.bass as bass
from concourse import mybir
from contextlib import ExitStack
from typing import NamedTuple

P = 128
D, SEQ, CTX = 1024, 512, 256
KT = D // P
TT = SEQ // P
HQ, HKV, HD = 4, 2, 128
KEYS = CTX + SEQ
JT = KEYS // P
FF = 2816
FT = FF // P
PARTS = [(0, 8), (8, 8), (16, 6)]
WINDOWS = (2, 4, 8, 16)
PAD = 8
EPS = 1e-6
GRID_W = 64
THETA = 10000.0

W_IN_COLS = [0, 256, 768, 512, 1536, 2048, 1024, 1792, 2304, 1280]
OUT0 = 10
FFN_SLOTS = FT + 4 * len(PARTS)
FFN_N = [OUT0 + 4, OUT0 + 4 + FFN_SLOTS + 1]
POOL_N = OUT0 + 4 + FFN_SLOTS
N_SLOTS = FFN_N[1] + FFN_SLOTS
ADA_SLOTS = 8
ADA_RING = 3
W_BEFORE = 3

C_C, C_CC, C_ADAB, C_MIXN, C_FFNN, C_POOL, C_QG, C_KG, C_ECW = 0, 8, 16, 112, 128, 144, 152, 153, 154
C_ROWS = [128, 38, 88, 88]
SH1, SC1, G1, SH2, SC2, G2 = range(0, 48, 8)


def c_fcw(layer, tap):
    return 256 + 128 * layer + tap * FT


def c_fcb(layer):
    return 256 + 128 * layer + 3 * FT


def last_gen(n):
    if n < 2:
        return 6 + n
    if n < 4:
        return 9 + 2 * (n - 2)
    if n < POOL_N:
        return n + 8
    if n == POOL_N:
        return n + 11
    return n + 11


def mixer_schedule():
    s = []

    def slot(n, between, after, ada=None):
        for k in range(8):
            s.append(("mm", n, k))
            s.extend(between.get(k, []))
            if k == 4 and ada is not None:
                s.append(("ada", ada))
        s.append(("ev", n))
        s.append(("sp", n + 2))
        s.extend(after)

    slot(0, {}, [])
    slot(1, {2: [("st", 0)], 3: [("st", 1)], 5: [("rot", 0)], 6: [("rot", 1), ("qf", 0)], 7: [("qf", 1)]}, [], 0)
    slot(2, {1: [("st", 2)], 2: [("st", 3)], 4: [("rot", 2)], 5: [("rot", 3), ("qf", 2)], 6: [("qf", 3)]}, [])
    slot(3, {}, [], 1)
    slot(4, {2: [("st", 4)], 3: [("st", 5)], 4: [("st", 6), ("qf", 4)], 5: [("rot", 5)],
             6: [("rot", 6), ("qf", 5)], 7: [("qf", 6)]}, [], 2)
    slot(5, {1: [("sc", 0, 0)], 3: [("sc", 0, 1), ("pn", 0, 0)], 5: [("sc", 0, 2), ("pn", 0, 1)],
             7: [("sc", 0, 3), ("pn", 0, 2)]}, [("cvc", 0), ("pn", 0, 3)], 3)

    def tp(h, j):
        return [("tr", h, j)] + ([("pv", h, j - 1)] if j else [])

    slot(6, {**{k: tp(0, k) for k in range(6)}, 6: [("pv", 0, 5), ("o", 0), ("sc", 1, 0)],
             7: [("sc", 1, 1), ("pn", 1, 0)]}, [("cvb", 0), ("pn", 1, 1)])
    slot(7, {0: [("sc", 1, 2)], 2: [("sc", 1, 3), ("pn", 1, 2)], 3: [("pn", 1, 3)],
             4: tp(1, 0), 5: tp(1, 1), 6: tp(1, 2), 7: tp(1, 3)}, [], 4)
    slot(8, {0: tp(1, 4), 1: tp(1, 5), 2: [("pv", 1, 5), ("o", 1), ("sc", 2, 0)], 4: [("sc", 2, 1), ("pn", 2, 0)],
             6: [("sc", 2, 2), ("pn", 2, 1)], 7: [("sc", 2, 3), ("pn", 2, 2)]}, [("cvc", 1), ("pn", 2, 3)], 5)
    slot(9, {**{k: tp(2, k) for k in range(6)}, 6: [("pv", 2, 5), ("o", 2), ("sc", 3, 0)],
             7: [("sc", 3, 1), ("pn", 3, 0)]}, [("cvb", 1), ("pn", 3, 1)])
    slot(10, {0: [("sc", 3, 2)], 1: [("sc", 3, 3), ("pn", 3, 2), ("pn", 3, 3)],
              3: tp(3, 0) + tp(3, 1) + tp(3, 2) + tp(3, 3) + tp(3, 4) + tp(3, 5) + [("pv", 3, 5), ("o", 3)]},
         [], 6)
    slot(11, {}, [], 7)
    slot(12, {}, [])
    for k in range(8):
        s.append(("mm", 13, k))
    s.append(("ev", 13))
    return s


MIX = mixer_schedule()
T_USE = {u: i for i, u in enumerate(u for u in MIX if u[0] in ("ada", "tr"))}
T_FFN0 = len(T_USE)
T_OUT = T_FFN0 + 12
AUX_USE = {u: i + 2 for i, u in enumerate(u for u in MIX if u[0] in ("st", "rot"))}
AUX_NORM = [1, 2 + len(AUX_USE), 3 + len(AUX_USE), 4 + len(AUX_USE)]
SC_USE = {u: i for i, u in enumerate(u for u in MIX if u[0] == "sc")}
ROTS = [u for u in MIX if u[0] == "rot"]
ADA0 = 8
ADA1 = 12


class Slot(NamedTuple):
    n: object
    r: int
    half: object
    g: object
    gr: int
    gh: object


START = [("tokens", 0), ("tokens", 1), ("ada", 0), ("tokens", 2), ("ada", 1), ("tokens", 3), ("ada", 2),
         ("tokens", 4), ("tokens", 5), ("ada", 3), ("ada", 4), ("ada", 5), ("ada", 6), ("ada", 7)]


def slot_at(n0, i=0, u=0):
    g0 = last_gen(n0)
    return Slot(n0 + u + 2 * i, (n0 + u) % 2, (n0 + u) // 2 + i, g0 + u + 2 * i, (g0 + u) % 2, (g0 + u) // 2 + i)


def build(nc, x, c, ctx, c_ctx, ada_w, ada_b, mix_norm, ffn_norm, w_in, q_gain, k_gain, conv_w, w_out,
          pool_w, pool_scale, w_up, fconv_w, fconv_b, w_down, ident_d, perm_d, rope_d, invcount_d, out):
    f32, f32r = mybir.dt.float32, mybir.dt.float32r
    ALU, ACT, AX = mybir.AluOpType, mybir.ActivationFunctionType, mybir.AxisListType

    with ExitStack() as stack:
        def sb(name, shape, dt=f32):
            return stack.enter_context(nc.sbuf_tensor(name, shape, dt))

        def sem(name):
            return stack.enter_context(nc.semaphore(name))

        xT = sb("xT", [P, KT, SEQ])
        a_hi, a_lo = sb("a_hi", [P, KT, SEQ], f32r), sb("a_lo", [P, KT, SEQ], f32r)
        h_hi, h_lo = sb("h_hi", [P, 10, SEQ], f32r), sb("h_lo", [P, 10, SEQ], f32r)
        QK = HQ * SEQ + HKV * KEYS
        qk_hi, qk_lo = sb("qk_hi", [P, QK], f32r), sb("qk_lo", [P, QK], f32r)
        v_hi, v_lo = sb("v_hi", [P, JT, HKV * HD], f32r), sb("v_lo", [P, JT, HKV * HD], f32r)
        w_raw = sb("w_raw", [P, 2, 2048])
        w_hi, w_lo = sb("w_hi", [P, 2, 2048], f32r), sb("w_lo", [P, 2, 2048], f32r)
        tmp = sb("tmp", [P, 6, SEQ])
        ada_raw = sb("ada_raw", [P, 2, 1024])
        acc = sb("acc", [P, 2, SEQ])
        tbl = sb("tbl", [P, 4, SEQ])
        gp = sb("gp", [P, 2, SEQ + 2])
        cb = sb("cb", [P, 2, SEQ])
        ident, ones = sb("ident", [P, P]), sb("ones", [P, P])
        perm = gp[:, 0, 1:1 + P]
        col = sb("col", [P, 4 * P])
        mod = sb("mod", [P, 2, 48])
        modc = sb("modc", [P, 16])
        gain = sb("gain", [P, 5, KT])
        gainc = sb("gainc", [P, KT])
        silu_c = sb("silu_c", [P, 16])
        eps = sb("eps", [P, 1])
        cstat = sb("cstat", [P, 4])
        red = sb("red", [P, 5])
        sm = sb("sm", [P, 4, 2])
        ctxa_hi = h_hi[:, 4:8, :].rearrange("p a (b t) -> p (a b) t", b=2)
        ctxa_lo = h_lo[:, 4:8, :].rearrange("p a (b t) -> p (a b) t", b=2)
        ctx_t = [cb[:, :, :].rearrange("p a (b t) -> p (a b) t", b=2),
                 tbl[:, 2:4, :].rearrange("p a (b t) -> p (a b) t", b=2)]
        stage = tmp[:, :, :].rearrange("p (a b) t -> p a (b t)", b=2)
        p_t = tmp[:, :, :].rearrange("p a t -> p (a t)").rearrange("p (q k) -> p q k", q=4)
        ss, rstd, sq, nt = tmp[:, 0, :], tmp[:, 1, :], tmp[:, 2:4, :], tmp[:, 4:6, :]
        ada_flat = ada_raw[:, :, :].rearrange("p a b -> p (a b)")
        WP = SEQ + 2 * PAD
        apad = [ada_flat[:, 0:WP], ada_flat[:, WP:2 * WP]]
        win = [ada_flat[:, 2 * WP:3 * WP], cb[:, :, :].rearrange("p a t -> p (a t)")[:, 0:WP]]

        pair = [stack.enter_context(nc.psum_tensor(f"pair{i}", [P, 2, SEQ], f32)) for i in range(2)]
        pS = stack.enter_context(nc.psum_tensor("pS", [P, 2, SEQ], f32))
        pT = stack.enter_context(nc.psum_tensor("pT", [P, SEQ], f32))
        pO = stack.enter_context(nc.psum_tensor("pO", [P, SEQ], f32))
        aux = [pS[:, 0, :], pS[:, 1, :], pO[:, :]]
        s_flat = pS[:, :, :].rearrange("p a t -> p (a t)")[:, 0:KEYS]

        const_loaded, rows_loaded, rope_loaded = sem("const_loaded"), sem("rows_loaded"), sem("rope_loaded")
        x_loaded = [sem(f"x_loaded{i}") for i in range(3)]
        w_loaded = [sem(f"w_loaded{i}") for i in range(2)]
        ada_loaded = [sem(f"ada_loaded{i}") for i in range(2)]
        count_loaded = sem("count_loaded")
        rows_zero, set_up = sem("rows_zero"), sem("set_up")
        mm_done = sem("mm_done")
        evac = [sem(f"evac{i}") for i in range(2)]
        ada_mm = sem("ada_mm")
        w_hi_done, w_split = sem("w_hi_done"), sem("w_split")
        t_ready, t_read = sem("t_ready"), sem("t_read")
        aux_ready = sem("aux_ready")
        aux_read = [sem(f"aux_read{i}") for i in range(3)]
        prod_done = sem("prod_done")
        acc_done = sem("acc_done")
        ada_ready = sem("ada_ready")
        ada3_loaded, row_copied, ada_cols = sem("ada3_loaded"), sem("row_copied"), sem("ada_cols")
        silu_done, mods_done, gains_done = sem("silu_done"), sem("mods_done"), sem("gains_done")
        ctx_ss, ctx_std, ctx_scaled = sem("ctx_ss"), sem("ctx_std"), sem("ctx_scaled")
        ctxa_full, ctxa_half, ctxa_ready = sem("ctxa_full"), sem("ctxa_half"), sem("ctxa_ready")
        sq_ready, ss_added = sem("sq_ready"), sem("ss_added")
        n_ready, a_half, a_ready = sem("n_ready"), sem("a_half"), sem("a_ready")
        pad_ready, pool_full = sem("pad_ready"), sem("pool_full")
        qsq_ready, qn_ready, q_full, q_half, q_done = (
            sem("qsq_ready"), sem("qn_ready"), sem("q_full"), sem("q_half"), sem("q_done"))
        v_half = sem("v_half")
        s_ready, s_max, s_read, p_ready = sem("s_ready"), sem("s_max"), sem("s_read"), sem("p_ready")
        pt_half, pv_done, o_half, o_read = sem("pt_half"), sem("pv_done"), sem("o_half"), sem("o_read")
        cc_ready, y_half, cv_ready = sem("cc_ready"), sem("y_half"), sem("cv_ready")
        conv_ready, g_ready, hh_ready, h_ready = (
            sem("conv_ready"), sem("g_ready"), sem("hh_ready"), sem("h_ready"))
        dve_seq = sem("dve_seq")
        tap_done = sem("tap_done")
        out_sent = [sem(f"out_sent{i}") for i in range(2)]

        def aux_wait(eng, u):
            if u >= 3:
                eng.wait_ge(aux_read[u % 3], u // 3)

        ada_slot = [w_raw[:, 0, :], w_raw[:, 1, :], ada_flat]
        ada_slot_loaded = [w_loaded[0], w_loaded[1], ada3_loaded]
        ada_row_bank = [pT, pO]

        def bank_evacuated(g):
            return evac[g % 2], 2 * (g // 2)

        def pairs(eng, trips, body, unroll=False):
            if unroll:
                for i in range(trips):
                    body(i)
            else:
                with eng.Fori(0, trips) as i:
                    body(i)

        def bank_done(s, v):
            return evac[s.gr], 2 * s.gh + v + 1

        def q_raw(i):
            return tmp[:, 2 * (i % 3), :]

        def q_sq(i):
            return tmp[:, 2 * (i % 3) + 1, :]

        def q_view(t, i):
            if i < HQ:
                return t[:, i * SEQ:(i + 1) * SEQ]
            keys = t[:, HQ * SEQ:].rearrange("p (h t) -> p h t", h=HKV)
            return keys[:, :, 0:CTX] if i == 4 else keys[:, i - 5, CTX:KEYS]

        def q_src(i):
            return q_raw(i).rearrange("p (h t) -> p h t", h=HKV) if i == 4 else q_raw(i)

        final_tiles = tmp[:, 2:6, :]
        FINAL_N = N_SLOTS - 4

        block = stack.enter_context(nc.Block())

        @block.sync
        def _(sp):
            sp.dma_start(ident[:], ident_d).then_inc(const_loaded, 16)
            sp.wait_ge(rows_zero, 1)
            stage_rows = acc[:, 0, :].rearrange("p (a b) -> p a b", a=4)

            def rows(t, r, src):
                n = src.shape[0]
                sp.dma_start(stage_rows[r:r + n, t, :], src).then_inc(rows_loaded, 16)
                return r + n
            r = rows(0, 0, c.rearrange("a (k p) -> (a k) p", p=P))
            r = rows(0, r, c_ctx.rearrange("(k p) -> k p", p=P))
            r = rows(0, r, ada_b.rearrange("l (k p) -> (l k) p", p=P))
            rows(0, r, mix_norm.rearrange("l (k p) -> (l k) p", p=P))
            r = rows(1, 0, ffn_norm.rearrange("l (k p) -> (l k) p", p=P))
            r = rows(1, r, pool_scale.rearrange("l (k p) -> (l k) p", p=P))
            r = rows(1, r, q_gain)
            r = rows(1, r, k_gain)
            rows(1, r, conv_w.rearrange("e t (k p) -> (e t k) p", p=P))
            for l in range(2):
                r = rows(2 + l, 0, fconv_w[l].rearrange("t (k p) -> (t k) p", p=P))
                rows(2 + l, r, fconv_b[l:l + 1].rearrange("a (k p) -> (a k) p", p=P))

            ada_v = ada_w[0].rearrange("(k p) n -> p k n", p=P)

            def load(r, src):
                nk = src.shape[1]
                for k in (0, nk // 2):
                    sp.dma_start(w_raw[:, r, k * 256:(k + nk // 2) * 256].rearrange("p (k n) -> p k n", n=256),
                                 src[:, k:k + nk // 2, :]).then_inc(w_loaded[r], 16)

            for kind, i in START:
                if kind == "tokens":
                    if i >= 3:
                        sp.wait_ge(mm_done, i - 2)
                    src = x[0, i * P:(i + 1) * P, :] if i < TT else ctx[0, (i - TT) * P:(i - TT + 1) * P, :]
                    sp.dma_start(stage[:, i % 3, :], src).then_inc(x_loaded[i % 3], 16)
                else:
                    if i >= ADA_RING:
                        sp.wait_ge(ada_mm, i - ADA_RING + 1)
                    for k in (0, 2):
                        sp.dma_start(ada_slot[i % ADA_RING][:, k * 512:(k + 2) * 512]
                                     .rearrange("p (k n) -> p k n", n=512),
                                     ada_v[:, i % 2 * 4 + k:i % 2 * 4 + k + 2, i // 2 * 512:(i // 2 + 1) * 512])\
                            .then_inc(ada_slot_loaded[i % ADA_RING], 16)
            sp.wait_ge(set_up, 1)
            sp.dma_start(perm, perm_d).then_inc(rope_loaded, 16)
            sp.dma_start(tbl[:, 0:2, :], rope_d.rearrange("p (a t) -> p a t", a=2)).then_inc(rope_loaded, 16)

            in_v = w_in[0].rearrange("(k p) n -> p k n", p=P)
            out_v = w_out[0].rearrange("(k p) n -> p k n", p=P)
            for n in range(OUT0 + 4):
                if n < 2:
                    sp.wait_ge(ada_mm, 7 + n)
                else:
                    sp.wait_ge(w_split, n - 1)
                src = in_v[:, :, W_IN_COLS[n]:W_IN_COLS[n] + 256] if n < OUT0 else \
                    out_v[:, :, (n - OUT0) * 256:(n - OUT0 + 1) * 256]
                load(n % 2, src)

            for l in range(2):
                n0 = FFN_N[l]
                up_v = w_up[l].rearrange("(k p) (g j n) -> p k g j n", p=P, g=2, j=FT)
                down_v = w_down[l].rearrange("(j p) (s n) -> p j s n", p=P, n=256)
                for j0, nk in PARTS:
                    def up(i):
                        for u in range(2):
                            s = slot_at(n0, i, u)
                            sp.wait_ge(w_split, s.n - 1)
                            for g in range(2):
                                sp.dma_start(w_raw[:, s.r, :].rearrange("p (k g n) -> p k g n", k=KT, g=2)[:, :, g, :],
                                             up_v[:, :, g, j0 + 2 * i + u, :]).then_inc(w_loaded[s.r], 16)
                    pairs(sp, nk // 2, up)
                    n0 += nk

                    def down(i):
                        for u in range(2):
                            s = slot_at(n0, i, u)
                            sp.wait_ge(w_split, s.n - 1)
                            load(s.r, down_v[:, j0:j0 + nk, 2 * i + u, :])
                    pairs(sp, 2, down)
                    n0 += 4
                if l == 0:
                    sp.wait_ge(w_split, POOL_N - 1)
                    load(POOL_N % 2, pool_w[0].rearrange("g (t p) n -> p (g t) n", p=P))
                    sp.dma_start(tbl[:, :, :], invcount_d.rearrange("p (a t) -> p a t", a=4))\
                        .then_inc(count_loaded, 16)

            out_v2 = out[0].rearrange("(b p) (m n) -> p m b n", p=P, n=P)
            for m in range(KT):
                sp.wait_ge(t_read, T_OUT + m + 1)
                sp.dma_start(out_v2[:, m], tmp[:, m % 2, :].rearrange("p (b n) -> p b n", b=TT))\
                    .then_inc(out_sent[m % 2], 16)
            for i in range(2):
                sp.wait_ge(out_sent[i], 16 * KT // 2)

        @block.gpsimd
        def _(pool):
            src0 = ada_w[0].rearrange("(k p) (b n) -> p k b n", p=P, n=512)
            src1 = ada_w[1].rearrange("(k p) (b n) -> p k b n", p=P, n=512)

            def chunk(src, col_block, q):
                pool.dma_start(ada_raw[:, q % 2, :].rearrange("p (k n) -> p k n", k=2),
                               src[:, 2 * q:2 * q + 2, col_block, :]).then_inc(ada_loaded[q % 2], 16)

            def ada_sum(b, u, src, col_block, next_src, next_block, first=False):
                if first:
                    pool.wait_ge(mods_done, 1)
                else:
                    pool.wait_ge(ada_ready, b - 1)
                for q in range(4):
                    w = ada_raw[:, q % 2, :].rearrange("p (k n) -> p k n", k=2)
                    pool.wait_ge(ada_loaded[q % 2], 32 * b + 16 * (q // 2 + 1))
                    nc.gpsimd.tensor_tensor(w, w, silu_c[:, 2 * q:2 * q + 2].unsqueeze(2).to_broadcast([P, 2, SEQ]),
                                            ALU.mult).then_inc(prod_done, 1)
                    pool.wait_ge(prod_done, 4 * b + q + 1)
                    if q == 0:
                        nc.gpsimd.tensor_tensor(acc[:, u, :], w[:, 0], w[:, 1], ALU.add).then_inc(acc_done, 1)
                    else:
                        for kk in range(2):
                            pool.wait_ge(acc_done, 7 * b + 2 * q - 1 + kk)
                            nc.gpsimd.tensor_tensor(acc[:, u, :], acc[:, u, :], w[:, kk], ALU.add)\
                                .then_inc(acc_done, 1)
                    if q < 2 or next_src is not None:
                        pool.wait_ge(acc_done, 7 * b + 2 * q + 1)
                        if q < 2:
                            chunk(src, col_block, q + 2)
                        else:
                            chunk(next_src, next_block, q - 2)

            pool.wait_ge(ada_mm, 6)
            chunk(src0, 4, 0)
            chunk(src0, 4, 1)
            for b in range(2):
                ada_sum(b, b, src0, b + 4, src0, b + 5, first=True)
            with pool.Fori(0, ADA0 // 2 - 2) as i:
                for u in range(2):
                    ada_sum(2 * i + 2 + u, u, src0, 2 * i + 6 + u, src0, 2 * i + 7 + u)
            ada_sum(ADA0 - 2, 0, src0, ADA0 + 2, src0, ADA0 + 3)
            ada_sum(ADA0 - 1, 1, src0, ADA0 + 3, src1, 0)
            with pool.Fori(0, ADA1 // 2 - 1) as i:
                for u in range(2):
                    ada_sum(2 * i + ADA0 + u, u, src1, 2 * i + u, src1, 2 * i + 1 + u)
            ada_sum(ADA0 + ADA1 - 2, 0, src1, ADA1 - 2, src1, ADA1 - 1)
            ada_sum(ADA0 + ADA1 - 1, 1, src1, ADA1 - 1, None, None)

        @block.tensor
        def _(pe):
            def product(dst, lh, ll, rh, rl, start, stop):
                nc.tensor.matmul(dst, lh, rh, start=start, stop=False)
                nc.tensor.matmul(dst, lh, rl, start=False, stop=False)
                return nc.tensor.matmul(dst, ll, rh, start=False, stop=stop)

            def stat(u, rhs):
                aux_wait(pe, u)
                nc.tensor.matmul(aux[u % 3], ones[:], rhs, start=True, stop=True).then_inc(aux_ready, 1)

            def step(s, idx, k, nk, rhs_h, rhs_l, ready=None):
                if idx == 0:
                    pe.wait_ge(w_split, s.n + 1)
                    pe.wait_ge(evac[s.gr], 2 * s.gh)
                if ready is not None:
                    pe.wait_ge(*ready)
                for m in range(2):
                    at = k * 256 + m * P
                    ins = product(pair[s.gr][:, m, :], w_hi[:, s.r, at:at + P], w_lo[:, s.r, at:at + P],
                                  rhs_h, rhs_l, idx == 0, idx == nk - 1)
                if idx == nk - 1:
                    ins.then_inc(mm_done, 1)

            pe.wait_ge(set_up, 1)
            pe.wait_ge(const_loaded, 16)
            pe.wait_ge(rows_loaded, 16 * 13)
            for t in range(4):
                ins = nc.tensor.transpose(aux[0][:, t * P:(t + 1) * P], acc[:, 0, t * P:(t + 1) * P], ident[:])
            ins.then_inc(aux_ready, 1)

            def token_tile(i):
                pe.wait_ge(x_loaded[i % 3], 16 * (i // 3 + 1))
                if i >= TT:
                    pe.wait_ge(ctx_scaled, i - TT + 1)
                if i >= 2:
                    pe.wait_ge(*bank_evacuated(i))
                for kt in range(KT):
                    ins = nc.tensor.transpose(pair[i % 2][:, kt // 4, kt % 4 * P:(kt % 4 + 1) * P],
                                              stage[:, i % 3, kt * P:(kt + 1) * P], ident[:])
                ins.then_inc(mm_done, 1)

            def ada_rows(s):
                b = s // 2
                if s == 0:
                    pe.wait_ge(silu_done, 1)
                if s % 2 == 0 and b >= 2:
                    pe.wait_ge(row_copied, b - 1)
                pe.wait_ge(ada_slot_loaded[s % ADA_RING], 32 * (s // ADA_RING + 1))
                for kk in range(4):
                    k = 4 * (s % 2) + kk
                    ins = nc.tensor.matmul(ada_row_bank[b % 2][0:2, :], silu_c[:, k:16:8],
                                           ada_slot[s % ADA_RING][:, kk * 512:(kk + 1) * 512],
                                           start=(k == 0), stop=(k == KT - 1))
                ins.then_inc(ada_mm, 1)

            def ada_row_columns(b):
                pe.wait_ge(row_copied, b + 1)
                if b == 0:
                    pe.wait_ge(aux_read[0], 1)
                for i in range(4):
                    at = 2 * (4 * b + i)
                    ins = nc.tensor.transpose(aux[0][:, at:at + 2], acc[0:2, b % 2, i * P:(i + 1) * P],
                                              ident[0:2, 0:2])
                ins.then_inc(ada_cols, 1)

            for kind, i in START:
                if kind == "tokens":
                    token_tile(i)
                else:
                    ada_rows(i)
                    if i == 4:
                        pe.wait_ge(ss_added, KT)
                        stat(AUX_NORM[0], ss)
                    if i % 2 and i > 1:
                        ada_row_columns(i // 2 - 1)
            ada_row_columns(3)

            def in_mm(n, k):
                s = slot_at(n)
                if n == 2:
                    if k >= 6:
                        return
                    if k == 0:
                        pe.wait_ge(w_split, n + 1)
                        pe.wait_ge(*bank_evacuated(8))
                    if k == 4:
                        pe.wait_ge(ctxa_ready, KT)
                        pe.wait_ge(*bank_evacuated(9))
                    g, i = (8, k) if k < 4 else (9, k - 4)
                    ah, al = (a_hi, a_lo) if k < 4 else (ctxa_hi, ctxa_lo)
                    for kt in range(KT):
                        dst = pair[g % 2][:, i // 2, i % 2 * 256:(i % 2 + 1) * 256]
                        w = slice(kt * 256, (kt + 1) * 256)
                        t = slice(i * P, (i + 1) * P)
                        ins = product(dst, ah[:, kt, t], al[:, kt, t], w_hi[:, s.r, w], w_lo[:, s.r, w],
                                      kt == 0, kt == KT - 1)
                    if k in (3, 5):
                        ins.then_inc(mm_done, 1)
                elif n == 3:
                    lat = s._replace(g=10, gr=0, gh=5)
                    step(lat, k, k, KT, a_hi[:, k, :], a_lo[:, k, :])
                    if k == KT - 1:
                        pe.wait_ge(*bank_evacuated(11))
                        for m in range(2):
                            for kt in range(KT):
                                at = kt * 256 + m * P
                                ins = product(pair[1][:, 0, m * CTX:(m + 1) * CTX], w_hi[:, s.r, at:at + P],
                                              w_lo[:, s.r, at:at + P], ctxa_hi[:, kt, :], ctxa_lo[:, kt, :],
                                              kt == 0, kt == KT - 1)
                        ins.then_inc(mm_done, 1)
                elif n < OUT0:
                    step(s, k, k, KT, a_hi[:, k, :], a_lo[:, k, :], (a_ready, k + 1) if n == 0 else None)
                else:
                    kt = (k + 4) % 8
                    ready = None
                    if n == OUT0:
                        ready = (cv_ready, kt - 3) if kt >= 4 else (o_read, kt + 1)
                    step(s, k, kt, KT, h_hi[:, kt, :], h_lo[:, kt, :], ready)

            def ada_reduce(b, u, use):
                pe.wait_ge(acc_done, 7 * b + 7)
                if isinstance(use, int) and use == 0:
                    pe.wait_ge(mods_done, 1)
                else:
                    pe.wait_ge(t_read, use)
                for i in range(4):
                    ins = nc.tensor.matmul(pT[:, i:i + 1], acc[:, u, i * P:(i + 1) * P], ones[:, 0:1],
                                           start=True, stop=True)
                ins.then_inc(ada_ready, 1)

            pe.wait_ge(rope_loaded, 32)
            for unit in MIX:
                kind = unit[0]
                if kind == "mm":
                    in_mm(unit[1], unit[2])
                elif kind == "ada":
                    ada_reduce(unit[1], unit[1] % 2, T_USE[unit])
                elif kind == "st":
                    pe.wait_ge(qsq_ready, unit[1] + 1)
                    stat(AUX_USE[unit], q_sq(unit[1]))
                elif kind == "rot":
                    u = AUX_USE[unit]
                    pe.wait_ge(qn_ready, ROTS.index(unit) + 1)
                    aux_wait(pe, u)
                    nc.tensor.matmul(aux[u % 3], perm, q_raw(unit[1]), start=True, stop=True)\
                        .then_inc(aux_ready, 1)
                elif kind == "sc":
                    _, h, q = unit
                    su = SC_USE[unit]
                    if su == 0:
                        pe.wait_ge(q_done, 7)
                        for b in range(3):
                            pe.wait_ge(aux_read[b], len(range(b, AUX_NORM[1], 3)))
                    else:
                        pe.wait_ge(s_read, su)
                    qs = slice(h * SEQ + q * P, h * SEQ + (q + 1) * P)
                    k0 = HQ * SEQ + (h // 2) * KEYS
                    for at, n in ((0, SEQ), (SEQ, KEYS - SEQ)):
                        ks = slice(k0 + at, k0 + at + n)
                        ins = product(s_flat[:, at:at + n], qk_hi[:, qs], qk_lo[:, qs], qk_hi[:, ks], qk_lo[:, ks],
                                      True, True)
                    ins.then_inc(s_ready, 1)
                elif kind == "tr":
                    _, h, j = unit
                    if j == 0:
                        pe.wait_ge(p_ready, 4 * (h + 1))
                    pe.wait_ge(t_read, T_USE[unit])
                    for q in range(4):
                        ins = nc.tensor.transpose(pT[:, q * P:(q + 1) * P], p_t[:, q, j * P:(j + 1) * P], ident[:])
                    ins.then_inc(t_ready, 1)
                elif kind == "pv":
                    _, h, j = unit
                    pe.wait_ge(t_read, T_USE[("tr", h, j)] + 1)
                    if j == 0 and h:
                        pe.wait_ge(o_read, h)
                    v = slice((h // 2) * HD, (h // 2 + 1) * HD)
                    product(pO[:, :], v_hi[:, j, v], v_lo[:, j, v], h_hi[:, 8 + j % 2, :], h_lo[:, 8 + j % 2, :],
                            j == 0, j == JT - 1).then_inc(pv_done, 1)

            pe.wait_ge(ss_added, 2 * KT)
            stat(AUX_NORM[1], ss)

            def out_transposes(m):
                pe.wait_ge(*bank_done(slot_at(FINAL_N + m // 2), m % 2))
                pe.wait_ge(t_read, T_OUT + m)
                for b in range(TT):
                    ins = nc.tensor.transpose(pT[:, b * P:(b + 1) * P],
                                              final_tiles[:, m % 4, b * P:(b + 1) * P], ident[:])
                ins.then_inc(t_ready, 1)

            for l in range(2):
                n0 = FFN_N[l]
                norm = 1 + 2 * l
                for part, (j0, nk) in enumerate(PARTS):
                    def up(i):
                        for u in range(2):
                            for k in range(KT):
                                step(slot_at(n0, i, u), k, k, KT, a_hi[:, k, :], a_lo[:, k, :],
                                     (a_ready, norm * KT + k + 1) if part == 0 and u == 0 else None)
                    pairs(pe, nk // 2, up)
                    n0 += nk
                    q0 = l * FT + j0
                    last = l == 1 and part == 2

                    def down(i):
                        for u in range(2):
                            for k in range(nk):
                                step(slot_at(n0, i, u), k, k, nk, h_hi[:, k, :], h_lo[:, k, :],
                                     (h_ready, q0 + k + 1) if u == 0 else None)
                                if l == 0 and k == 4:
                                    b = 4 * part + 2 * i + u
                                    ada_reduce(ADA0 + b, u, T_FFN0 + b)
                                if last and k == 3 and 2 * i + u > 0:
                                    for v in range(2):
                                        out_transposes(2 * (2 * i + u - 1) + v)
                    pairs(pe, 2, down, unroll=last)
                    n0 += 4
                if l == 0:
                    pe.wait_ge(ss_added, 3 * KT)
                    stat(AUX_NORM[2], ss)
                    pe.wait_ge(w_split, POOL_N + 1)
                    r = POOL_N % 2
                    for t in range(4):
                        g = POOL_N + 8 + t
                        pe.wait_ge(*bank_evacuated(g))
                        for kk in range(2):
                            k = 2 * t + kk
                            pe.wait_ge(a_ready, 2 * KT + k + 1)
                            for m in range(2):
                                at = k * 256 + m * P
                                ins = product(pair[g % 2][:, m, :], w_hi[:, r, at:at + P], w_lo[:, r, at:at + P],
                                              a_hi[:, k, :], a_lo[:, k, :], kk == 0, kk == 1)
                        ins.then_inc(mm_done, 1)
                    pe.wait_ge(ss_added, 4 * KT)
                    stat(AUX_NORM[3], ss)
            for m in (6, 7):
                out_transposes(m)

        @block.scalar
        def _(act):
            def hi_of_slot(s):
                act.wait_ge(w_loaded[s.r], 32 * (W_BEFORE + s.half + 2))
                act.wait_ge(mm_done, s.g + 1)
                nc.scalar.activation(w_hi[:, s.r, :], w_raw[:, s.r, :], ACT.Copy).then_inc(w_hi_done, 1)

            def hi_of_first(n):
                act.wait_ge(w_loaded[n], 32 * (W_BEFORE + 1))
                nc.scalar.activation(w_hi[:, n, :], w_raw[:, n, :], ACT.Copy).then_inc(w_hi_done, 1)

            def square(norm, k, final):
                act.wait_ge(*final)
                f = norm * KT + k
                if f >= 2:
                    act.wait_ge(ss_added, f - 1)
                nc.scalar.activation(sq[:, k % 2, :], xT[:, k, :], ACT.Square).then_inc(sq_ready, 1)

            def norm_std(norm):
                u = AUX_NORM[norm]
                act.wait_ge(aux_ready, u + 1)
                nc.scalar.activation(rstd, aux[u % 3], ACT.Sqrt, bias=eps[:, 0:1], scale=1.0 / D)\
                    .then_inc(aux_read[u % 3], 1)

            def norm_tiles(norm, shift, ks):
                for k in ks:
                    act.wait_ge(n_ready, norm * KT + k + 1)
                    nc.scalar.activation(a_hi[:, k, :], nt[:, k % 2, :], ACT.Identity,
                                         bias=shift[:, k:k + 1]).then_inc(a_half, 1)

            act.wait_ge(aux_ready, 1)
            nc.scalar.activation(col[:, :], aux[0], ACT.Copy).then_inc(aux_read[0], 1)
            act.wait_ge(aux_read[0], 1)
            nc.scalar.activation(silu_c[:, :], col[:, 0:16], ACT.Silu).then_inc(silu_done, 1)

            def tokens_out(i, dst):
                act.wait_ge(mm_done, i + 1)
                nc.scalar.activation(dst, pair[i % 2][:, 0, :].rearrange("p (k t) -> p k t", k=4), ACT.Copy)\
                    .then_inc(evac[i % 2], 1)

            def copy_rows(b):
                act.wait_ge(ada_mm, 2 * b + 2)
                if b >= 2:
                    act.wait_ge(ada_cols, b - 1)
                nc.scalar.activation(acc[0:2, b % 2, :], ada_row_bank[b % 2][0:2, :], ACT.Copy)\
                    .then_inc(row_copied, 1)

            for i in range(TT):
                tokens_out(i, xT[:, 0:4, i * P:(i + 1) * P])
            copy_rows(0)
            act.wait_ge(set_up, 1)
            for i in range(2):
                act.wait_ge(x_loaded[(TT + i) % 3], 32)
                if i:
                    act.wait_ge(ctx_ss, 1)
                nc.scalar.activation(tbl[:, 2:4, :].rearrange("p a t -> p (a t)"), stage[:, (TT + i) % 3, :],
                                     ACT.Square, accum_out=cstat[:, i:i + 1]).then_inc(ctx_ss, 1)
            act.wait_ge(ctx_ss, 2)
            nc.scalar.activation(cstat[:, 2:4], cstat[:, 0:2], ACT.Sqrt, bias=eps[:, 0:1], scale=1.0 / D)\
                .then_inc(ctx_std, 1)
            for i in range(2):
                tokens_out(TT + i, ctx_t[0][:, :, i * P:(i + 1) * P])
            copy_rows(1)
            for k in range(KT):
                square(0, k, (evac[1], 6))
            norm_std(0)
            copy_rows(2)
            copy_rows(3)
            sh = mod[:, 0, SH1:SH1 + 8]
            norm_tiles(0, sh, range(4))
            hi_of_first(0)
            norm_tiles(0, sh, range(4, 8))
            hi_of_first(1)
            for k in range(KT):
                act.wait_ge(ctxa_full, k + 1)
                nc.scalar.activation(ctxa_hi[:, k, :], ctx_t[k // 4][:, k % 4, :], ACT.Copy).then_inc(ctxa_half, 1)

            def q_evac(i, g, b, n):
                act.wait_ge(mm_done, g + 1)
                if i >= 3:
                    act.wait_ge(q_done, i - 2)
                nc.scalar.activation(q_sq(i), pair[g % 2][:, b, :], ACT.Square).then_inc(qsq_ready, 1)
                nc.scalar.activation(q_raw(i), pair[g % 2][:, b, :], ACT.Copy).then_inc(evac[g % 2], n)

            def evac_in(n):
                s = slot_at(n)
                if n < 2:
                    q_evac(2 * n, s.g, 0, 1)
                    q_evac(2 * n + 1, s.g, 1, 1)
                elif n == 2:
                    for g, b, j in ((8, 0, 2), (8, 1, 4), (9, 0, 0)):
                        act.wait_ge(mm_done, g + 1)
                        nc.scalar.activation(v_hi[:, j:j + 2, :],
                                             pair[g % 2][:, b, :].rearrange("p (a n) -> p a n", a=2), ACT.Copy)\
                            .then_inc(v_half, 1)
                elif n == 3:
                    q_evac(4, 11, 0, 2)
                    q_evac(5, 10, 0, 1)
                    q_evac(6, 10, 1, 1)
                elif n in (4, 7):
                    act.wait_ge(mm_done, s.g + 1)
                    for v in range(2):
                        nc.scalar.activation(tbl[:, 2 + v, :], pair[s.gr][:, v, :], ACT.Copy).then_inc(evac[s.gr], 1)
                elif n >= OUT0:
                    for v in range(2):
                        square(1, 2 * (n - OUT0) + v, bank_done(s, v))

            for unit in MIX:
                kind = unit[0]
                if kind == "ev":
                    evac_in(unit[1])
                elif kind == "sp":
                    hi_of_slot(slot_at(unit[1] - 2))
                elif kind == "st":
                    u = AUX_USE[unit]
                    act.wait_ge(aux_ready, u + 1)
                    nc.scalar.activation(q_sq(unit[1]), aux[u % 3], ACT.Sqrt, bias=eps[:, 0:1],
                                         scale=1.0 / HD).then_inc(aux_read[u % 3], 1)
                elif kind == "qf":
                    i = unit[1]
                    act.wait_ge(q_full, i + 1)
                    nc.scalar.activation(q_view(qk_hi, i), q_src(i), ACT.Copy).then_inc(q_half, 1)
                elif kind == "sc":
                    _, h, q = unit
                    su = SC_USE[unit]
                    act.wait_ge(s_max, su + 1)
                    if q == 0 and h:
                        act.wait_ge(t_ready, h * JT)
                    nc.scalar.activation(p_t[:, q, :], s_flat, ACT.Exp, bias=sm[:, q, 0:1], scale=HD ** -0.5,
                                         accum_out=sm[:, q, 1:2]).then_inc(s_read, 1)
                elif kind == "tr":
                    _, h, j = unit
                    act.wait_ge(t_ready, h * JT + j + 1)
                    if h * JT + j >= 2:
                        act.wait_ge(pv_done, h * JT + j - 1)
                    nc.scalar.activation(h_hi[:, 8 + j % 2, :], pT[:, :], ACT.Copy).then_inc(pt_half, 1)
                elif kind == "o":
                    h = unit[1]
                    act.wait_ge(pv_done, JT * (h + 1))
                    nc.scalar.activation(h_hi[:, h, :], pO[:, :], ACT.Copy).then_inc(o_half, 1)
                elif kind == "cvc":
                    s = slot_at(5 + 3 * unit[1])
                    for v in range(2):
                        ct = 2 * unit[1] + v
                        act.wait_ge(*bank_done(s, v))
                        if unit[1]:
                            act.wait_ge(cv_ready, v + 1)
                        nc.scalar.activation(cb[:, v, :], gp[:, v, 1:1 + SEQ], ACT.Copy,
                                             scale=col[:, C_ECW + 4 + ct:C_ECW + 5 + ct]).then_inc(cc_ready, 1)
                elif kind == "cvb":
                    s = slot_at(6 + 3 * unit[1])
                    for v in range(2):
                        act.wait_ge(*bank_done(s, v))
                        nc.scalar.activation(h_hi[:, 4 + 2 * unit[1] + v, :], cb[:, v, :], ACT.Copy)\
                            .then_inc(y_half, 1)

            def pad_row(k):
                act.wait_ge(n_ready, 2 * KT + k + 1)
                nc.scalar.activation(apad[k % 2][:, PAD:PAD + SEQ], nt[:, k % 2, :], ACT.Identity,
                                     bias=mod[:, 1, SH1 + k:SH1 + k + 1]).then_inc(pad_ready, 1)

            def pool_tiles(ks):
                for k in ks:
                    if k + 1 < KT:
                        pad_row(k + 1)
                    act.wait_ge(pool_full, k + 1)
                    nc.scalar.activation(a_hi[:, k, :], nt[:, k % 2, :], ACT.Copy).then_inc(a_half, 1)

            for l in range(2):
                n0 = FFN_N[l]
                norm = 1 + 2 * l
                norm_std(norm)
                sh = mod[:, l, SH2:SH2 + 8]
                norm_tiles(norm, sh, range(4))
                hi_of_slot(slot_at(n0 - 1))
                norm_tiles(norm, sh, range(4, 8))
                for part, (j0, nk) in enumerate(PARTS):
                    q0 = l * FT + j0

                    def up(i):
                        for u in range(2):
                            s = slot_at(n0, i, u)
                            q, jj, v = q0 + u + 2 * i, j0 + u + 2 * i, (q0 + u) % 2
                            act.wait_ge(mm_done, s.g + 1)
                            nc.scalar.activation(cb[:, v, :], pair[s.gr][:, 0, :], ACT.Identity,
                                                 bias=col[:, bass.ds(c_fcb(l) + jj, 1)],
                                                 scale=col[:, bass.ds(c_fcw(l, 1) + jj, 1)])
                            nc.scalar.activation(gp[:, v, 1:1 + SEQ], pair[s.gr][:, 0, :], ACT.Copy)\
                                .then_inc(evac[s.gr], 1)
                            act.wait_ge(conv_ready, q + 1)
                            nc.scalar.activation(cb[:, v, :], cb[:, v, :], ACT.Silu).then_inc(g_ready, 1)
                            act.wait_ge(*bank_done(s, 1))
                            nc.scalar.activation(h_hi[:, 2 * i + u, :], cb[:, v, :], ACT.Copy).then_inc(hh_ready, 1)
                            hi_of_slot(s)
                    pairs(act, nk // 2, up)
                    n0 += nk
                    final = part == 2

                    def out_copy(m):
                        act.wait_ge(t_ready, HQ * JT + m + 1)
                        if m >= 2:
                            act.wait_ge(out_sent[m % 2], 16 * (m // 2))
                        nc.scalar.activation(tmp[:, m % 2, :], pT[:, :], ACT.Copy).then_inc(t_read, 1)

                    def down(i):
                        for u in range(2):
                            s = slot_at(n0, i, u)
                            if final and l == 0:
                                for v in range(2):
                                    square(2, 2 * (2 * i + u) + v, bank_done(s, v))
                            if not final or s.n + 2 < min(N_SLOTS, n0 + 5):
                                hi_of_slot(s)
                            if final and l == 1:
                                for v in range(2):
                                    out_copy(2 * (2 * i + u) + v)

                    pairs(act, 2, down, unroll=final)
                    n0 += 4
                if l == 0:
                    norm_std(2)
                    pad_row(0)
                    pool_tiles(range(4))
                    hi_of_slot(slot_at(POOL_N - 1))
                    pool_tiles(range(4, 8))
                    for t in range(4):
                        g = POOL_N + 8 + t
                        for v in range(2):
                            square(3, 2 * t + v, (evac[g % 2], 2 * (g // 2) + v + 1))

        @block.vector
        def _(dve):
            steps = [0]

            def chain(ins):
                steps[0] += 1
                ins.then_inc(dve_seq, 1)
                dve.wait_ge(dve_seq, steps[0])

            def lo(dst, full, hi):
                return nc.vector.tensor_tensor(dst, full, hi.bitcast(f32), ALU.subtract)

            def lo_of_slot(n, r):
                dve.wait_ge(w_hi_done, n + 1)
                lo(w_lo[:, r, :], w_raw[:, r, :], w_hi[:, r, :]).then_inc(w_split, 1)

            def lo_next(s):
                lo_of_slot(s.n + 2, s.r)

            def residual(dst, s, v, factor, old):
                if v == 0:
                    dve.wait_ge(mm_done, s.g + 1)
                nc.vector.scalar_tensor_tensor(out=dst, in0=pair[s.gr][:, v, :], scalar=factor, in1=old,
                                               op0=ALU.mult, op1=ALU.add).then_inc(evac[s.gr], 1)

            def add_square(norm, k):
                f = norm * KT + k
                dve.wait_ge(sq_ready, f + 1)
                if k == 0:
                    nc.vector.tensor_copy(ss, sq[:, 0, :]).then_inc(ss_added, 1)
                else:
                    dve.wait_ge(ss_added, f)
                    nc.vector.tensor_tensor(ss, ss, sq[:, k % 2, :], ALU.add).then_inc(ss_added, 1)

            def rms_inverse(norm):
                u = AUX_NORM[norm]
                dve.wait_ge(aux_read[u % 3], u // 3 + 1)
                chain(nc.vector.reciprocal(rstd, rstd))

            def scaled(norm, k):
                if k >= 2:
                    dve.wait_ge(a_ready, norm * KT + k - 1)
                nc.vector.scalar_tensor_tensor(out=nt[:, k % 2, :], in0=xT[:, k, :], scalar=gain[:, norm, k:k + 1],
                                               in1=rstd, op0=ALU.mult, op1=ALU.mult).then_inc(n_ready, 1)

            def normed_lo(norm, k, shift):
                dve.wait_ge(a_half, norm * KT + k + 1)
                nc.vector.scalar_tensor_tensor(out=a_lo[:, k, :], in0=nt[:, k % 2, :], scalar=shift[:, k:k + 1],
                                               in1=a_hi[:, k, :].bitcast(f32), op0=ALU.add, op1=ALU.subtract)\
                    .then_inc(a_ready, 1)

            def norm_tiles(norm, shift, between):
                rms_inverse(norm)
                for k in range(KT + 1):
                    if k < KT:
                        scaled(norm, k)
                    if k:
                        normed_lo(norm, k - 1, shift)
                    if k == 4:
                        between()

            def gain_of(dst, scale_at, layer, gain_col):
                chain(nc.vector.scalar_tensor_tensor(out=dst, in0=mod[:, layer, scale_at:scale_at + 8], scalar=1.0,
                                                     in1=col[:, gain_col:gain_col + 8], op0=ALU.add, op1=ALU.mult))

            def ada_columns(b, dst, bias):
                dve.wait_ge(ada_ready, b + 1)
                nc.vector.tensor_tensor(dst, pT[:, 0:4], bias, ALU.add).then_inc(t_read, 1)

            nc.vector.memset(acc[:, 0, :], 0.0).then_inc(rows_zero, 1)
            nc.vector.memset(ones[:, :], 1.0)
            nc.vector.memset(gp[:, :, :], 0.0)
            nc.vector.memset(eps[:, :], EPS).then_inc(set_up, 1)

            def tokens_out(i, dst):
                dve.wait_ge(mm_done, i + 1)
                dve.wait_ge(*half_evacuated(i))
                nc.vector.tensor_copy(dst, pair[i % 2][:, 1, :].rearrange("p (k t) -> p k t", k=4))\
                    .then_inc(evac[i % 2], 1)

            def half_evacuated(g):
                return evac[g % 2], 2 * (g // 2) + 1
            for i in range(TT):
                tokens_out(i, xT[:, 4:8, i * P:(i + 1) * P])
            dve.wait_ge(ctx_std, 1)
            chain(nc.vector.reciprocal(cstat[:, 2:4], cstat[:, 2:4]))
            for i in range(2):
                t = stage[:, (TT + i) % 3, :]
                nc.vector.tensor_scalar(t, t, cstat[:, 2 + i:3 + i], None, ALU.mult).then_inc(ctx_scaled, 1)
            for i in range(2):
                tokens_out(TT + i, ctx_t[1][:, :, i * P:(i + 1) * P])
            for k in range(KT):
                add_square(0, k)
            dve.wait_ge(ada_cols, 4)
            nc.vector.tensor_tensor(mod[:, 0, 0:16], aux[0][:, 0:32:2], col[:, C_ADAB:C_ADAB + 16], ALU.add)
            nc.vector.tensor_tensor(modc[:, :], aux[0][:, 1:32:2], col[:, C_ADAB:C_ADAB + 16], ALU.add)\
                .then_inc(mods_done, 1)
            dve.wait_ge(mods_done, 1)
            gain_of(gain[:, 0, :], SC1, 0, C_MIXN)
            chain(nc.vector.scalar_tensor_tensor(out=gainc[:, :], in0=modc[:, 8:16], scalar=1.0,
                                                 in1=col[:, C_MIXN:C_MIXN + 8], op0=ALU.add, op1=ALU.mult))
            norm_tiles(0, mod[:, 0, SH1:SH1 + 8], lambda: lo_of_slot(0, 0))
            lo_of_slot(1, 1)
            for k in range(KT + 1):
                if k < KT:
                    t = ctx_t[k // 4][:, k % 4, :]
                    nc.vector.tensor_scalar(t, t, gainc[:, k:k + 1], modc[:, k:k + 1], ALU.mult, ALU.add)\
                        .then_inc(ctxa_full, 1)
                if k:
                    dve.wait_ge(ctxa_half, k)
                    lo(ctxa_lo[:, k - 1, :], ctx_t[(k - 1) // 4][:, (k - 1) % 4, :], ctxa_hi[:, k - 1, :])\
                        .then_inc(ctxa_ready, 1)

            def evac_in(n):
                s = slot_at(n)
                if n == 2:
                    for i, (g, b, j, inc) in enumerate(((8, 0, 2, 1), (8, 1, 4, 1), (9, 0, 0, 2))):
                        dve.wait_ge(v_half, i + 1)
                        lo(v_lo[:, j:j + 2, :], pair[g % 2][:, b, :].rearrange("p (a n) -> p a n", a=2),
                           v_hi[:, j:j + 2, :]).then_inc(evac[g % 2], inc)
                elif n in (5, 8):
                    before = slot_at(n - 1)
                    dve.wait_ge(mm_done, s.g + 1)
                    for v in range(2):
                        dve.wait_ge(*bank_done(before, v))
                        nc.vector.tensor_tensor(gp[:, v, 1:1 + SEQ], pair[s.gr][:, v, :], tbl[:, 2 + v, :], ALU.mult)\
                            .then_inc(evac[s.gr], 1)
                elif n in (6, 9):
                    dve.wait_ge(mm_done, s.g + 1)
                    for v in range(2):
                        nc.vector.tensor_tensor(cb[:, v, :], cb[:, v, :], pair[s.gr][:, v, :], ALU.mult)\
                            .then_inc(evac[s.gr], 1)
                elif n >= OUT0:
                    for v in range(2):
                        m = 2 * (n - OUT0) + v
                        residual(xT[:, m, :], s, v, mod[:, 0, G1 + m:G1 + m + 1], xT[:, m, :])
                    for v in range(2):
                        add_square(1, 2 * (n - OUT0) + v)

            for unit in MIX:
                kind = unit[0]
                if kind == "ada":
                    at = 16 + 4 * unit[1]
                    ada_columns(unit[1], mod[:, 0, at:at + 4], col[:, C_ADAB + at:C_ADAB + at + 4])
                elif kind == "ev":
                    evac_in(unit[1])
                elif kind == "sp":
                    lo_of_slot(unit[1], unit[1] % 2)
                elif kind == "st":
                    i, u = unit[1], AUX_USE[unit]
                    dve.wait_ge(aux_read[u % 3], u // 3 + 1)
                    chain(nc.vector.reciprocal(q_sq(i), q_sq(i)))
                    g = C_QG if i < HQ else C_KG
                    nc.vector.scalar_tensor_tensor(out=q_raw(i), in0=q_raw(i), scalar=col[:, g:g + 1], in1=q_sq(i),
                                                   op0=ALU.mult, op1=ALU.mult)\
                        .then_inc(q_full if i == 4 else qn_ready, 1)
                elif kind == "rot":
                    i, u = unit[1], AUX_USE[unit]
                    dve.wait_ge(aux_ready, u + 1)
                    nc.vector.tensor_tensor(q_sq(i), aux[u % 3], tbl[:, 1, :], ALU.mult).then_inc(aux_read[u % 3], 1)
                    chain(nc.vector.tensor_tensor(q_raw(i), q_raw(i), tbl[:, 0, :], ALU.mult))
                    nc.vector.tensor_tensor(q_raw(i), q_raw(i), q_sq(i), ALU.add).then_inc(q_full, 1)
                elif kind == "qf":
                    i = unit[1]
                    dve.wait_ge(q_half, i + 1)
                    lo(q_view(qk_lo, i), q_src(i), q_view(qk_hi, i)).then_inc(q_done, 1)
                elif kind == "sc":
                    q = unit[2]
                    dve.wait_ge(s_ready, SC_USE[unit] + 1)
                    chain(nc.vector.reduce_max(red[:, 4:5], s_flat, axis=AX.X))
                    nc.vector.tensor_scalar(sm[:, q, 0:1], red[:, 4:5], -HD ** -0.5, None, ALU.mult)\
                        .then_inc(s_max, 1)
                elif kind == "pn":
                    _, h, q = unit
                    dve.wait_ge(s_read, SC_USE[("sc", h, q)] + 1)
                    chain(nc.vector.reciprocal(sm[:, q, 1:2], sm[:, q, 1:2]))
                    nc.vector.tensor_scalar(p_t[:, q, :], p_t[:, q, :], sm[:, q, 1:2], None, ALU.mult)\
                        .then_inc(p_ready, 1)
                elif kind == "tr":
                    _, h, j = unit
                    dve.wait_ge(pt_half, h * JT + j + 1)
                    lo(h_lo[:, 8 + j % 2, :], pT[:, :], h_hi[:, 8 + j % 2, :]).then_inc(t_read, 1)
                elif kind == "o":
                    h = unit[1]
                    dve.wait_ge(o_half, h + 1)
                    lo(h_lo[:, h, :], pO[:, :], h_hi[:, h, :]).then_inc(o_read, 1)
                elif kind == "cvc":
                    for tap, at in ((0, 0), (2, 2)):
                        for v in range(2):
                            ct = 2 * unit[1] + v
                            dve.wait_ge(cc_ready, ct + 1)
                            w = C_ECW + 4 * tap + ct
                            chain(nc.vector.scalar_tensor_tensor(
                                out=cb[:, v, :], in0=gp[:, v, at:at + SEQ], scalar=col[:, w:w + 1],
                                in1=cb[:, v, :], op0=ALU.mult, op1=ALU.add))
                elif kind == "cvb":
                    for v in range(2):
                        ct = 2 * unit[1] + v
                        dve.wait_ge(y_half, ct + 1)
                        lo(h_lo[:, 4 + ct, :], cb[:, v, :], h_hi[:, 4 + ct, :]).then_inc(cv_ready, 1)

            def window_mean(k):
                dve.wait_ge(pad_ready, k + 1)
                src, half = apad[k % 2], 0
                for level in range(k // 2 + 1):
                    dst = win[level % 2]
                    if level == 0:
                        lo_i, hi_i = 1, WP
                        a, b = src[:, 0:WP - 1], src[:, 1:WP]
                    else:
                        half = 2 ** (level - 1)
                        lo_i, hi_i = lo_i + half, hi_i - half
                        a, b = src[:, lo_i - half:hi_i - half], src[:, lo_i + half:hi_i + half]
                    chain(nc.vector.tensor_tensor(dst[:, lo_i:hi_i], a, b, ALU.add))
                    src = dst
                chain(nc.vector.tensor_tensor(nt[:, k % 2, :], src[:, PAD:PAD + SEQ], tbl[:, k // 2, :], ALU.mult))
                nc.vector.tensor_tensor(nt[:, k % 2, :], nt[:, k % 2, :], apad[k % 2][:, PAD:PAD + SEQ],
                                        ALU.subtract).then_inc(pool_full, 1)

            def pooled_lo(k):
                dve.wait_ge(a_half, 2 * KT + k + 1)
                lo(a_lo[:, k, :], nt[:, k % 2, :], a_hi[:, k, :]).then_inc(a_ready, 1)

            for l in range(2):
                n0 = FFN_N[l]
                norm = 1 + 2 * l
                if l == 0:
                    gain_of(gain[:, 1, :], SC2, 0, C_FFNN)
                norm_tiles(norm, mod[:, l, SH2:SH2 + 8], lambda: lo_next(slot_at(n0 - 1)))
                for part, (j0, nk) in enumerate(PARTS):
                    q0 = l * FT + j0

                    def up(i):
                        for u in range(2):
                            s = slot_at(n0, i, u)
                            q, jj, v = q0 + u + 2 * i, j0 + u + 2 * i, (q0 + u) % 2
                            dve.wait_ge(*bank_done(s, 0))
                            nc.vector.scalar_tensor_tensor(
                                out=cb[:, v, :], in0=gp[:, v, 0:SEQ], scalar=col[:, bass.ds(c_fcw(l, 0) + jj, 1)],
                                in1=cb[:, v, :], op0=ALU.mult, op1=ALU.add).then_inc(tap_done, 1)
                            dve.wait_ge(tap_done, q + 1)
                            nc.vector.scalar_tensor_tensor(
                                out=cb[:, v, :], in0=gp[:, v, 2:2 + SEQ], scalar=col[:, bass.ds(c_fcw(l, 2) + jj, 1)],
                                in1=cb[:, v, :], op0=ALU.mult, op1=ALU.add).then_inc(conv_ready, 1)
                            dve.wait_ge(g_ready, q + 1)
                            nc.vector.tensor_tensor(cb[:, v, :], cb[:, v, :], pair[s.gr][:, 1, :], ALU.mult)\
                                .then_inc(evac[s.gr], 1)
                            dve.wait_ge(hh_ready, q + 1)
                            lo(h_lo[:, 2 * i + u, :], cb[:, v, :], h_hi[:, 2 * i + u, :]).then_inc(h_ready, 1)
                            lo_next(s)
                    pairs(dve, nk // 2, up)
                    n0 += nk
                    final = part == 2

                    def down(i):
                        for u in range(2):
                            s = slot_at(n0, i, u)
                            b = 4 * part + 2 * i + u
                            if l == 0:
                                ada_columns(ADA0 + b, mod[:, 1, bass.ds(4 * b, 4)],
                                            col[:, bass.ds(C_ADAB + 48 + 4 * b, 4)])
                            for v in range(2):
                                m = 2 * (2 * i + u) + v
                                old = xT[:, m, :]
                                if final and l == 1:
                                    if m >= 4:
                                        dve.wait_ge(t_ready, HQ * JT + m - 3)
                                    dst = final_tiles[:, m % 4, :]
                                else:
                                    dst = old
                                residual(dst, s, v, mod[:, l, bass.ds(G2 + m, 1)], old)
                            if final and l == 0:
                                for v in range(2):
                                    add_square(2, 2 * (2 * i + u) + v)
                            if not final or s.n + 2 < min(N_SLOTS, n0 + 5):
                                lo_next(s)

                    pairs(dve, 2, down, unroll=final)
                    n0 += 4
                if l == 0:
                    for t in apad:
                        nc.vector.memset(t[:, 0:PAD], 0.0)
                        nc.vector.memset(t[:, PAD + SEQ:], 0.0)
                    gain_of(gain[:, 2, :], SC1, 1, C_MIXN + 8)
                    gain_of(gain[:, 3, :], SC2, 1, C_FFNN + 8)
                    chain(nc.vector.tensor_tensor(gain[:, 4, :], mod[:, 1, G1:G1 + 8], col[:, C_POOL:C_POOL + 8],
                                                  ALU.mult))
                    dve.wait_ge(count_loaded, 16)
                    rms_inverse(2)
                    scaled(2, 0)
                    for k in range(KT):
                        if k:
                            pooled_lo(k - 1)
                        if k == 4:
                            lo_next(slot_at(POOL_N - 1))
                        if k + 1 < KT:
                            scaled(2, k + 1)
                        window_mean(k)
                    pooled_lo(KT - 1)
                    for t in range(4):
                        s = Slot(POOL_N, POOL_N % 2, POOL_N // 2, POOL_N + 8 + t, t % 2, (POOL_N + 8 + t) // 2)
                        for v in range(2):
                            m = 2 * t + v
                            residual(xT[:, m, :], s, v, gain[:, 4, m:m + 1], xT[:, m, :])
                        for v in range(2):
                            add_square(3, 2 * t + v)


_INS = ["x", "c", "ctx", "c_ctx", "ada_w", "ada_b", "mix_norm", "ffn_norm", "even_w_in", "even_q_gain",
        "even_k_gain", "even_conv_w", "even_w_out", "odd_pool_w", "odd_pool_scale", "ffn_w_up", "ffn_conv_w",
        "ffn_conv_b", "ffn_w_down"]


def shape_constants():
    f = np.float32
    ident = np.eye(P, dtype=f)
    perm = ident[np.arange(P) ^ (HD // 4)]
    t = np.arange(SEQ)
    axis_dim = HD // 2
    inv_freq = np.power(f(THETA), -np.arange(0, axis_dim, 2, dtype=f) / f(axis_dim)).astype(f)
    pos = np.stack([t // GRID_W, t % GRID_W]).astype(f)
    dim = np.arange(HD)
    ang = pos[dim // axis_dim] * inv_freq[dim % (HD // 4)][:, None]
    sign = np.where(dim // (HD // 4) % 2 == 0, f(-1), f(1))[:, None]
    rope = np.concatenate([np.cos(ang), np.sin(ang) * sign], axis=1).astype(f)
    counts = [np.minimum(t + w - w // 2, SEQ) - np.maximum(t - w // 2, 0) for w in WINDOWS]
    inv = np.concatenate([f(1) / n.astype(f) for n in counts]).astype(f)
    return {"ident": ident, "perm": perm, "rope": rope, "invcount": np.ascontiguousarray(np.tile(inv, (P, 1)))}


def kernel(**inputs):
    import concourse.bacc as _bacc
    from concourse import mybir as _mybir
    from concourse.bass_utils import run_bass_kernel_spmd as _run

    nc = _bacc.Bacc("TRN2", target_bir_lowering=False, num_devices=1, dynamic_dma_scratch_size=4096)
    arrays, args = {}, []
    given = {name: inputs[name] for name in _INS}
    given.update(shape_constants())
    for name, a in given.items():
        a = np.ascontiguousarray(a)
        arrays[f"in_{name}_dram"] = a
        args.append(nc.dram_tensor(f"in_{name}_dram", a.shape, _mybir.dt.from_np(a.dtype), kind="ExternalInput").ap())
    args.append(nc.dram_tensor("out_0_dram", (1, SEQ, D), _mybir.dt.float32, kind="ExternalOutput").ap())
    build(nc, *args)
    r = _run(nc, [arrays], core_ids=[0])
    return r.results[0]["out_0_dram"]
```

```python
import numpy as np
import concourse.bass as bass
from concourse import mybir
from contextlib import ExitStack
from typing import NamedTuple

P = 128
D, SEQ, CTX = 1024, 512, 256
KT = D // P
TT = SEQ // P
HQ, HKV, HD = 4, 2, 128
KEYS = CTX + SEQ
JT = KEYS // P
FF = 2816
FT = FF // P
PARTS = [(0, 8), (8, 8), (16, 6)]
WINDOWS = (2, 4, 8, 16)
PAD = 8
EPS = 1e-6
GRID_W = 64
THETA = 10000.0

W_IN_COLS = [0, 512, 768, 256, 1536, 2048, 1024, 1792, 2304, 1280]
OUT0 = 10
FFN_SLOTS = FT + 4 * len(PARTS)
FFN_N = [OUT0 + 4, OUT0 + 4 + FFN_SLOTS + 1]
POOL_N = OUT0 + 4 + FFN_SLOTS
N_SLOTS = FFN_N[1] + FFN_SLOTS
ADA_SLOTS = 8
ADA_RING = 3
W_BEFORE = [2, 3]

C_C, C_CC, C_ADAB, C_MIXN, C_FFNN, C_POOL, C_QG, C_KG, C_ECW = 0, 8, 16, 112, 128, 144, 152, 153, 154
C_ROWS = [128, 38, 88, 88]
SH1, SC1, G1, SH2, SC2, G2 = range(0, 48, 8)


def c_fcw(layer, tap):
    return 256 + 128 * layer + tap * FT


def c_fcb(layer):
    return 256 + 128 * layer + 3 * FT


def last_gen(n):
    if n == 0:
        return 6
    if n == 1:
        return 8
    return n + 8 if n < POOL_N else n + 11


def mixer_schedule():
    s = []

    attention = {}
    for h in range(HQ):
        t0 = 15 * h + 2
        for q in range(4):
            attention.setdefault(t0 + 2 * q, []).append(("sc", h, q))
            if q:
                attention[t0 + 2 * q].append(("pn", h, q - 1))
        attention[t0 + 6].append(("pn", h, 3))
        for j in range(JT):
            attention.setdefault(t0 + 9 + j, []).extend([("tr", h, j)] + ([("pv", h, j - 1)] if j else []))
        attention.setdefault(t0 + 15, []).extend([("pv", h, JT - 1), ("o", h)])
    head_tiles = {
        1: {2: [("st", 0)], 3: [("st", 1), ("iv", 0)], 4: [("iv", 1)], 5: [("rot", 0)], 6: [("rot", 1), ("qf", 0)],
            7: [("qf", 1)]},
        2: {0: [("st", 2), ("st", 3)], 1: [("iv", 2), ("iv", 3), ("st", 4)], 2: [("rot", 2), ("rot", 3), ("iv", 4)],
            3: [("qf", 2), ("qf", 3)], 4: [("qf", 4)]},
        4: {1: [("st", 5)], 2: [("iv", 5)], 3: [("st", 6), ("rot", 5)], 4: [("iv", 6)], 5: [("qf", 5)],
            6: [("rot", 6)], 7: [("qf", 6)]}}
    ada_steps = {(2, 0): 0, (3, 4): 1, (5, 4): 2, (7, 0): 3, (8, 4): 4, (9, 4): 5, (11, 4): 6, (13, 6): 7}
    conv = {5: ("cvc", 0), 6: ("cvb", 0), 8: ("cvc", 1), 9: ("cvb", 1)}
    for n in range(OUT0 + 4):
        free = [k for k in range(8) if not any(u[0] == "sc" for u in attention.get(8 * (n - 3) + k, []))]
        split_steps = free[::2] if len(free) == 8 else free[:4]
        for k in range(8):
            s.extend(attention.get(8 * (n - 3) + k, []))
            s.append(("mm", n, k))
            s.extend(head_tiles.get(n, {}).get(k, []))
            if n - 1 in (5, 8) and k in (1, 2, 3, 4):
                s.append(("tap", (n - 6) // 3, (k - 1) // 2, (k - 1) % 2))
            if (n, k) in ada_steps:
                s.append(("ada", ada_steps[n, k]))
            if n and k in split_steps:
                s.append(("sp", n + 1, split_steps.index(k)))
        s.append(("ev", n))
        if n in conv:
            s.append(conv[n])
    return s


MIX = mixer_schedule()
T_USE = {u: i for i, u in enumerate(u for u in MIX if u[0] in ("ada", "tr") or
                             u[0] in ("st", "iv", "rot") and u[1] >= 5)}
T_FFN0 = len(T_USE)
T_OUT = T_FFN0 + 12
T_READY = {u: i for i, u in enumerate(u for u in T_USE if u[0] != "ada")}
AUX_USE = {u: i + 3 for i, u in enumerate(u for u in MIX if u[0] in ("st", "iv", "rot") and u[1] < 5)}
AUX_UNIT = {u: unit for unit, u in AUX_USE.items()}
AUX_NORM = [1] + [3 + len(AUX_USE) + 2 * i for i in range(3)]
SC_USE = {u: i for i, u in enumerate(u for u in MIX if u[0] == "sc")}
ROTS = [u for u in MIX if u[0] == "rot"]
ADA0 = 8
ADA1 = 12


BY_POOL = (6, 7)
LO_BY_POOL = (2, 3, 4, 5)
POOL_ORDER = BY_POOL + tuple(range(6))


class Slot(NamedTuple):
    n: object
    r: int
    half: object
    g: object
    gr: int
    gh: object


START = [("tokens", 0), ("tokens", 1), ("ada", 0), ("tokens", 2), ("ada", 1), ("tokens", 3), ("ada", 2),
         ("tokens", 4), ("tokens", 5), ("ada", 3), ("ada", 4), ("ada", 5), ("ada", 6), ("ada", 7)]


def slot_at(n0, i=0, u=0):
    g0 = last_gen(n0)
    return Slot(n0 + u + 2 * i, (n0 + u) % 2, (n0 + u) // 2 + i, g0 + u + 2 * i, (g0 + u) % 2, (g0 + u) // 2 + i)


def build(nc, x, c, ctx, c_ctx, ada_w, ada_b, mix_norm, ffn_norm, w_in, q_gain, k_gain, conv_w, w_out,
          pool_w, pool_scale, w_up, fconv_w, fconv_b, w_down, ident_d, perm_d, rope_d, edge_counts_d, out):
    f32, f32r = mybir.dt.float32, mybir.dt.float32r
    ALU, ACT, AX = mybir.AluOpType, mybir.ActivationFunctionType, mybir.AxisListType

    with ExitStack() as stack:
        def sb(name, shape, dt=f32):
            return stack.enter_context(nc.sbuf_tensor(name, shape, dt))

        def sem(name):
            return stack.enter_context(nc.semaphore(name))

        xT = sb("xT", [P, KT, SEQ])
        a_hi, a_lo = sb("a_hi", [P, KT, SEQ], f32r), sb("a_lo", [P, KT, SEQ], f32r)
        h_hi, h_lo = sb("h_hi", [P, 10, SEQ], f32r), sb("h_lo", [P, 10, SEQ], f32r)
        QK = HQ * SEQ + HKV * KEYS
        qk_hi, qk_lo = sb("qk_hi", [P, QK], f32r), sb("qk_lo", [P, QK], f32r)
        v_hi, v_lo = sb("v_hi", [P, JT, HKV * HD], f32r), sb("v_lo", [P, JT, HKV * HD], f32r)
        w_raw = sb("w_raw", [P, 2, 2048])
        w_hi, w_lo = sb("w_hi", [P, 2, 2048], f32r), sb("w_lo", [P, 2, 2048], f32r)
        tmp = sb("tmp", [P, 6, SEQ])
        ada_raw = sb("ada_raw", [P, 2, 1024])
        acc = sb("acc", [P, 2, SEQ])
        tbl = sb("tbl", [P, 4, SEQ])
        gp = sb("gp", [P, 2, SEQ + 2])
        cb = sb("cb", [P, 2, SEQ])
        ident, ones = sb("ident", [P, P]), sb("ones", [P, P])
        perm = gp[:, 0, 1:1 + P]
        col = sb("col", [P, 4 * P])
        mod = sb("mod", [P, 2, 48])
        modc = sb("modc", [P, 16])
        gain = sb("gain", [P, 5, KT])
        gainc = sb("gainc", [P, KT])
        silu_c = sb("silu_c", [P, 16])
        eps = sb("eps", [P, 1])
        cstat = sb("cstat", [P, 4])
        small = sb("small", [P, 16])
        ada4 = modc[:, 0:4]
        inv4 = small[:, 12:16]
        red = small[:, 8:9]
        sm = small[:, 0:8].rearrange("p (q a) -> p q a", a=2)
        ctxa_hi = h_hi[:, 4:8, :].rearrange("p a (b t) -> p (a b) t", b=2)
        ctxa_lo = h_lo[:, 4:8, :].rearrange("p a (b t) -> p (a b) t", b=2)
        ctx_t = [cb[:, :, :].rearrange("p a (b t) -> p (a b) t", b=2),
                 tbl[:, 2:4, :].rearrange("p a (b t) -> p (a b) t", b=2)]
        stage = tmp[:, :, :].rearrange("p (a b) t -> p a (b t)", b=2)
        p_t = tmp[:, :, :].rearrange("p a t -> p (a t)").rearrange("p (q k) -> p q k", q=4)
        ss, inv_wide, sq, nt = tmp[:, 0, :], tmp[:, 1, :], tmp[:, 2:4, :], tmp[:, 4:6, :]
        ada_flat = ada_raw[:, :, :].rearrange("p a b -> p (a b)")
        WP = SEQ + 2 * PAD
        tbl_flat = tbl[:, :, :].rearrange("p a t -> p (a t)")
        apads = [ada_flat[:, 0:WP], ada_flat[:, WP:2 * WP], tbl_flat[:, 0:WP], tbl_flat[:, WP:2 * WP]]
        dve_win = [ada_flat[:, 2 * WP:3 * WP], cb[:, :, :].rearrange("p a t -> p (a t)")[:, 0:WP]]
        pool_win = [tbl_flat[:, 2 * WP:3 * WP], acc[:, :, :].rearrange("p a t -> p (a t)")[:, 0:WP]]
        edge_counts = tbl_flat[:, 3 * WP:3 * WP + 16 * len(WINDOWS)].rearrange("p (g a t) -> p g a t", a=2, t=8)
        edge = small[:, :].rearrange("p (a t) -> p a t", t=8)

        pair = [stack.enter_context(nc.psum_tensor(f"pair{i}", [P, 2, SEQ], f32)) for i in range(2)]
        pS = stack.enter_context(nc.psum_tensor("pS", [P, 2, SEQ], f32))
        pT = stack.enter_context(nc.psum_tensor("pT", [P, SEQ], f32))
        pO = stack.enter_context(nc.psum_tensor("pO", [P, SEQ], f32))
        aux = [pS[:, 0, :], pS[:, 1, :], pO[:, :]]
        s_flat = pS[:, :, :].rearrange("p a t -> p (a t)")[:, 0:KEYS]

        const_loaded, rows_loaded, rope_loaded = sem("const_loaded"), sem("rows_loaded"), sem("rope_loaded")
        x_loaded = [sem(f"x_loaded{i}") for i in range(3)]
        w_loaded = [sem(f"w_loaded{i}") for i in range(2)]
        ada_loaded = [sem(f"ada_loaded{i}") for i in range(2)]
        count_loaded = sem("count_loaded")
        rows_zero, set_up = sem("rows_zero"), sem("set_up")
        mm_done = sem("mm_done")
        evac = [sem(f"evac{i}") for i in range(2)]
        ada_mm = sem("ada_mm")
        w_hi_done, w_split = sem("w_hi_done"), sem("w_split")
        w_quarter = sem("w_quarter")
        t_ready, t_read = sem("t_ready"), sem("t_read")
        aux_ready = sem("aux_ready")
        aux_read = [sem(f"aux_read{i}") for i in range(3)]
        prod_done = sem("prod_done")
        acc_done = sem("acc_done")
        ada_ready = sem("ada_ready")
        ada_summed = sem("ada_summed")
        ada3_loaded, row_copied, ada_cols = sem("ada3_loaded"), sem("row_copied"), sem("ada_cols")
        silu_done, mods_done = sem("silu_done"), sem("mods_done")
        ctx_ss, ctx_std, ctx_scaled = sem("ctx_ss"), sem("ctx_std"), sem("ctx_scaled")
        ctxa_full, ctxa_half, ctxa_ready = sem("ctxa_full"), sem("ctxa_half"), sem("ctxa_ready")
        inv_ready = sem("inv_ready")
        sq_ready, ss_added = sem("sq_ready"), sem("ss_added")
        n_ready, a_half, a_ready = sem("n_ready"), sem("a_half"), sem("a_ready")
        pad_ready, pool_full = sem("pad_ready"), sem("pool_full")
        win_seq, win_summed = sem("win_seq"), sem("win_summed")
        qsq_ready, qn_ready, q_full, q_half, q_done = (
            sem("qsq_ready"), sem("qn_ready"), sem("q_full"), sem("q_half"), sem("q_done"))
        v_half, wide_ready = sem("v_half"), sem("wide_ready")
        s_ready, s_max, s_read, p_ready = sem("s_ready"), sem("s_max"), sem("s_read"), sem("p_ready")
        pt_half, pv_done, o_half, o_read = sem("pt_half"), sem("pv_done"), sem("o_half"), sem("o_read")
        cc_ready, y_half, cv_ready = sem("cc_ready"), sem("y_half"), sem("cv_ready")
        conv_ready, g_ready, hh_ready, h_ready = (
            sem("conv_ready"), sem("g_ready"), sem("hh_ready"), sem("h_ready"))
        dve_seq = sem("dve_seq")
        tap_done = sem("tap_done")
        out_sent = [sem(f"out_sent{i}") for i in range(2)]

        def aux_read_at(u):
            rows = [v + 1 for v in AUX_NORM]
            if u in rows:
                return n_ready, (rows.index(u) + 1) * KT
            unit = AUX_UNIT.get(u, ("",))
            if unit[0] == "iv":
                return (q_full, 5) if unit[1] == 4 else (qn_ready, unit[1] + 1)
            own = [v for v in range(u % 3, u + 1, 3) if v not in rows and AUX_UNIT.get(v, ("",))[0] != "iv"]
            return aux_read[u % 3], len(own)

        def aux_wait(eng, u):
            if u >= 3:
                eng.wait_ge(*aux_read_at(u - 3))

        ada_slot = [w_raw[:, 1, :], ada_flat, w_raw[:, 0, :]]
        ada_slot_loaded = [w_loaded[1], ada3_loaded, w_loaded[0]]
        ada_row_bank = [pT, pO]

        def bank_evacuated(g):
            return evac[g % 2], 2 * (g // 2)

        def pairs(eng, trips, body, unroll=False):
            if unroll:
                for i in range(trips):
                    body(i)
            else:
                with eng.Fori(0, trips) as i:
                    body(i)

        def bank_done(s, v):
            return evac[s.gr], 2 * s.gh + v + 1

        def apad(k):
            return apads[k % 2 + (2 if k in BY_POOL else 0)]

        def pooled(k):
            return sq[:, k % 2, :] if k in BY_POOL else gp[:, k % 2, 1:1 + SEQ]

        def window_sum(k, engine, places, link):
            src, lo_i, hi_i = apad(k), 0, WP
            for level in range(k // 2 + 1):
                left, right = (1, 0) if level == 0 else (2 ** (level - 1), 2 ** (level - 1))
                last = level == k // 2
                lo_i, hi_i = (PAD, PAD + SEQ) if last else (lo_i + left, hi_i - right)
                dst = pooled(k) if last else places[level % 2][:, lo_i:hi_i]
                ins = engine.tensor_tensor(dst, src[:, lo_i - left:hi_i - left], src[:, lo_i + right:hi_i + right],
                                           ALU.add)
                link(ins, last)
                src = places[level % 2]

        def edges(row):
            return row.rearrange("p (a t) -> p a t", t=8)[:, 0:SEQ // 8:SEQ // 8 - 1, :]

        def q_raw(i):
            return tmp[:, 2 * (i % 3), :] if i < 5 else tbl[:, 2, :] if i == 5 else cb[:, 0, :]

        def q_sq(i):
            return tmp[:, 2 * (i % 3) + 1, :] if i < 5 else tbl[:, 3, :] if i == 5 else cb[:, 1, :]

        def q_view(t, i):
            if i not in (2, 3, 4):
                h = i if i < 2 else i - 3
                return t[:, h * SEQ:(h + 1) * SEQ]
            keys = t[:, HQ * SEQ:].rearrange("p (h t) -> p h t", h=HKV)
            return keys[:, :, 0:CTX] if i == 4 else keys[:, i - 2, CTX:KEYS]

        def q_src(i):
            return q_raw(i).rearrange("p (h t) -> p h t", h=HKV) if i == 4 else q_raw(i)

        def stat_bank(unit):
            return aux[AUX_USE[unit] % 3] if unit in AUX_USE else pT[:, :]

        def stat_ready(unit):
            return (aux_ready, AUX_USE[unit] + 1) if unit in AUX_USE else (t_ready, T_READY[unit] + 1)

        def stat_read(unit):
            if unit in AUX_USE:
                return aux_read_at(AUX_USE[unit])
            return t_read, T_USE[unit] + 1

        final_tiles = tmp[:, 2:6, :]
        FINAL_N = N_SLOTS - 4

        block = stack.enter_context(nc.Block())

        @block.sync
        def _(sp):
            sp.dma_start(ident[:], ident_d).then_inc(const_loaded, 16)
            ada_v = ada_w[0].rearrange("(k p) n -> p k n", p=P)

            def load(r, src):
                nk = src.shape[1]
                for k in (0, nk // 2):
                    sp.dma_start(w_raw[:, r, k * 256:(k + nk // 2) * 256].rearrange("p (k n) -> p k n", n=256),
                                 src[:, k:k + nk // 2, :]).then_inc(w_loaded[r], 16)

            for kind, i in START:
                if (kind, i) == ("ada", 4):
                    sp.wait_ge(set_up, 1)
                    sp.dma_start(perm, perm_d).then_inc(rope_loaded, 16)
                    sp.dma_start(tbl[:, 0:2, :], rope_d.rearrange("p (a t) -> p a t", a=2)).then_inc(rope_loaded, 16)
                if kind == "tokens":
                    if i >= 3:
                        sp.wait_ge(mm_done, i - 2)
                    src = x[0, i * P:(i + 1) * P, :] if i < TT else ctx[0, (i - TT) * P:(i - TT + 1) * P, :]
                    sp.dma_start(stage[:, i % 3, :], src).then_inc(x_loaded[i % 3], 16)
                else:
                    if i >= ADA_RING:
                        sp.wait_ge(ada_mm, i - ADA_RING + 1)
                    for k in (0, 2):
                        sp.dma_start(ada_slot[i % ADA_RING][:, k * 512:(k + 2) * 512]
                                     .rearrange("p (k n) -> p k n", n=512),
                                     ada_v[:, i % 2 * 4 + k:i % 2 * 4 + k + 2, i // 2 * 512:(i // 2 + 1) * 512])\
                            .then_inc(ada_slot_loaded[i % ADA_RING], 16)

            in_v = w_in[0].rearrange("(k p) n -> p k n", p=P)
            out_v = w_out[0].rearrange("(k p) n -> p k n", p=P)
            for n in range(OUT0 + 4):
                if n < 2:
                    sp.wait_ge(ada_mm, 6 + n)
                else:
                    sp.wait_ge(w_split, n - 1)
                src = in_v[:, :, W_IN_COLS[n]:W_IN_COLS[n] + 256] if n < OUT0 else \
                    out_v[:, :, (n - OUT0) * 256:(n - OUT0 + 1) * 256]
                load(n % 2, src)

            for l in range(2):
                n0 = FFN_N[l]
                up_v = w_up[l].rearrange("(k p) (g j n) -> p k g j n", p=P, g=2, j=FT)
                down_v = w_down[l].rearrange("(j p) (s n) -> p j s n", p=P, n=256)
                for j0, nk in PARTS:
                    def up(i):
                        for u in range(2):
                            s = slot_at(n0, i, u)
                            sp.wait_ge(w_split, s.n - 1)
                            for g in range(2):
                                sp.dma_start(w_raw[:, s.r, :].rearrange("p (k g n) -> p k g n", k=KT, g=2)[:, :, g, :],
                                             up_v[:, :, g, j0 + 2 * i + u, :]).then_inc(w_loaded[s.r], 16)
                    pairs(sp, nk // 2, up)
                    n0 += nk

                    def down(i):
                        for u in range(2):
                            s = slot_at(n0, i, u)
                            sp.wait_ge(w_split, s.n - 1)
                            load(s.r, down_v[:, j0:j0 + nk, 2 * i + u, :])
                    pairs(sp, 2, down)
                    n0 += 4
                if l == 0:
                    sp.wait_ge(w_split, POOL_N - 1)
                    load(POOL_N % 2, pool_w[0].rearrange("g (t p) n -> p (g t) n", p=P))
                    sp.dma_start(tbl_flat[:, 3 * WP:3 * WP + 16 * len(WINDOWS)], edge_counts_d)\
                        .then_inc(count_loaded, 16)

            out_v2 = out[0].rearrange("(b p) (m n) -> p m b n", p=P, n=P)
            for m in range(KT):
                sp.wait_ge(t_read, T_OUT + m + 1)
                sp.dma_start(out_v2[:, m], tmp[:, m % 2, :].rearrange("p (b n) -> p b n", b=TT))\
                    .then_inc(out_sent[m % 2], 16)
            for i in range(2):
                sp.wait_ge(out_sent[i], 16 * KT // 2)

        @block.gpsimd
        def _(pool):
            src0 = ada_w[0].rearrange("(k p) (b n) -> p k b n", p=P, n=512)
            src1 = ada_w[1].rearrange("(k p) (b n) -> p k b n", p=P, n=512)

            def chunk(src, col_block, q):
                pool.dma_start(ada_raw[:, q % 2, :].rearrange("p (k n) -> p k n", k=2),
                               src[:, 2 * q:2 * q + 2, col_block, :]).then_inc(ada_loaded[q % 2], 16)

            def ada_sum(b, src, col_block, next_src, next_block, first=False):
                for q in range(4):
                    w = ada_raw[:, q % 2, :].rearrange("p (k n) -> p k n", k=2)
                    pool.wait_ge(ada_loaded[q % 2], 32 * b + 16 * (q // 2 + 1))
                    nc.gpsimd.tensor_tensor(w, w, silu_c[:, 2 * q:2 * q + 2].unsqueeze(2).to_broadcast([P, 2, SEQ]),
                                            ALU.mult).then_inc(prod_done, 1)
                    pool.wait_ge(prod_done, 4 * b + q + 1)
                    if q == 0:
                        if first:
                            pool.wait_ge(mods_done, 1)
                        else:
                            pool.wait_ge(ada_ready, b)
                        nc.gpsimd.tensor_tensor(acc[:, 0, :], w[:, 0], w[:, 1], ALU.add).then_inc(acc_done, 1)
                    else:
                        for kk in range(2):
                            pool.wait_ge(acc_done, 7 * b + 2 * q - 1 + kk)
                            nc.gpsimd.tensor_tensor(acc[:, 0, :], acc[:, 0, :], w[:, kk], ALU.add)\
                                .then_inc(acc_done, 1)
                    if q < 2 or next_src is not None:
                        pool.wait_ge(acc_done, 7 * b + 2 * q + 1)
                        if q < 2:
                            chunk(src, col_block, q + 2)
                        else:
                            chunk(next_src, next_block, q - 2)

            def lo_by_pool(n):
                pool.wait_ge(w_split, n)
                pool.wait_ge(w_hi_done, n + 1)
                nc.gpsimd.tensor_tensor(w_lo[:, n % 2, :], w_raw[:, n % 2, :], w_hi[:, n % 2, :].bitcast(f32),
                                        ALU.subtract).then_inc(w_split, 1)

            pool.wait_ge(ada_mm, 8)
            chunk(src0, 4, 0)
            chunk(src0, 4, 1)
            lo_by_pool(1)
            ada_sum(0, src0, 4, src0, 5, first=True)
            with pool.Fori(0, ADA0 - 2) as i:
                ada_sum(i + 1, src0, i + 5, src0, i + 6)
            ada_sum(ADA0 - 1, src0, ADA0 + 3, src1, 0)
            with pool.Fori(0, ADA1 - 1) as i:
                ada_sum(i + ADA0, src1, i, src1, i + 1)
            ada_sum(ADA0 + ADA1 - 1, src1, ADA1 - 1, None, None)

            pool.wait_ge(ada_ready, ADA0 + ADA1)
            steps = [0]

            def link(ins, last):
                if last:
                    ins.then_inc(win_summed, 1)
                else:
                    steps[0] += 1
                    ins.then_inc(win_seq, 1)
                    pool.wait_ge(win_seq, steps[0])
            for i, k in enumerate(BY_POOL):
                pool.wait_ge(pad_ready, i + 1)
                if i:
                    pool.wait_ge(win_summed, i)
                window_sum(k, nc.gpsimd, pool_win, link)
            pool.wait_ge(a_ready, 2 * KT + LO_BY_POOL[0])
            for k in LO_BY_POOL:
                pool.wait_ge(a_half, 2 * KT + k + 1)
                nc.gpsimd.tensor_tensor(a_lo[:, k, :], pooled(k), a_hi[:, k, :].bitcast(f32), ALU.subtract)\
                    .then_inc(a_ready, 1)
            lo_by_pool(POOL_N + 1)
            lo_by_pool(POOL_N + 2)

        @block.tensor
        def _(pe):
            def product(dst, lh, ll, rh, rl, start, stop):
                nc.tensor.matmul(dst, lh, rh, start=start, stop=False)
                nc.tensor.matmul(dst, lh, rl, start=False, stop=False)
                return nc.tensor.matmul(dst, ll, rh, start=False, stop=stop)

            def norm_stat(norm):
                u = AUX_NORM[norm]
                pe.wait_ge(ss_added, (norm + 1) * KT)
                aux_wait(pe, u)
                for i in range(TT):
                    ins = nc.tensor.matmul(aux[u % 3][:, i:i + 1], ss[:, i * P:(i + 1) * P], ones[:, 0:1],
                                           start=True, stop=True)
                ins.then_inc(aux_ready, 1)

            def norm_rows(norm):
                u = AUX_NORM[norm] + 1
                pe.wait_ge(inv_ready, norm + 1)
                aux_wait(pe, u)
                for i in range(TT):
                    ins = nc.tensor.transpose(aux[u % 3][:, i * P:(i + 1) * P], inv_wide[:, i * P:(i + 1) * P],
                                              ident[:])
                ins.then_inc(aux_ready, 1)

            def bank_free(unit):
                if unit in AUX_USE:
                    aux_wait(pe, AUX_USE[unit])
                else:
                    pe.wait_ge(t_read, T_USE[unit])

            def step(s, idx, k, nk, rhs_h, rhs_l, ready=None):
                if idx == 0:
                    pe.wait_ge(w_split, s.n + 1)
                    pe.wait_ge(evac[s.gr], 2 * s.gh)
                if ready is not None:
                    pe.wait_ge(*ready)
                for m in range(2):
                    at = k * 256 + m * P
                    ins = product(pair[s.gr][:, m, :], w_hi[:, s.r, at:at + P], w_lo[:, s.r, at:at + P],
                                  rhs_h, rhs_l, idx == 0, idx == nk - 1)
                if idx == nk - 1:
                    ins.then_inc(mm_done, 1)

            pe.wait_ge(set_up, 1)
            pe.wait_ge(const_loaded, 16)
            pe.wait_ge(rows_loaded, 16 * 13)
            for t in range(4):
                ins = nc.tensor.transpose(aux[0][:, t * P:(t + 1) * P], acc[:, 0, t * P:(t + 1) * P], ident[:])
            ins.then_inc(aux_ready, 1)

            def token_tile(i):
                pe.wait_ge(x_loaded[i % 3], 16 * (i // 3 + 1))
                if i >= TT:
                    pe.wait_ge(ctx_scaled, i - TT + 1)
                if i >= 2:
                    pe.wait_ge(*bank_evacuated(i))
                for kt in range(KT):
                    ins = nc.tensor.transpose(pair[i % 2][:, kt // 4, kt % 4 * P:(kt % 4 + 1) * P],
                                              stage[:, i % 3, kt * P:(kt + 1) * P], ident[:])
                ins.then_inc(mm_done, 1)

            def ada_rows(s):
                b = s // 2
                if s == 0:
                    pe.wait_ge(silu_done, 1)
                if s % 2 == 0 and b >= 2:
                    pe.wait_ge(row_copied, b - 1)
                pe.wait_ge(ada_slot_loaded[s % ADA_RING], 32 * (s // ADA_RING + 1))
                for kk in range(4):
                    k = 4 * (s % 2) + kk
                    ins = nc.tensor.matmul(ada_row_bank[b % 2][0:2, :], silu_c[:, k:16:8],
                                           ada_slot[s % ADA_RING][:, kk * 512:(kk + 1) * 512],
                                           start=(k == 0), stop=(k == KT - 1))
                ins.then_inc(ada_mm, 1)

            def ada_row_columns(b):
                pe.wait_ge(row_copied, b + 1)
                if b == 0:
                    pe.wait_ge(*aux_read_at(0))
                for i in range(4):
                    at = 2 * (4 * b + i)
                    ins = nc.tensor.transpose(aux[0][:, at:at + 2], acc[0:2, b % 2, i * P:(i + 1) * P],
                                              ident[0:2, 0:2])
                ins.then_inc(ada_cols, 1)

            for kind, i in START:
                if kind == "tokens":
                    token_tile(i)
                else:
                    ada_rows(i)
                    if i == 5:
                        norm_stat(0)
                    if i % 2 and i > 1:
                        ada_row_columns(i // 2 - 1)
            ada_row_columns(3)
            norm_rows(0)

            def in_mm(n, k):
                s = slot_at(n)
                if n == 2:
                    if k >= 6:
                        return
                    if k == 0:
                        pe.wait_ge(w_split, n + 1)
                        pe.wait_ge(*bank_evacuated(9))
                    if k == 4:
                        pe.wait_ge(*bank_evacuated(10))
                    g, i = (9, k) if k < 4 else (10, k - 4)
                    ah, al = (a_hi, a_lo) if k < 4 else (ctxa_hi, ctxa_lo)
                    for kt in range(KT):
                        dst = pair[g % 2][:, i // 2, i % 2 * 256:(i % 2 + 1) * 256]
                        w = slice(kt * 256, (kt + 1) * 256)
                        t = slice(i * P, (i + 1) * P)
                        ins = product(dst, ah[:, kt, t], al[:, kt, t], w_hi[:, s.r, w], w_lo[:, s.r, w],
                                      kt == 0, kt == KT - 1)
                    if k in (3, 5):
                        ins.then_inc(mm_done, 1)
                elif n == 1:
                    lat = s._replace(g=7, gr=1, gh=3)
                    step(lat, k, k, KT, a_hi[:, k, :], a_lo[:, k, :])
                    if k == KT - 1:
                        pe.wait_ge(ctxa_ready, KT)
                        pe.wait_ge(*bank_evacuated(8))
                        for m in range(2):
                            for kt in range(KT):
                                at = kt * 256 + m * P
                                ins = product(pair[0][:, 0, m * CTX:(m + 1) * CTX], w_hi[:, s.r, at:at + P],
                                              w_lo[:, s.r, at:at + P], ctxa_hi[:, kt, :], ctxa_lo[:, kt, :],
                                              kt == 0, kt == KT - 1)
                        ins.then_inc(mm_done, 1)
                elif n < OUT0:
                    step(s, k, k, KT, a_hi[:, k, :], a_lo[:, k, :], (a_ready, k + 1) if n == 0 else None)
                else:
                    kt = (k + 4) % 8
                    ready = None
                    if n == OUT0:
                        ready = (cv_ready, kt - 3) if kt >= 4 else (o_read, kt + 1)
                    step(s, k, kt, KT, h_hi[:, kt, :], h_lo[:, kt, :], ready)

            def ada_reduce(b, use):
                pe.wait_ge(acc_done, 7 * b + 7)
                if isinstance(use, int) and use == 0:
                    pe.wait_ge(mods_done, 1)
                else:
                    pe.wait_ge(t_read, use)
                for i in range(4):
                    ins = nc.tensor.transpose(pT[:, i * P:(i + 1) * P], acc[:, 0, i * P:(i + 1) * P], ident[:])
                ins.then_inc(ada_ready, 1)

            for unit in MIX:
                kind = unit[0]
                if kind == "mm":
                    in_mm(unit[1], unit[2])
                elif kind == "ada":
                    ada_reduce(unit[1], T_USE[unit])
                elif kind == "st":
                    pe.wait_ge(qsq_ready, unit[1] + 1)
                    bank_free(unit)
                    for i in range(TT):
                        ins = nc.tensor.matmul(stat_bank(unit)[:, i:i + 1], q_sq(unit[1])[:, i * P:(i + 1) * P],
                                               ones[:, 0:1], start=True, stop=True)
                    ins.then_inc(stat_ready(unit)[0], 1)
                elif kind == "iv":
                    pe.wait_ge(wide_ready, unit[1] + 1)
                    bank_free(unit)
                    for i in range(TT):
                        ins = nc.tensor.transpose(stat_bank(unit)[:, i * P:(i + 1) * P],
                                                  q_sq(unit[1])[:, i * P:(i + 1) * P], ident[:])
                    ins.then_inc(stat_ready(unit)[0], 1)
                elif kind == "rot":
                    if unit == ROTS[0]:
                        pe.wait_ge(rope_loaded, 32)
                    if unit in AUX_USE:
                        pe.wait_ge(qn_ready, unit[1] + 1)
                    bank_free(unit)
                    nc.tensor.matmul(stat_bank(unit), perm, q_raw(unit[1]), start=True, stop=True)\
                        .then_inc(stat_ready(unit)[0], 1)
                elif kind == "sc":
                    _, h, q = unit
                    su = SC_USE[unit]
                    if su == 0:
                        pe.wait_ge(q_done, 5)
                        for b in range(3):
                            pe.wait_ge(*aux_read_at(AUX_NORM[1] - 1 - b))
                    else:
                        pe.wait_ge(s_read, su)
                    if h == 2 and q == 0:
                        pe.wait_ge(q_done, 7)
                    qs = slice(h * SEQ + q * P, h * SEQ + (q + 1) * P)
                    k0 = HQ * SEQ + (h // 2) * KEYS
                    for at, n in ((0, SEQ), (SEQ, KEYS - SEQ)):
                        ks = slice(k0 + at, k0 + at + n)
                        ins = product(s_flat[:, at:at + n], qk_hi[:, qs], qk_lo[:, qs], qk_hi[:, ks], qk_lo[:, ks],
                                      True, True)
                    ins.then_inc(s_ready, 1)
                elif kind == "tr":
                    _, h, j = unit
                    if j == 0:
                        pe.wait_ge(p_ready, 4 * (h + 1))
                    pe.wait_ge(t_read, T_USE[unit])
                    for q in range(4):
                        ins = nc.tensor.transpose(pT[:, q * P:(q + 1) * P], p_t[:, q, j * P:(j + 1) * P], ident[:])
                    ins.then_inc(t_ready, 1)
                elif kind == "pv":
                    _, h, j = unit
                    pe.wait_ge(t_read, T_USE[("tr", h, j)] + 1)
                    if j == 0 and h:
                        pe.wait_ge(o_read, h)
                    v = slice((h // 2) * HD, (h // 2 + 1) * HD)
                    product(pO[:, :], v_hi[:, j, v], v_lo[:, j, v], h_hi[:, 8 + j % 2, :], h_lo[:, 8 + j % 2, :],
                            j == 0, j == JT - 1).then_inc(pv_done, 1)

            norm_stat(1)
            norm_rows(1)

            def out_transposes(m):
                pe.wait_ge(*bank_done(slot_at(FINAL_N + m // 2), m % 2))
                pe.wait_ge(t_read, T_OUT + m)
                for b in range(TT):
                    ins = nc.tensor.transpose(pT[:, b * P:(b + 1) * P],
                                              final_tiles[:, m % 4, b * P:(b + 1) * P], ident[:])
                ins.then_inc(t_ready, 1)

            for l in range(2):
                n0 = FFN_N[l]
                norm = 1 + 2 * l
                for part, (j0, nk) in enumerate(PARTS):
                    def up(i):
                        for u in range(2):
                            for k in range(KT):
                                step(slot_at(n0, i, u), k, k, KT, a_hi[:, k, :], a_lo[:, k, :],
                                     (a_ready, norm * KT + k + 1) if part == 0 and u == 0 else None)
                                if l == 0 and u == 1 and k == 4:
                                    ada_reduce(ADA0 + j0 // 2 + i, T_FFN0 + j0 // 2 + i)
                    pairs(pe, nk // 2, up)
                    n0 += nk
                    q0 = l * FT + j0
                    last = l == 1 and part == 2

                    def down(i):
                        for u in range(2):
                            for k in range(nk):
                                step(slot_at(n0, i, u), k, k, nk, h_hi[:, k, :], h_lo[:, k, :],
                                     (h_ready, q0 + k + 1) if u == 0 else None)
                                if l == 0 and part == 2 and k == 4 and 2 * i + u == 3:
                                    ada_reduce(ADA0 + ADA1 - 1, T_OUT - 1)
                                if last and k == 3 and 2 * i + u > 0:
                                    for v in range(2):
                                        out_transposes(2 * (2 * i + u - 1) + v)
                    pairs(pe, 2, down, unroll=part == 2)
                    n0 += 4
                if l == 0:
                    norm_stat(2)
                    norm_rows(2)
                    pe.wait_ge(w_split, POOL_N + 1)
                    r = POOL_N % 2
                    for t in range(4):
                        g = POOL_N + 8 + t
                        pe.wait_ge(*bank_evacuated(g))
                        for kk in range(2):
                            k = 2 * t + kk
                            pe.wait_ge(a_ready, 2 * KT + k + 1)
                            for m in range(2):
                                at = k * 256 + m * P
                                ins = product(pair[g % 2][:, m, :], w_hi[:, r, at:at + P], w_lo[:, r, at:at + P],
                                              a_hi[:, k, :], a_lo[:, k, :], kk == 0, kk == 1)
                        ins.then_inc(mm_done, 1)
                    norm_stat(3)
                    norm_rows(3)
            for m in (6, 7):
                out_transposes(m)

        @block.scalar
        def _(act):
            def hi_of_slot(s):
                act.wait_ge(w_loaded[s.r], 32 * (W_BEFORE[s.r] + s.half + 2))
                act.wait_ge(mm_done, s.g + 1)
                nc.scalar.activation(w_hi[:, s.r, :], w_raw[:, s.r, :], ACT.Copy).then_inc(w_hi_done, 1)

            def hi_of_first(n):
                act.wait_ge(w_loaded[n], 32 * (W_BEFORE[n] + 1))
                nc.scalar.activation(w_hi[:, n, :], w_raw[:, n, :], ACT.Copy).then_inc(w_hi_done, 1)

            def hi_quarter(n, c):
                if c == 0:
                    act.wait_ge(w_loaded[n % 2], 32 * (W_BEFORE[n % 2] + n // 2 + 1))
                    act.wait_ge(mm_done, last_gen(n - 2) + 1)
                part = slice(c * 512, (c + 1) * 512)
                nc.scalar.activation(w_hi[:, n % 2, part], w_raw[:, n % 2, part], ACT.Copy)\
                    .then_inc(w_hi_done if c == 3 else w_quarter, 1)

            def square(norm, k, final):
                act.wait_ge(*final)
                f = norm * KT + k
                if f >= 2:
                    act.wait_ge(ss_added, f - 1)
                nc.scalar.activation(sq[:, k % 2, :], xT[:, k, :], ACT.Square).then_inc(sq_ready, 1)

            def norm_std(norm):
                u = AUX_NORM[norm]
                act.wait_ge(aux_ready, u + 1)
                nc.scalar.activation(inv4, aux[u % 3][:, 0:TT], ACT.Sqrt, bias=eps[:, 0:1], scale=1.0 / D)\
                    .then_inc(aux_read[u % 3], 1)

            def norm_tiles(norm, shift, ks):
                for k in ks:
                    act.wait_ge(n_ready, norm * KT + k + 1)
                    nc.scalar.activation(a_hi[:, k, :], nt[:, k % 2, :], ACT.Identity,
                                         bias=shift[:, k:k + 1]).then_inc(a_half, 1)

            act.wait_ge(rows_zero, 1)
            stage_rows = acc[:, 0, :].rearrange("p (a b) -> p a b", a=4)

            def rows(t, r, src):
                n = src.shape[0]
                act.dma_start(stage_rows[r:r + n, t, :], src).then_inc(rows_loaded, 16)
                return r + n
            r = rows(0, 0, c.rearrange("a (k p) -> (a k) p", p=P))
            r = rows(0, r, c_ctx.rearrange("(k p) -> k p", p=P))
            r = rows(0, r, ada_b.rearrange("l (k p) -> (l k) p", p=P))
            rows(0, r, mix_norm.rearrange("l (k p) -> (l k) p", p=P))
            r = rows(1, 0, ffn_norm.rearrange("l (k p) -> (l k) p", p=P))
            r = rows(1, r, pool_scale.rearrange("l (k p) -> (l k) p", p=P))
            r = rows(1, r, q_gain)
            r = rows(1, r, k_gain)
            rows(1, r, conv_w.rearrange("e t (k p) -> (e t k) p", p=P))
            for l in range(2):
                r = rows(2 + l, 0, fconv_w[l].rearrange("t (k p) -> (t k) p", p=P))
                rows(2 + l, r, fconv_b[l:l + 1].rearrange("a (k p) -> (a k) p", p=P))

            act.wait_ge(aux_ready, 1)
            nc.scalar.activation(col[:, :], aux[0], ACT.Copy).then_inc(aux_read[0], 1)
            act.wait_ge(aux_read[0], 1)
            nc.scalar.activation(silu_c[:, :], col[:, 0:16], ACT.Silu).then_inc(silu_done, 1)

            def tokens_out(i, dst):
                act.wait_ge(mm_done, i + 1)
                nc.scalar.activation(dst, pair[i % 2][:, 0, :].rearrange("p (k t) -> p k t", k=4), ACT.Copy)\
                    .then_inc(evac[i % 2], 1)

            def copy_rows(b):
                act.wait_ge(ada_mm, 2 * b + 2)
                if b >= 2:
                    act.wait_ge(ada_cols, b - 1)
                nc.scalar.activation(acc[0:2, b % 2, :], ada_row_bank[b % 2][0:2, :], ACT.Copy)\
                    .then_inc(row_copied, 1)

            for i in range(TT):
                tokens_out(i, xT[:, 0:4, i * P:(i + 1) * P])
            copy_rows(0)
            act.wait_ge(set_up, 1)
            for i in range(2):
                act.wait_ge(x_loaded[(TT + i) % 3], 32)
                if i:
                    act.wait_ge(ctx_ss, 1)
                nc.scalar.activation(tbl[:, 2:4, :].rearrange("p a t -> p (a t)"), stage[:, (TT + i) % 3, :],
                                     ACT.Square, accum_out=cstat[:, i:i + 1]).then_inc(ctx_ss, 1)
            act.wait_ge(ctx_ss, 2)
            nc.scalar.activation(cstat[:, 2:4], cstat[:, 0:2], ACT.Sqrt, bias=eps[:, 0:1], scale=1.0 / D)\
                .then_inc(ctx_std, 1)
            for i in range(2):
                tokens_out(TT + i, ctx_t[0][:, :, i * P:(i + 1) * P])
            copy_rows(1)
            for k in range(KT):
                square(0, k, (evac[1], 6))
            norm_std(0)
            copy_rows(2)
            hi_of_first(0)
            copy_rows(3)
            sh = mod[:, 0, SH1:SH1 + 8]
            norm_tiles(0, sh, range(4))
            hi_of_first(1)
            norm_tiles(0, sh, range(4, 8))
            for k in range(KT):
                act.wait_ge(ctxa_full, k + 1)
                nc.scalar.activation(ctxa_hi[:, k, :], ctx_t[k // 4][:, k % 4, :], ACT.Copy).then_inc(ctxa_half, 1)

            def q_evac(i, g, b, n):
                act.wait_ge(mm_done, g + 1)
                if i >= 5:
                    act.wait_ge(ctxa_ready, KT)
                elif i >= 3:
                    act.wait_ge(q_done, i - 2)
                nc.scalar.activation(q_sq(i), pair[g % 2][:, b, :], ACT.Square).then_inc(qsq_ready, 1)
                nc.scalar.activation(q_raw(i), pair[g % 2][:, b, :], ACT.Copy).then_inc(evac[g % 2], n)

            def evac_in(n):
                s = slot_at(n)
                if n in (0, 3):
                    i = 0 if n == 0 else 5
                    q_evac(i, s.g, 0, 1)
                    q_evac(i + 1, s.g, 1, 1)
                elif n == 2:
                    for g, b, j in ((9, 0, 2), (9, 1, 4), (10, 0, 0)):
                        act.wait_ge(mm_done, g + 1)
                        nc.scalar.activation(v_hi[:, j:j + 2, :],
                                             pair[g % 2][:, b, :].rearrange("p (a n) -> p a n", a=2), ACT.Copy)\
                            .then_inc(v_half, 1)
                elif n == 1:
                    q_evac(2, 7, 0, 1)
                    q_evac(3, 7, 1, 1)
                    q_evac(4, 8, 0, 2)
                elif n in (4, 7):
                    act.wait_ge(mm_done, s.g + 1)
                    if n == 4:
                        act.wait_ge(q_done, 7)
                    for v in range(2):
                        nc.scalar.activation(tbl[:, 2 + v, :], pair[s.gr][:, v, :], ACT.Copy).then_inc(evac[s.gr], 1)
                elif n >= OUT0:
                    for v in range(2):
                        square(1, 2 * (n - OUT0) + v, bank_done(s, v))

            for unit in MIX:
                kind = unit[0]
                if kind == "ev":
                    evac_in(unit[1])
                elif kind == "sp":
                    hi_quarter(unit[1], unit[2])
                elif kind == "st":
                    act.wait_ge(*stat_ready(unit))
                    if unit[1]:
                        act.wait_ge(wide_ready, unit[1])
                    nc.scalar.activation(inv4, stat_bank(unit)[:, 0:TT], ACT.Sqrt, bias=eps[:, 0:1],
                                         scale=1.0 / HD).then_inc(stat_read(unit)[0], 1)
                elif kind == "qf":
                    i = unit[1]
                    act.wait_ge(q_full, i + 1)
                    nc.scalar.activation(q_view(qk_hi, i), q_src(i), ACT.Copy).then_inc(q_half, 1)
                elif kind == "sc":
                    _, h, q = unit
                    su = SC_USE[unit]
                    act.wait_ge(s_max, su + 1)
                    if q == 0 and h:
                        act.wait_ge(t_ready, T_READY[("tr", h - 1, JT - 1)] + 1)
                    nc.scalar.activation(p_t[:, q, :], s_flat, ACT.Exp, bias=sm[:, q, 0:1], scale=HD ** -0.5,
                                         accum_out=sm[:, q, 1:2]).then_inc(s_read, 1)
                elif kind == "tr":
                    _, h, j = unit
                    act.wait_ge(t_ready, T_READY[unit] + 1)
                    if h * JT + j >= 2:
                        act.wait_ge(pv_done, h * JT + j - 1)
                    nc.scalar.activation(h_hi[:, 8 + j % 2, :], pT[:, :], ACT.Copy).then_inc(pt_half, 1)
                elif kind == "o":
                    h = unit[1]
                    act.wait_ge(pv_done, JT * (h + 1))
                    nc.scalar.activation(h_hi[:, h, :], pO[:, :], ACT.Copy).then_inc(o_half, 1)
                elif kind == "cvc":
                    s = slot_at(5 + 3 * unit[1])
                    for v in range(2):
                        ct = 2 * unit[1] + v
                        act.wait_ge(*bank_done(s, v))
                        if unit[1]:
                            act.wait_ge(cv_ready, v + 1)
                        nc.scalar.activation(cb[:, v, :], gp[:, v, 1:1 + SEQ], ACT.Copy,
                                             scale=col[:, C_ECW + 4 + ct:C_ECW + 5 + ct]).then_inc(cc_ready, 1)
                elif kind == "cvb":
                    s = slot_at(6 + 3 * unit[1])
                    for v in range(2):
                        act.wait_ge(*bank_done(s, v))
                        nc.scalar.activation(h_hi[:, 4 + 2 * unit[1] + v, :], cb[:, v, :], ACT.Copy)\
                            .then_inc(y_half, 1)

            def pad_row(i):
                k = POOL_ORDER[i]
                act.wait_ge(n_ready, 2 * KT + i + 1)
                if k in range(2, BY_POOL[0]):
                    act.wait_ge(pool_full, k - 1)
                nc.scalar.activation(apad(k)[:, PAD:PAD + SEQ], nt[:, i % 2, :], ACT.Identity,
                                     bias=mod[:, 1, SH1 + k:SH1 + k + 1]).then_inc(pad_ready, 1)

            for l in range(2):
                n0 = FFN_N[l]
                norm = 1 + 2 * l
                norm_std(norm)
                sh = mod[:, l, SH2:SH2 + 8]
                norm_tiles(norm, sh, range(4))
                hi_of_slot(slot_at(n0 - 1))
                norm_tiles(norm, sh, range(4, 8))
                for part, (j0, nk) in enumerate(PARTS):
                    q0 = l * FT + j0

                    def up(i):
                        for u in range(2):
                            s = slot_at(n0, i, u)
                            q, jj, v = q0 + u + 2 * i, j0 + u + 2 * i, (q0 + u) % 2
                            act.wait_ge(mm_done, s.g + 1)
                            nc.scalar.activation(cb[:, v, :], pair[s.gr][:, 0, :], ACT.Identity,
                                                 bias=col[:, bass.ds(c_fcb(l) + jj, 1)],
                                                 scale=col[:, bass.ds(c_fcw(l, 1) + jj, 1)])
                            nc.scalar.activation(gp[:, v, 1:1 + SEQ], pair[s.gr][:, 0, :], ACT.Copy)\
                                .then_inc(evac[s.gr], 1)
                            act.wait_ge(conv_ready, q + 1)
                            nc.scalar.activation(cb[:, v, :], cb[:, v, :], ACT.Silu).then_inc(g_ready, 1)
                            act.wait_ge(*bank_done(s, 1))
                            nc.scalar.activation(h_hi[:, 2 * i + u, :], cb[:, v, :], ACT.Copy).then_inc(hh_ready, 1)
                            hi_of_slot(s)
                    pairs(act, nk // 2, up)
                    n0 += nk
                    final = part == 2

                    def out_copy(m):
                        act.wait_ge(t_ready, len(T_READY) + m + 1)
                        if m >= 2:
                            act.wait_ge(out_sent[m % 2], 16 * (m // 2))
                        nc.scalar.activation(tmp[:, m % 2, :], pT[:, :], ACT.Copy).then_inc(t_read, 1)

                    def down(i):
                        for u in range(2):
                            s = slot_at(n0, i, u)
                            if final and l == 0:
                                for v in range(2):
                                    square(2, 2 * (2 * i + u) + v, bank_done(s, v))
                            if not final or s.n + 2 < min(N_SLOTS, n0 + 5):
                                hi_of_slot(s)
                            if final and l == 1:
                                for v in range(2):
                                    out_copy(2 * (2 * i + u) + v)

                    pairs(act, 2, down, unroll=final)
                    n0 += 4
                if l == 0:
                    norm_std(2)
                    for i in range(4):
                        pad_row(i)
                    hi_of_slot(slot_at(POOL_N - 1))
                    for k in range(KT):
                        act.wait_ge(pool_full, k + 1)
                        nc.scalar.activation(a_hi[:, k, :], pooled(k), ACT.Copy).then_inc(a_half, 1)
                        if k + 4 < KT:
                            pad_row(k + 4)
                    for t in range(4):
                        g = POOL_N + 8 + t
                        for v in range(2):
                            square(3, 2 * t + v, (evac[g % 2], 2 * (g // 2) + v + 1))

        @block.vector
        def _(dve):
            steps = [0]

            def chain(ins):
                steps[0] += 1
                ins.then_inc(dve_seq, 1)
                dve.wait_ge(dve_seq, steps[0])

            def lo(dst, full, hi):
                return nc.vector.tensor_tensor(dst, full, hi.bitcast(f32), ALU.subtract)

            def lo_of_slot(n, r):
                dve.wait_ge(w_hi_done, n + 1)
                lo(w_lo[:, r, :], w_raw[:, r, :], w_hi[:, r, :]).then_inc(w_split, 1)

            def lo_quarter(n, c):
                part = slice(c * 512, (c + 1) * 512)
                if c == 3:
                    dve.wait_ge(w_hi_done, n + 1)
                else:
                    dve.wait_ge(w_quarter, 3 * (n - 2) + c + 1)
                ins = lo(w_lo[:, n % 2, part], w_raw[:, n % 2, part], w_hi[:, n % 2, part])
                if c == 3:
                    ins.then_inc(w_split, 1)

            def lo_next(s):
                lo_of_slot(s.n + 2, s.r)

            def residual(dst, s, v, factor, old):
                if v == 0:
                    dve.wait_ge(mm_done, s.g + 1)
                nc.vector.scalar_tensor_tensor(out=dst, in0=pair[s.gr][:, v, :], scalar=factor, in1=old,
                                               op0=ALU.mult, op1=ALU.add).then_inc(evac[s.gr], 1)

            def add_square(norm, k):
                f = norm * KT + k
                dve.wait_ge(sq_ready, f + 1)
                if k == 0:
                    nc.vector.tensor_copy(ss, sq[:, 0, :]).then_inc(ss_added, 1)
                else:
                    dve.wait_ge(ss_added, f)
                    nc.vector.tensor_tensor(ss, ss, sq[:, k % 2, :], ALU.add).then_inc(ss_added, 1)

            def rms_inverse(norm):
                dve.wait_ge(*aux_read_at(AUX_NORM[norm]))
                chain(nc.vector.reciprocal(inv4, inv4))
                nc.vector.tensor_copy(inv_wide.rearrange("p (i t) -> p i t", i=TT),
                                      inv4.unsqueeze(2).to_broadcast([P, TT, P])).then_inc(inv_ready, 1)

            def norm_scaled(norm, i, k):
                u = AUX_NORM[norm] + 1
                if i == 0:
                    dve.wait_ge(aux_ready, u + 1)
                nc.vector.scalar_tensor_tensor(out=nt[:, i % 2, :], in0=xT[:, k, :], scalar=gain[:, norm, k:k + 1],
                                               in1=aux[u % 3], op0=ALU.mult, op1=ALU.mult).then_inc(n_ready, 1)

            def scaled(norm, k):
                if k >= 2:
                    dve.wait_ge(a_ready, norm * KT + k - 1)
                norm_scaled(norm, k, k)

            def normed_lo(norm, k, shift):
                dve.wait_ge(a_half, norm * KT + k + 1)
                nc.vector.scalar_tensor_tensor(out=a_lo[:, k, :], in0=nt[:, k % 2, :], scalar=shift[:, k:k + 1],
                                               in1=a_hi[:, k, :].bitcast(f32), op0=ALU.add, op1=ALU.subtract)\
                    .then_inc(a_ready, 1)

            def norm_tiles(norm, shift, between=None):
                if norm:
                    rms_inverse(norm)
                for k in range(KT + 1):
                    if k < KT:
                        scaled(norm, k)
                    if k:
                        normed_lo(norm, k - 1, shift)
                    if k == 4 and between is not None:
                        between()

            def gain_of(dst, scale_at, layer, gain_col):
                chain(nc.vector.scalar_tensor_tensor(out=dst, in0=mod[:, layer, scale_at:scale_at + 8], scalar=1.0,
                                                     in1=col[:, gain_col:gain_col + 8], op0=ALU.add, op1=ALU.mult))

            def ada_columns(b, dst, bias):
                dve.wait_ge(ada_ready, b + 1)
                nc.vector.reduce_sum(ada4, pT[:, :].rearrange("p (a b) -> p a b", b=P), axis=AX.X)\
                    .then_inc(ada_summed, 1)
                dve.wait_ge(ada_summed, b + 1)
                nc.vector.tensor_tensor(dst, ada4, bias, ALU.add).then_inc(t_read, 1)

            nc.vector.memset(acc[:, 0, :], 0.0).then_inc(rows_zero, 1)
            nc.vector.memset(ones[:, :], 1.0)
            nc.vector.memset(gp[:, :, :], 0.0)
            nc.vector.memset(eps[:, :], EPS).then_inc(set_up, 1)

            def tokens_out(i, dst):
                dve.wait_ge(mm_done, i + 1)
                dve.wait_ge(*half_evacuated(i))
                nc.vector.tensor_copy(dst, pair[i % 2][:, 1, :].rearrange("p (k t) -> p k t", k=4))\
                    .then_inc(evac[i % 2], 1)

            def half_evacuated(g):
                return evac[g % 2], 2 * (g // 2) + 1
            for i in range(TT):
                tokens_out(i, xT[:, 4:8, i * P:(i + 1) * P])
            dve.wait_ge(ctx_std, 1)
            chain(nc.vector.reciprocal(cstat[:, 2:4], cstat[:, 2:4]))
            for i in range(2):
                t = stage[:, (TT + i) % 3, :]
                nc.vector.tensor_scalar(t, t, cstat[:, 2 + i:3 + i], None, ALU.mult).then_inc(ctx_scaled, 1)
            for i in range(2):
                tokens_out(TT + i, ctx_t[1][:, :, i * P:(i + 1) * P])
            for k in range(KT):
                add_square(0, k)
            rms_inverse(0)
            lo_of_slot(0, 0)
            dve.wait_ge(ada_cols, 4)
            nc.vector.tensor_tensor(mod[:, 0, 0:16], aux[0][:, 0:32:2], col[:, C_ADAB:C_ADAB + 16], ALU.add)
            nc.vector.tensor_tensor(modc[:, :], aux[0][:, 1:32:2], col[:, C_ADAB:C_ADAB + 16], ALU.add)\
                .then_inc(mods_done, 1)
            dve.wait_ge(mods_done, 1)
            gain_of(gain[:, 0, :], SC1, 0, C_MIXN)
            chain(nc.vector.scalar_tensor_tensor(out=gainc[:, :], in0=modc[:, 8:16], scalar=1.0,
                                                 in1=col[:, C_MIXN:C_MIXN + 8], op0=ALU.add, op1=ALU.mult))
            norm_tiles(0, mod[:, 0, SH1:SH1 + 8])
            for k in range(KT + 1):
                if k < KT:
                    t = ctx_t[k // 4][:, k % 4, :]
                    nc.vector.tensor_scalar(t, t, gainc[:, k:k + 1], modc[:, k:k + 1], ALU.mult, ALU.add)\
                        .then_inc(ctxa_full, 1)
                if k:
                    dve.wait_ge(ctxa_half, k)
                    lo(ctxa_lo[:, k - 1, :], ctx_t[(k - 1) // 4][:, (k - 1) % 4, :], ctxa_hi[:, k - 1, :])\
                        .then_inc(ctxa_ready, 1)

            def evac_in(n):
                s = slot_at(n)
                if n == 2:
                    for i, (g, b, j, inc) in enumerate(((9, 0, 2, 1), (9, 1, 4, 1), (10, 0, 0, 2))):
                        dve.wait_ge(v_half, i + 1)
                        lo(v_lo[:, j:j + 2, :], pair[g % 2][:, b, :].rearrange("p (a n) -> p a n", a=2),
                           v_hi[:, j:j + 2, :]).then_inc(evac[g % 2], inc)
                elif n in (5, 8):
                    before = slot_at(n - 1)
                    dve.wait_ge(mm_done, s.g + 1)
                    for v in range(2):
                        dve.wait_ge(*bank_done(before, v))
                        nc.vector.tensor_tensor(gp[:, v, 1:1 + SEQ], pair[s.gr][:, v, :], tbl[:, 2 + v, :], ALU.mult)\
                            .then_inc(evac[s.gr], 1)
                elif n in (6, 9):
                    dve.wait_ge(mm_done, s.g + 1)
                    for v in range(2):
                        nc.vector.tensor_tensor(cb[:, v, :], cb[:, v, :], pair[s.gr][:, v, :], ALU.mult)\
                            .then_inc(evac[s.gr], 1)
                elif n >= OUT0:
                    for v in range(2):
                        m = 2 * (n - OUT0) + v
                        residual(xT[:, m, :], s, v, mod[:, 0, G1 + m:G1 + m + 1], xT[:, m, :])
                    for v in range(2):
                        add_square(1, 2 * (n - OUT0) + v)

            for unit in MIX:
                kind = unit[0]
                if kind == "ada":
                    at = 16 + 4 * unit[1]
                    ada_columns(unit[1], mod[:, 0, at:at + 4], col[:, C_ADAB + at:C_ADAB + at + 4])
                elif kind == "ev":
                    evac_in(unit[1])
                elif kind == "sp":
                    if unit[1:] == (2, 0):
                        dve.wait_ge(w_split, 2)
                    lo_quarter(unit[1], unit[2])
                elif kind == "st":
                    dve.wait_ge(*stat_read(unit))
                    chain(nc.vector.reciprocal(inv4, inv4))
                    nc.vector.tensor_copy(q_sq(unit[1]).rearrange("p (i t) -> p i t", i=TT),
                                          inv4.unsqueeze(2).to_broadcast([P, TT, P])).then_inc(wide_ready, 1)
                elif kind == "iv":
                    i = unit[1]
                    dve.wait_ge(*stat_ready(unit))
                    g = C_KG if i in (2, 3, 4) else C_QG
                    nc.vector.scalar_tensor_tensor(out=q_raw(i), in0=q_raw(i), scalar=col[:, g:g + 1],
                                                   in1=stat_bank(unit), op0=ALU.mult, op1=ALU.mult)\
                        .then_inc(t_read if i >= 5 else q_full if i == 4 else qn_ready, 1)
                elif kind == "rot":
                    i = unit[1]
                    dve.wait_ge(*stat_ready(unit))
                    nc.vector.tensor_tensor(q_sq(i), stat_bank(unit), tbl[:, 1, :], ALU.mult)\
                        .then_inc(stat_read(unit)[0], 1)
                    chain(nc.vector.tensor_tensor(q_raw(i), q_raw(i), tbl[:, 0, :], ALU.mult))
                    nc.vector.tensor_tensor(q_raw(i), q_raw(i), q_sq(i), ALU.add).then_inc(q_full, 1)
                elif kind == "qf":
                    i = unit[1]
                    dve.wait_ge(q_half, i + 1)
                    lo(q_view(qk_lo, i), q_src(i), q_view(qk_hi, i)).then_inc(q_done, 1)
                elif kind == "sc":
                    q = unit[2]
                    dve.wait_ge(s_ready, SC_USE[unit] + 1)
                    chain(nc.vector.reduce_max(red, s_flat, axis=AX.X))
                    nc.vector.tensor_scalar(sm[:, q, 0:1], red, -HD ** -0.5, None, ALU.mult)\
                        .then_inc(s_max, 1)
                elif kind == "pn":
                    _, h, q = unit
                    dve.wait_ge(s_read, SC_USE[("sc", h, q)] + 1)
                    chain(nc.vector.reciprocal(sm[:, q, 1:2], sm[:, q, 1:2]))
                    nc.vector.tensor_scalar(p_t[:, q, :], p_t[:, q, :], sm[:, q, 1:2], None, ALU.mult)\
                        .then_inc(p_ready, 1)
                elif kind == "tr":
                    _, h, j = unit
                    dve.wait_ge(pt_half, h * JT + j + 1)
                    lo(h_lo[:, 8 + j % 2, :], pT[:, :], h_hi[:, 8 + j % 2, :]).then_inc(t_read, 1)
                elif kind == "o":
                    h = unit[1]
                    dve.wait_ge(o_half, h + 1)
                    lo(h_lo[:, h, :], pO[:, :], h_hi[:, h, :]).then_inc(o_read, 1)
                elif kind == "tap":
                    _, half, side, v = unit
                    ct = 2 * half + v
                    dve.wait_ge(cc_ready, ct + 1)
                    w = C_ECW + 8 * side + ct
                    chain(nc.vector.scalar_tensor_tensor(
                        out=cb[:, v, :], in0=gp[:, v, 2 * side:2 * side + SEQ], scalar=col[:, w:w + 1],
                        in1=cb[:, v, :], op0=ALU.mult, op1=ALU.add))
                elif kind == "cvb":
                    for v in range(2):
                        ct = 2 * unit[1] + v
                        dve.wait_ge(y_half, ct + 1)
                        lo(h_lo[:, 4 + ct, :], cb[:, v, :], h_hi[:, 4 + ct, :]).then_inc(cv_ready, 1)

            def window_mean(k):
                if k in BY_POOL:
                    dve.wait_ge(win_summed, k - BY_POOL[0] + 1)
                else:
                    dve.wait_ge(pad_ready, POOL_ORDER.index(k) + 1)
                    if k >= 2:
                        dve.wait_ge(a_ready, 2 * KT + k - 1)
                    window_sum(k, nc.vector, dve_win, lambda ins, last: chain(ins))
                row, ident_row = pooled(k), apad(k)[:, PAD:PAD + SEQ]
                if k:
                    dve.wait_ge(pool_full, k)
                chain(nc.vector.tensor_tensor(edge, edges(row), edge_counts[:, k // 2], ALU.mult))
                chain(nc.vector.scalar_tensor_tensor(out=row, in0=row, scalar=1.0 / WINDOWS[k // 2], in1=ident_row,
                                                     op0=ALU.mult, op1=ALU.subtract))
                nc.vector.tensor_tensor(edges(row), edge, edges(ident_row), ALU.subtract).then_inc(pool_full, 1)

            def pool_scaled(i):
                k = POOL_ORDER[i]
                if i >= 2:
                    dve.wait_ge(pad_ready, i - 1)
                norm_scaled(2, i, k)

            def pooled_lo(k):
                if k - 1 in LO_BY_POOL:
                    dve.wait_ge(a_ready, 2 * KT + k)
                dve.wait_ge(a_half, 2 * KT + k + 1)
                lo(a_lo[:, k, :], pooled(k), a_hi[:, k, :]).then_inc(a_ready, 1)

            for l in range(2):
                n0 = FFN_N[l]
                norm = 1 + 2 * l
                if l == 0:
                    gain_of(gain[:, 1, :], SC2, 0, C_FFNN)
                norm_tiles(norm, mod[:, l, SH2:SH2 + 8], (lambda: lo_next(slot_at(n0 - 1))) if l == 0 else None)
                if l == 1:
                    dve.wait_ge(w_split, n0 + 2)
                for part, (j0, nk) in enumerate(PARTS):
                    q0 = l * FT + j0

                    def up(i):
                        for u in range(2):
                            s = slot_at(n0, i, u)
                            q, jj, v = q0 + u + 2 * i, j0 + u + 2 * i, (q0 + u) % 2
                            if l == 0 and u == 1:
                                b = j0 // 2 + i
                                ada_columns(ADA0 + b, mod[:, 1, bass.ds(4 * b, 4)],
                                            col[:, bass.ds(C_ADAB + 48 + 4 * b, 4)])
                            dve.wait_ge(*bank_done(s, 0))
                            nc.vector.scalar_tensor_tensor(
                                out=cb[:, v, :], in0=gp[:, v, 0:SEQ], scalar=col[:, bass.ds(c_fcw(l, 0) + jj, 1)],
                                in1=cb[:, v, :], op0=ALU.mult, op1=ALU.add).then_inc(tap_done, 1)
                            dve.wait_ge(tap_done, q + 1)
                            nc.vector.scalar_tensor_tensor(
                                out=cb[:, v, :], in0=gp[:, v, 2:2 + SEQ], scalar=col[:, bass.ds(c_fcw(l, 2) + jj, 1)],
                                in1=cb[:, v, :], op0=ALU.mult, op1=ALU.add).then_inc(conv_ready, 1)
                            dve.wait_ge(g_ready, q + 1)
                            nc.vector.tensor_tensor(cb[:, v, :], cb[:, v, :], pair[s.gr][:, 1, :], ALU.mult)\
                                .then_inc(evac[s.gr], 1)
                            dve.wait_ge(hh_ready, q + 1)
                            lo(h_lo[:, 2 * i + u, :], cb[:, v, :], h_hi[:, 2 * i + u, :]).then_inc(h_ready, 1)
                            lo_next(s)
                    pairs(dve, nk // 2, up)
                    n0 += nk
                    final = part == 2

                    def down(i):
                        for u in range(2):
                            s = slot_at(n0, i, u)
                            if l == 0 and final and 2 * i + u == 3:
                                b = ADA1 - 1
                                ada_columns(ADA0 + b, mod[:, 1, 4 * b:4 * b + 4],
                                            col[:, C_ADAB + 48 + 4 * b:C_ADAB + 52 + 4 * b])
                            for v in range(2):
                                m = 2 * (2 * i + u) + v
                                old = xT[:, m, :]
                                if final and l == 1:
                                    if m >= 4:
                                        dve.wait_ge(t_ready, len(T_READY) + m - 3)
                                    dst = final_tiles[:, m % 4, :]
                                else:
                                    dst = old
                                residual(dst, s, v, mod[:, l, bass.ds(G2 + m, 1)], old)
                            if final and l == 0:
                                for v in range(2):
                                    add_square(2, 2 * (2 * i + u) + v)
                            if not final or s.n + 2 < min(N_SLOTS, n0 + 5):
                                lo_next(s)

                    pairs(dve, 2, down, unroll=final)
                    n0 += 4
                if l == 0:
                    for t in apads:
                        nc.vector.memset(t[:, 0:PAD], 0.0)
                        nc.vector.memset(t[:, PAD + SEQ:], 0.0)
                    gain_of(gain[:, 2, :], SC1, 1, C_MIXN + 8)
                    gain_of(gain[:, 3, :], SC2, 1, C_FFNN + 8)
                    chain(nc.vector.tensor_tensor(gain[:, 4, :], mod[:, 1, G1:G1 + 8], col[:, C_POOL:C_POOL + 8],
                                                  ALU.mult))
                    dve.wait_ge(count_loaded, 16)
                    rms_inverse(2)
                    for i in range(4):
                        pool_scaled(i)
                    for k in range(KT):
                        window_mean(k)
                        if k + 4 < KT:
                            pool_scaled(k + 4)
                        if k and k - 1 not in LO_BY_POOL:
                            pooled_lo(k - 1)
                    pooled_lo(KT - 1)
                    for t in range(4):
                        s = Slot(POOL_N, POOL_N % 2, POOL_N // 2, POOL_N + 8 + t, t % 2, (POOL_N + 8 + t) // 2)
                        for v in range(2):
                            m = 2 * t + v
                            residual(xT[:, m, :], s, v, gain[:, 4, m:m + 1], xT[:, m, :])
                        for v in range(2):
                            add_square(3, 2 * t + v)


_INS = ["x", "c", "ctx", "c_ctx", "ada_w", "ada_b", "mix_norm", "ffn_norm", "even_w_in", "even_q_gain",
        "even_k_gain", "even_conv_w", "even_w_out", "odd_pool_w", "odd_pool_scale", "ffn_w_up", "ffn_conv_w",
        "ffn_conv_b", "ffn_w_down"]


def shape_constants():
    f = np.float32
    ident = np.eye(P, dtype=f)
    perm = ident[np.arange(P) ^ (HD // 4)]
    t = np.arange(SEQ)
    axis_dim = HD // 2
    inv_freq = np.power(f(THETA), -np.arange(0, axis_dim, 2, dtype=f) / f(axis_dim)).astype(f)
    pos = np.stack([t // GRID_W, t % GRID_W]).astype(f)
    dim = np.arange(HD)
    ang = pos[dim // axis_dim] * inv_freq[dim % (HD // 4)][:, None]
    sign = np.where(dim // (HD // 4) % 2 == 0, f(-1), f(1))[:, None]
    rope = np.concatenate([np.cos(ang), np.sin(ang) * sign], axis=1).astype(f)
    counts = [np.minimum(t + w - w // 2, SEQ) - np.maximum(t - w // 2, 0) for w in WINDOWS]
    inv = np.concatenate([f(1) / n[e].astype(f) for n in counts for e in (slice(0, PAD), slice(SEQ - PAD, SEQ))])
    return {"ident": ident, "perm": perm, "rope": rope, "edge_counts": np.ascontiguousarray(np.tile(inv, (P, 1)))}


def kernel(**inputs):
    import concourse.bacc as _bacc
    from concourse import mybir as _mybir
    from concourse.bass_utils import run_bass_kernel_spmd as _run

    nc = _bacc.Bacc("TRN2", target_bir_lowering=False, num_devices=1, dynamic_dma_scratch_size=4096)
    arrays, args = {}, []
    given = {name: inputs[name] for name in _INS}
    given.update(shape_constants())
    for name, a in given.items():
        a = np.ascontiguousarray(a)
        arrays[f"in_{name}_dram"] = a
        args.append(nc.dram_tensor(f"in_{name}_dram", a.shape, _mybir.dt.from_np(a.dtype), kind="ExternalInput").ap())
    args.append(nc.dram_tensor("out_0_dram", (1, SEQ, D), _mybir.dt.float32, kind="ExternalOutput").ap())
    build(nc, *args)
    r = _run(nc, [arrays], core_ids=[0])
    return r.results[0]["out_0_dram"]
```
